# Optimizing a Trainium2 kernel written in Bass

```python
import math, functools
import jax, jax.numpy as jnp
from jax import lax
import numpy as np

D_MODEL = 1024
BATCH = 1
SEQ = 512
DEPTH = 1
DEC_BATCH = 8
DEC_SEQ = 1
PAST_LEN = 2048
PAGE_SIZE = 128

HEAD_DIM = D_MODEL // 16
NSA_HEADS = 8
NSA_KV_HEADS = 2
NSA_GROUP = NSA_HEADS // NSA_KV_HEADS
MLSTM_HEADS = 4
POOL_GROUPS = 4
NSA_W = NSA_HEADS * HEAD_DIM
KV_W = NSA_KV_HEADS * HEAD_DIM
MLSTM_W = MLSTM_HEADS * HEAD_DIM
POOL_W = POOL_GROUPS * HEAD_DIM
MIX_W = NSA_W + MLSTM_W + POOL_W
IN_SPLITS = (NSA_W, 6 * KV_W, 3 * NSA_HEADS, 3 * MLSTM_W, 2 * MLSTM_HEADS, MLSTM_W, POOL_W)
IN_W = NSA_W + 6 * KV_W + 3 * NSA_HEADS + 3 * MLSTM_W + 2 * MLSTM_HEADS + MLSTM_W + POOL_W
CMP_STRIDE = 16
CMP_LEN = 2 * CMP_STRIDE
SLC_BLOCK = 64
SLC_RATIO = SLC_BLOCK // CMP_STRIDE
N_SEL = 16
WINDOW = 512
Q_BLOCK = 128
MLSTM_CHUNK = 64
POOL_WINDOWS = (2, 4, 8, 16)
POOL_STATE = 15
D_FF = 2816
FFN_CONV = 3
RMS_EPS = 1e-6
NEG = -1e30
FORCE = 1e6

kernel_name = 'hybrid_nsa_mlstm_pool_decoder_step'

def rmsnorm(x, g):
    x32 = x.astype(jnp.float32)
    y = x32 * lax.rsqrt(jnp.mean(x32 * x32, axis=-1, keepdims=True) + RMS_EPS) * g
    return y.astype(x.dtype)

def masked_softmax(s, mask):
    s = jnp.where(mask, s, NEG)
    e = jnp.exp(s - s.max(axis=-1, keepdims=True)) * mask
    return e / jnp.maximum(e.sum(axis=-1, keepdims=True), jnp.finfo(jnp.float32).tiny)

def split_cols(p):
    outs, o = [], 0
    for w in IN_SPLITS:
        outs.append(p[..., o:o + w])
        o += w
    return outs

def compress(rows, wpos, w, b):
    B, Tp = rows.shape[:2]
    seg = rows.reshape(B, Tp // CMP_STRIDE, CMP_STRIDE, NSA_KV_HEADS, HEAD_DIM)
    pooled = (jnp.einsum('bnjhd,jd->bnhd', seg[:, :-1], wpos[:CMP_STRIDE])
              + jnp.einsum('bnjhd,jd->bnhd', seg[:, 1:], wpos[CMP_STRIDE:]))
    return jnp.einsum('bnhd,de->bnhe', pooled, w) + b

def nsa_core(q, g, qpos, kc, vc, ks, vs, kw, vw, kpos):
    B, Tq = q.shape[:2]
    f32 = jnp.float32
    scale = HEAD_DIM ** -0.5
    qg = q.reshape(B, Tq, NSA_KV_HEADS, NSA_GROUP, HEAD_DIM)
    nc = kc.shape[1]
    cmp_end = CMP_STRIDE * jnp.arange(nc) + CMP_LEN - 1
    s_c = jnp.einsum('bqhgd,bnhd->bhgqn', qg, kc, preferred_element_type=f32) * scale
    p_c = masked_softmax(s_c, cmp_end[None, :] <= qpos[:, None])
    o_c = jnp.einsum('bhgqn,bnhd->bqhgd', p_c, vc.astype(f32))
    ns = ks.shape[2]
    imp = jnp.pad(p_c.sum(axis=2), ((0, 0), (0, 0), (0, 0), (1, SLC_RATIO * ns - nc)))
    imp = (imp[..., :SLC_RATIO * ns].reshape(B, NSA_KV_HEADS, Tq, ns, SLC_RATIO).sum(-1)
           + imp[..., SLC_RATIO::SLC_RATIO])
    j = jnp.arange(ns)[None, :]
    cur = (qpos // SLC_BLOCK)[:, None]
    valid = j * SLC_BLOCK <= qpos[:, None]
    forced = (j == 0) | (j == cur) | (j == cur - 1)
    score = jnp.where(valid, jnp.where(forced, FORCE, imp), -1.0)
    top, idx = lax.top_k(score, min(N_SEL, ns))
    gather = jax.vmap(jax.vmap(lambda blocks, ix: blocks[ix]))
    gk = gather(ks, idx)
    gv = gather(vs, idx)
    s_s = jnp.einsum('bqhgd,bhqksd->bhgqks', qg, gk, preferred_element_type=f32) * scale
    tok = idx[..., None] * SLC_BLOCK + jnp.arange(SLC_BLOCK)
    m_s = (top >= 0)[..., None] & (tok <= qpos[:, None, None])
    sh = s_s.shape
    p_s = masked_softmax(s_s.reshape(sh[:4] + (-1,)),
                         m_s.reshape(B, NSA_KV_HEADS, 1, Tq, -1)).reshape(sh)
    o_s = jnp.einsum('bhgqks,bhqksd->bqhgd', p_s, gv.astype(f32))
    s_w = jnp.einsum('bqhgd,bkhd->bhgqk', qg, kw, preferred_element_type=f32) * scale
    dlt = qpos[:, None] - kpos[None, :]
    p_w = masked_softmax(s_w, (dlt >= 0) & (dlt < WINDOW) & (kpos >= 0)[None, :])
    o_w = jnp.einsum('bhgqk,bkhd->bqhgd', p_w, vw.astype(f32))
    gt = jax.nn.sigmoid(g.astype(f32)).reshape(B, Tq, NSA_KV_HEADS, NSA_GROUP, 3)
    o = gt[..., 0:1] * o_c + gt[..., 1:2] * o_s + gt[..., 2:3] * o_w
    return o.reshape(B, Tq, NSA_W).astype(q.dtype)

def unpack_nsa(nq, nkv):
    B, T = nq.shape[:2]
    kv = nkv.reshape(B, T, 6, NSA_KV_HEADS, HEAD_DIM)
    return [kv[:, :, i] for i in range(6)]

def nsa_prompt(nq, nkv, ng, cmp_pos, cmp_w, cmp_b):
    B, S = nq.shape[:2]
    k_cmp, v_cmp, k_slc, v_slc, k_win, v_win = unpack_nsa(nq, nkv)
    kc = compress(k_cmp, cmp_pos[0], cmp_w[0], cmp_b[0])
    vc = compress(v_cmp, cmp_pos[1], cmp_w[1], cmp_b[1])
    ns = S // SLC_BLOCK
    ks = k_slc.reshape(B, ns, SLC_BLOCK, NSA_KV_HEADS, HEAD_DIM).transpose(0, 3, 1, 2, 4)
    vs = v_slc.reshape(B, ns, SLC_BLOCK, NSA_KV_HEADS, HEAD_DIM).transpose(0, 3, 1, 2, 4)
    pad = ((0, 0), (WINDOW, 0), (0, 0), (0, 0))
    kw, vw = jnp.pad(k_win, pad), jnp.pad(v_win, pad)
    nqb = S // Q_BLOCK
    qb = nq.reshape(B, nqb, Q_BLOCK, NSA_W).swapaxes(0, 1)
    gb = ng.reshape(B, nqb, Q_BLOCK, 3 * NSA_HEADS).swapaxes(0, 1)

    def one_block(args):
        i, qi, gi = args
        start = i * Q_BLOCK
        qpos = start + jnp.arange(Q_BLOCK)
        kpos = start - WINDOW + jnp.arange(WINDOW + Q_BLOCK)
        kwi = lax.dynamic_slice_in_dim(kw, start, WINDOW + Q_BLOCK, axis=1)
        vwi = lax.dynamic_slice_in_dim(vw, start, WINDOW + Q_BLOCK, axis=1)
        return nsa_core(qi, gi, qpos, kc, vc, ks, vs, kwi, vwi, kpos)

    o = lax.map(one_block, (jnp.arange(nqb), qb, gb)).swapaxes(0, 1).reshape(B, S, NSA_W)
    wb = min(WINDOW, S)
    new_k = jnp.stack([k_cmp, k_slc], axis=2)
    new_v = jnp.stack([v_cmp, v_slc], axis=2)
    return o, (new_k, new_v, k_win[:, S - wb:], v_win[:, S - wb:])

def nsa_sample(nq, nkv, ng, past_k, past_v, win_k, win_v, cmp_pos, cmp_w, cmp_b):
    DB, DS = nq.shape[:2]
    past = past_k.shape[1]
    k_cmp, v_cmp, k_slc, v_slc, k_win, v_win = unpack_nsa(nq, nkv)
    tot = past + DS
    tp = -(-tot // SLC_BLOCK) * SLC_BLOCK
    pad = ((0, 0), (0, tp - tot), (0, 0), (0, 0))
    rows = lambda old, new: jnp.pad(jnp.concatenate([old.astype(new.dtype), new], axis=1), pad)
    kc = compress(rows(past_k[:, :, 0], k_cmp), cmp_pos[0], cmp_w[0], cmp_b[0])
    vc = compress(rows(past_v[:, :, 0], v_cmp), cmp_pos[1], cmp_w[1], cmp_b[1])
    ns = tp // SLC_BLOCK
    ks = rows(past_k[:, :, 1], k_slc).reshape(DB, ns, SLC_BLOCK, NSA_KV_HEADS, HEAD_DIM).transpose(0, 3, 1, 2, 4)
    vs = rows(past_v[:, :, 1], v_slc).reshape(DB, ns, SLC_BLOCK, NSA_KV_HEADS, HEAD_DIM).transpose(0, 3, 1, 2, 4)
    wb = win_k.shape[1]
    kw = jnp.concatenate([win_k.astype(k_win.dtype), k_win], axis=1)
    vw = jnp.concatenate([win_v.astype(v_win.dtype), v_win], axis=1)
    kpos = past - wb + jnp.arange(wb + DS)
    qpos = past + jnp.arange(DS)
    o = nsa_core(nq, ng, qpos, kc, vc, ks, vs, kw, vw, kpos)
    new_k = jnp.stack([k_cmp, k_slc], axis=2)
    new_v = jnp.stack([v_cmp, v_slc], axis=2)
    return o, (new_k, new_v, kw[:, -wb:], vw[:, -wb:])

def mlstm_chunk(carry, xs):
    C, n, m = carry
    q, k, v, ig, lf = xs
    L = q.shape[1]
    b = jnp.cumsum(lf, axis=1)
    a = b + m[:, None, :]
    bt, it, at = b.transpose(0, 2, 1), ig.transpose(0, 2, 1), a.transpose(0, 2, 1)
    causal = jnp.tril(jnp.ones((L, L), dtype=bool))
    logd = jnp.where(causal, bt[..., :, None] - bt[..., None, :] + it[..., None, :], -jnp.inf)
    mt = jnp.maximum(at, logd.max(axis=-1))
    dm = jnp.exp(logd - mt[..., None])
    inter = jnp.exp(at - mt)
    qk = jnp.einsum('blhd,bshd->bhls', q, k) * dm
    num = jnp.einsum('bhls,bshd->blhd', qk, v) + jnp.einsum('bhl,blhd,bhde->blhe', inter, q, C)
    den = qk.sum(axis=-1) + inter * jnp.einsum('blhd,bhd->bhl', q, n)
    h = num / jnp.maximum(jnp.abs(den), jnp.exp(-mt)).transpose(0, 2, 1)[..., None]
    mL = mt[:, :, -1]
    w = jnp.exp(b[:, -1:, :] - b + ig - mL[:, None, :])
    decay = jnp.exp(a[:, -1] - mL)
    C = decay[..., None, None] * C + jnp.einsum('bsh,bshd,bshe->bhde', w, k, v)
    n = decay[..., None] * n + jnp.einsum('bsh,bshd->bhd', w, k)
    return (C, n, mL), h

def mlstm(q, k, v, ig, lf, state):
    B, T = q.shape[:2]
    L = math.gcd(T, MLSTM_CHUNK)
    nc = T // L
    chunk = lambda t: t.reshape((B, nc, L) + t.shape[2:]).swapaxes(0, 1)
    state = tuple(s.astype(jnp.float32) for s in state)
    state, h = lax.scan(mlstm_chunk, state, tuple(chunk(t) for t in (q, k, v, ig, lf)))
    return h.swapaxes(0, 1).reshape(B, T, MLSTM_HEADS, HEAD_DIM), state

def pool_mix(u, prev, pos0, w_grp, scale):
    B, T, _ = u.shape
    zr = jnp.concatenate([prev.astype(u.dtype), u], axis=1)
    z = zr.astype(jnp.float32)
    cs = jnp.concatenate([jnp.zeros((B, 1, POOL_W), jnp.float32), jnp.cumsum(z, axis=1)], axis=1)
    P = POOL_STATE
    pos = pos0 + jnp.arange(T)
    end = cs[:, P + 1:]
    outs = []
    for gi, w in enumerate(POOL_WINDOWS):
        sl = slice(gi * HEAD_DIM, (gi + 1) * HEAD_DIM)
        cnt = jnp.minimum(w, pos + 1).astype(jnp.float32)[None, :, None]
        mean = (end[..., sl] - cs[:, P + 1 - w:P + 1 - w + T, sl]) / cnt
        outs.append((mean - z[:, P:, sl]) @ w_grp[gi].astype(jnp.float32))
    return jnp.concatenate(outs, axis=-1) * scale, zr[:, -P:]

def conv_ffn(h, prev, w_up, conv_w, conv_b, w_down):
    T = h.shape[1]
    up = h @ w_up
    z = jnp.concatenate([prev.astype(up.dtype), up], axis=1)
    y = conv_b
    for j in range(FFN_CONV):
        y = y + conv_w[j] * z[:, j:j + T]
    a, b = jnp.split(y, 2, axis=-1)
    return (jax.nn.silu(a) * b) @ w_down, z[:, -(FFN_CONV - 1):]

def trunk_layer(x, c, lw, nsa_fn, mstate, pool_prev, ffn_prev, pos0):
    (g1, g2, ada_w, ada_b, w_in, gate_b, pool_w, pool_scale, w_out, w_up, conv_w, conv_b, w_down) = lw
    B, T, _ = x.shape
    f32 = jnp.float32
    mod = jax.nn.silu(c) @ ada_w + ada_b
    sh1, sc1, gt1, sh2, sc2, gt2 = [t[:, None, :] for t in jnp.split(mod, 6, axis=-1)]
    h = rmsnorm(x, g1) * (1 + sc1) + sh1
    nq, nkv, ng, mqkv, mif, mo, pu = split_cols(h @ w_in)
    o_nsa, nsa_state = nsa_fn(nq, nkv, ng)
    mq, mk, mv = [t.astype(f32).reshape(B, T, MLSTM_HEADS, HEAD_DIM) for t in jnp.split(mqkv, 3, axis=-1)]
    gates = mif.astype(f32) + gate_b
    ig = gates[..., :MLSTM_HEADS]
    lf = jax.nn.log_sigmoid(gates[..., MLSTM_HEADS:])
    hm, mstate = mlstm(mq, mk * HEAD_DIM ** -0.5, mv, ig, lf, mstate)
    o_m = jax.nn.sigmoid(mo.astype(f32)) * hm.reshape(B, T, MLSTM_W)
    o_p, pool_state = pool_mix(pu, pool_prev, pos0, pool_w, pool_scale)
    mix = jnp.concatenate([o_nsa.astype(x.dtype), o_m.astype(x.dtype), o_p.astype(x.dtype)], axis=-1) @ w_out
    x = x + gt1 * mix
    h2 = rmsnorm(x, g2) * (1 + sc2) + sh2
    f, ffn_state = conv_ffn(h2, ffn_prev, w_up, conv_w, conv_b, w_down)
    x = x + gt2 * f
    return x, nsa_state, mstate, pool_state, ffn_state

def setup_inputs(seed: int = 0) -> dict:
    key = jax.random.key(seed)
    keys = iter(jax.random.split(key, 48))
    nrm = lambda shape, s=1.0: s * jax.random.normal(next(keys), shape, jnp.float32)
    n_pages = PAST_LEN // PAGE_SIZE
    n_phys = (5 * DEC_BATCH * n_pages + 3) // 4
    wb = min(WINDOW, PAST_LEN)
    d = D_MODEL
    inp = {}
    inp['x_prompt'] = nrm((BATCH, SEQ, d))
    inp['x_sample'] = nrm((DEC_BATCH, DEC_SEQ, d))
    inp['cache_k'] = nrm((DEPTH, n_phys, PAGE_SIZE, 2, NSA_KV_HEADS, HEAD_DIM))
    inp['cache_v'] = nrm((DEPTH, n_phys, PAGE_SIZE, 2, NSA_KV_HEADS, HEAD_DIM))
    inp['cache_win_k'] = nrm((DEPTH, DEC_BATCH, wb, NSA_KV_HEADS, HEAD_DIM))
    inp['cache_win_v'] = nrm((DEPTH, DEC_BATCH, wb, NSA_KV_HEADS, HEAD_DIM))
    inp['state_mlstm_C'] = nrm((DEPTH, DEC_BATCH, MLSTM_HEADS, HEAD_DIM, HEAD_DIM), 0.5)
    inp['state_mlstm_n'] = nrm((DEPTH, DEC_BATCH, MLSTM_HEADS, HEAD_DIM), 0.5)
    inp['state_mlstm_m'] = nrm((DEPTH, DEC_BATCH, MLSTM_HEADS))
    inp['state_pool'] = nrm((DEPTH, DEC_BATCH, POOL_STATE, POOL_W))
    inp['state_ffn_conv'] = nrm((DEPTH, DEC_BATCH, FFN_CONV - 1, 2 * D_FF))
    perm = jax.random.permutation(next(keys), n_phys)
    inp['page_table'] = perm[:DEC_BATCH * n_pages].reshape(DEC_BATCH, n_pages).astype(jnp.int32)
    inp['c_prompt'] = nrm((BATCH, d))
    inp['c_sample'] = nrm((DEC_BATCH, d))
    inp['norm1_g'] = 1.0 + nrm((DEPTH, d), 0.02)
    inp['norm2_g'] = 1.0 + nrm((DEPTH, d), 0.02)
    inp['ada_w'] = nrm((DEPTH, d, 6 * d), 0.5 * d ** -0.5)
    inp['ada_b'] = nrm((DEPTH, 6 * d), 0.02)
    inp['w_in'] = nrm((DEPTH, d, IN_W), d ** -0.5)
    inp['nsa_cmp_pos'] = nrm((DEPTH, 2, CMP_LEN, HEAD_DIM), CMP_LEN ** -0.5)
    inp['nsa_cmp_w'] = nrm((DEPTH, 2, HEAD_DIM, HEAD_DIM), HEAD_DIM ** -0.5)
    inp['nsa_cmp_b'] = nrm((DEPTH, 2, HEAD_DIM), 0.02)
    inp['mlstm_gate_b'] = jnp.concatenate([nrm((DEPTH, MLSTM_HEADS), 0.1),
                                           3.0 + nrm((DEPTH, MLSTM_HEADS), 0.5)], axis=-1)
    inp['pool_w'] = nrm((DEPTH, POOL_GROUPS, HEAD_DIM, HEAD_DIM), HEAD_DIM ** -0.5)
    inp['pool_scale'] = 1.0 + nrm((DEPTH, POOL_W), 0.1)
    inp['w_out'] = nrm((DEPTH, MIX_W, d), MIX_W ** -0.5)
    inp['ffn_w_up'] = nrm((DEPTH, d, 2 * D_FF), d ** -0.5)
    inp['ffn_conv_w'] = nrm((DEPTH, FFN_CONV, 2 * D_FF), FFN_CONV ** -0.5)
    inp['ffn_conv_b'] = nrm((DEPTH, 2 * D_FF), 0.02)
    inp['ffn_w_down'] = nrm((DEPTH, D_FF, d), D_FF ** -0.5)
    inp['final_g'] = 1.0 + nrm((d,), 0.02)
    return inp

def reference(x_prompt, x_sample, cache_k, cache_v, cache_win_k, cache_win_v, state_mlstm_C,
              state_mlstm_n, state_mlstm_m, state_pool, state_ffn_conv, page_table, c_prompt, c_sample,
              norm1_g, norm2_g, ada_w, ada_b, w_in, nsa_cmp_pos, nsa_cmp_w, nsa_cmp_b, mlstm_gate_b,
              pool_w, pool_scale, w_out, ffn_w_up, ffn_conv_w, ffn_conv_b, ffn_w_down, final_g):
    B = x_prompt.shape[0]
    DB = x_sample.shape[0]
    past = page_table.shape[1] * cache_k.shape[2]
    f32 = jnp.float32
    xp, xq = x_prompt, x_sample
    acc_p = [[] for _ in range(9)]
    acc_s = [[] for _ in range(9)]
    for l in range(DEPTH):
        lw = (norm1_g[l], norm2_g[l], ada_w[l], ada_b[l], w_in[l], mlstm_gate_b[l], pool_w[l],
              pool_scale[l], w_out[l], ffn_w_up[l], ffn_conv_w[l], ffn_conv_b[l], ffn_w_down[l])
        cp, cw, cb = nsa_cmp_pos[l], nsa_cmp_w[l], nsa_cmp_b[l]
        m0 = (jnp.zeros((B, MLSTM_HEADS, HEAD_DIM, HEAD_DIM), f32),
              jnp.zeros((B, MLSTM_HEADS, HEAD_DIM), f32),
              jnp.zeros((B, MLSTM_HEADS), f32))
        xp, nsa_p, m_p, pool_p, ffn_p = trunk_layer(
            xp, c_prompt, lw, functools.partial(nsa_prompt, cmp_pos=cp, cmp_w=cw, cmp_b=cb), m0,
            jnp.zeros((B, POOL_STATE, POOL_W), xp.dtype),
            jnp.zeros((B, FFN_CONV - 1, 2 * D_FF), xp.dtype), 0)
        past_k = cache_k[l][page_table].reshape((DB, past) + cache_k.shape[3:])
        past_v = cache_v[l][page_table].reshape((DB, past) + cache_v.shape[3:])
        nsa_fn = functools.partial(nsa_sample, past_k=past_k, past_v=past_v, win_k=cache_win_k[l],
                                   win_v=cache_win_v[l], cmp_pos=cp, cmp_w=cw, cmp_b=cb)
        xq, nsa_s, m_s, pool_s, ffn_s = trunk_layer(
            xq, c_sample, lw, nsa_fn, (state_mlstm_C[l], state_mlstm_n[l], state_mlstm_m[l]),
            state_pool[l], state_ffn_conv[l], past)
        for a, v in zip(acc_p, nsa_p + m_p + (pool_p, ffn_p)):
            a.append(v)
        for a, v in zip(acc_s, nsa_s + m_s + (pool_s, ffn_s)):
            a.append(v)
    sp = [jnp.stack(a, axis=0) for a in acc_p]
    ss = [jnp.stack(a, axis=0) for a in acc_s]
    y_prompt = rmsnorm(xp, final_g)
    y_sample = rmsnorm(xq, final_g)
    return (y_prompt, y_sample, sp[0], sp[1], sp[2], sp[3], sp[4], sp[5], sp[6], sp[7], sp[8],
            ss[0], ss[1], ss[2], ss[3], ss[4], ss[5], ss[6], ss[7], ss[8])


_drawn_inputs = setup_inputs


def setup_inputs(seed=0):
    import zlib

    import numpy as np

    out = dict(_drawn_inputs(seed))
    spreads = {}
    factors = {'cache_k': 3.711,
     'cache_v': 3.005,
     'norm2_g': 3.124,
     'nsa_cmp_b': 21.939,
     'pool_scale': 4.383,
     'ffn_conv_b': 8.0,
     'final_g': 8.067}
    for name, (base, spread) in spreads.items():
        noise = np.random.default_rng([zlib.crc32(name.encode()), seed]).standard_normal(out[name].shape)
        drawn = base * np.exp(spread * noise) if base else spread * noise
        out[name] = __import__('jax').numpy.asarray(drawn.astype(out[name].dtype))
    for name, factor in factors.items():
        out[name] = (out[name] * factor).astype(out[name].dtype)
    return out
```

```python
from contextlib import ExitStack

import numpy as np
import concourse.bass as bass
from concourse import mybir

F32 = mybir.dt.float32
I32 = mybir.dt.int32
ALU = mybir.AluOpType
ACT = mybir.ActivationFunctionType
AX = mybir.AxisListType.X

P = 128
D = 1024
KD = D // P
S = 512
NB = 8
T = S + NB
ST = S // P
HD = 64
G = 4
NH = 8
PAGE = 128
NPG = 16
NPHYS = 160
HALF = NPG // 2
NCB = 127
NCP = S // 16 - 1
NSB = 33
NSEL = 16
FF = 2816
FC = FF // P
SCALE = HD ** -0.5
NEG = -1e30
EPS = 1e-6

(T_Q, T_KC, T_VC, T_KS, T_KW, T_MK, T_MQ, T_MO, T_PU, T_G, T_VS, T_VW, T_MV) = (0, 4, 5, 6, 7, 8, 10, 12, 14, 16, 17, 18, 19)
N_IN = 21
N_FM = 17

RING = 6

def _layout(parts):
    at, out = 0, {}
    for name, n in parts:
        out[name] = (at, n)
        at += n
    return out, at

PAR, NPAR = _layout([("g1", 8), ("g2", 8), ("gf", 8), ("ada_b", 48), ("conv_w", 132), ("conv_b", 44), ("pool_s", 2),
                     ("wpos", 64), ("bk", 1), ("gate_b", 1), ("igb", 1), ("fgb", 1), ("c", 72),
                     ("cw", 256), ("bv", 128), ("pw", 256), ("mn", 64), ("mm", 1)])
CON, NCON = _layout([("ident", 128), ("ones", 128), ("mean", 128), ("cq", 128), ("ct", 128), ("cadd", 124), ("cmul", 124),
                     ("rw", 2), ("rcnt", 32), ("hot", 512), ("grp", 64), ("newm", 8), ("ltri", NSB * NSB)])


def plan():
    part1 = [("ada", t, 1) for t in range(16)]
    done = 16
    for t in range(N_IN):
        part1.append(("in", t, 1))
        while done < 16 + (32 * (t + 1)) // N_IN:
            part1.append(("ada", done, 1))
            done += 1
    part2 = [("out", m, 1) for m in range(KD)]
    for j in range(FC):
        part2 += [("up", j, 1), ("up", FC + j, 1)]
    part2 += [("down", m, 3) for m in range(KD)]
    return part1, part2


PART1, PART2 = plan()
N_UP0 = len(PART1) + KD
N_DOWN0 = N_UP0 + 2 * FC
NSLOT = sum(i[2] for i in PART1 + PART2)


def events():
    out, pend = [], []
    for n, (kind, t, _) in enumerate(PART1):
        out.append(("lin", n))
        while pend:
            out.append(pend.pop(0))
        if kind == "in" and 4 <= t < 4 + 2 * NB:
            b = (t - 4) // 2
            out.append(("slc", b, t % 2))
            if t % 2:
                out.append(("blocks", b))
                pend.append(("cmp", b))
    return out


EVENTS = events()


def trunk_kernel(nc, xT, wst, par_d, con_d, pt_d, cacheA, cacheV, winK, winV, mC, mst, plst, ffst,
                 o_y, o_fm, o_vn, o_st, o_wk, o_wv, o_C, o_m, o_pool, o_sC, o_sn, o_sm, o_spool, o_ffp, o_ffs):
    with ExitStack() as ctx:
        def sb(name, shape, dt=F32):
            return ctx.enter_context(nc.sbuf_tensor(name, shape, dt))

        def sem(name):
            return ctx.enter_context(nc.semaphore(name))

        x = sb("x", [P, KD, T])
        h = sb("h", [P, KD, T])
        big = sb("big", [P, 17 * S + 2 * HALF * 384])
        pT = big[:, 0:17 * S].rearrange("p (t n) -> p t n", t=17)
        pages = big[:, 17 * S:17 * S + 2 * HALF * 384].rearrange("p (s j n) -> p s j n", s=2, j=HALF)
        vpages = big[:, 17 * S:17 * S + 3 * NPG * P].rearrange("p (s j n) -> p s j n", s=3, j=NPG)
        kwin = big[:, 0:4096].rearrange("p (b n) -> p b n", b=NB)
        vwin = big[:, 4096:8192].rearrange("p (b c n) -> p b c n", b=NB, c=ST)
        fT = big[:, 0:FC * T].rearrange("p (j n) -> p j n", j=FC)
        ring = sb("ring", [P, RING, KD, P])
        vn = sb("vn", [P, ST, 2 * P])
        vm = sb("vm", [P, ST, 4, HD + 1])
        par = sb("par", [P, NPAR])
        con = sb("con", [P, NCON])
        sT = sb("sT", [P, N_IN, NB])
        mod = sb("mod", [P, 48, 9])
        sc = sb("sc", [P, KD, 9])
        sc2 = sb("sc2", [P, KD, 9])
        ab = sb("ab", [P, KD, 9])
        sq = sb("sq", [P, 2, T])
        rstd = sb("rstd", [P, T])
        t8 = sb("t8", [P, NB])
        qs = sb("qs", [P, NB, NH])
        sall = sb("sall", [64, NPG * P + NB])
        scm = sb("scm", [64, P])
        vc = sb("vc", [P, NB, P])
        ptt = sb("ptt", [1, NB * NPG], I32)

        SCR = 9472
        scr = sb("scr", [P, SCR])

        def lay(at, parts):
            out = []
            for n in parts:
                out.append(scr[:, at:at + n])
                at += n
            assert at <= SCR, at
            return out

        KEEP = 1152 + 96 + 260 + 214 + 1024
        tmp, poolA, poolB, sst = lay(0, [1024, 256, 256, 2176])
        poolA = poolA.rearrange("p (k n) -> p k n", k=2)
        poolB = poolB.rearrange("p (k n) -> p k n", k=2)
        sn, gN, cout, smr, cst = lay(0, [1152, 96, 260, 214, 1024])
        gN = gN.rearrange("p (i n) -> p i n", i=ST)
        cout = cout.rearrange("p (h n) -> p h n", h=4)
        ctmp, kN, wj, dt_, wk, hN, r36, mro = lay(KEEP, [1024, 1024, 1280, 1024, 256, 1024, 512, 512])
        kN = kN.rearrange("p (t i n) -> p t i n", t=2, i=ST)
        dt_ = dt_.rearrange("p (a n) -> p a n", a=2)
        wk = wk.rearrange("p (j n) -> p j n", j=ST)
        hN = hN.rearrange("p (i n) -> p i n", i=ST)
        lfo, zro, bro = sq[:, 0, 0:S], sq[:, 1, 0:S], rstd[:, 0:S]
        pr, prT, pc, md, mds = lay(KEEP, [2048, 2048, 1024, 1024, 16])
        pr = pr.rearrange("p (a r n) -> p a r n", a=2, r=2)
        prT = prT.rearrange("p (a r n) -> p a r n", a=2, r=2)
        pc = pc.rearrange("p (u n) -> p u n", n=32)
        md = md.rearrange("p (t n) -> p t n", t=2)
        mds = mds.rearrange("p (t n) -> p t n", t=2)
        zp = lay(KEEP + 2048, [2 * (15 + S)])[0].rearrange("p (t n) -> p t n", t=2)
        swin, ptS, simp, rank, tie, sst2 = lay(KEEP, [520, (NPG + ST + 3) * 64, 136, 1089, 1089, 512])
        ptS = ptS.rearrange("p (c r) -> p c r", r=64)
        yab, sil, ffst_t, ffo_s, ffo_p = lay(KEEP, [2 * T, T, 704, 704, 88])
        yab = yab.rearrange("p (a n) -> p a n", a=2)
        ffst_t = ffst_t.rearrange("p (c j b) -> p c j b", c=2 * FC, j=2)
        ffo_s = ffo_s.rearrange("p (c j b) -> p c j b", c=2 * FC, j=2)
        ffo_p = ffo_p.rearrange("p (c j) -> p c j", j=2)

        kct = sb("kct", [P, P])
        pcT = sb("pcT", [P, 2, P])
        vcp = sb("vcp", [P, P])
        pooled = sb("pooled", [P, 2, P])
        rT = sb("rT", [P, ST, 36])
        enm = sb("enm", [P, ST, 4])
        d4 = sb("d4", [P, 8])
        mx = sb("mx", [P, 4, 32])
        sm = sb("sm", [P, 2, 2])
        nmx = sb("nmx", [P, 2, 2])
        fac = sb("fac", [P, 2, 2])
        zs = sb("zs", [P, 2, NB, 16])
        zsum = sb("zsum", [P, 2, NB])
        mout = sb("mout", [4, 2])
        mv = sb("mv", [P, 32])
        qc = sb("qc", [P, 16])
        shh = sb("shh", [P, 16])
        hs8 = sb("hs8", [NB, 4 * HD])
        emos = sb("emos", [P, 2, NB])
        sg = sb("sg", [64, 4])
        sel = sb("sel", [64, 4, 34])
        ssx = sb("ssx", [64, 16])

        ps = ctx.enter_context(nc.psum_tensor("ps", [P, 8, 512], F32))

        def con_(name, a=0, b=None, rows=P):
            at, n = CON[name]
            return con[0:rows, at + a:at + (n if b is None else b)]

        def par_(name, a=0, b=None, lo=0, hi=P):
            at, n = PAR[name]
            return par[lo:hi, at + a:at + (n if b is None else b)]

        ident = con_("ident")
        hr = [slice(0, HD), slice(HD, P)]

        x_landed, par_landed, con_landed = sem("x_landed"), sem("par_landed"), sem("con_landed")
        slot_landed = [sem(f"slot_landed{i}") for i in range(RING)]
        slot_done = sem("slot_done")
        table_landed = sem("table_landed")
        cache_landed = [sem(f"cache_landed{i}") for i in range(2)]
        vcache_landed = [sem(f"vcache_landed{i}") for i in range(3)]
        win_landed = sem("win_landed")
        rec_landed = sem("rec_landed")
        ffst_landed = sem("ffst_landed")
        memset_done = sem("memset_done")
        early_out, state_out, end_out = sem("early_out"), sem("state_out"), sem("end_out")
        sq_ready, sq_used, var_ready, root_ready = sem("sq_ready"), sem("sq_used"), sem("var_ready"), sem("root_ready")
        silu_exp, silu_ready = sem("silu_exp"), sem("silu_ready")
        xn_ready, h_prompt, h_sample = sem("xn_ready"), sem("h_prompt"), sem("h_sample")
        evac_act, evac_dve = sem("evac_act"), sem("evac_dve")
        qs_ready = sem("qs_ready")
        slc_scored, slc_evac = sem("slc_scored"), sem("slc_evac")
        comp_done, pooled_ready = sem("comp_done"), sem("pooled_ready")
        blocks_done, blocks_evac = sem("blocks_done"), sem("blocks_evac")
        cmp_scored, cmp_evac, sst_moved = sem("cmp_scored"), sem("cmp_evac"), sem("sst_moved")
        kn_T, sn_T, g_T, kn_evac, sn_evac, g_exp = (sem("kn_T"), sem("sn_T"), sem("g_T"), sem("kn_evac"),
                                                    sem("sn_evac"), sem("g_exp"))
        az_ready, ln_ready, rows_ready, r_T, rt_evac = (sem("az_ready"), sem("ln_ready"), sem("rows_ready"), sem("r_T"),
                                                        sem("rt_evac"))
        act_step = sem("act_step")
        bc_done, mscore_done, dmask_done, dt_done, w_done = (sem("bc_done"), sem("mscore_done"), sem("dmask_done"),
                                                             sem("dt_done"), sem("w_done"))
        num_done, num_evac, hT_done, emo_ready, mmix_ready = (sem("num_done"), sem("num_evac"), sem("hT_done"),
                                                              sem("emo_ready"), sem("mmix_ready"))
        rows_moved, saz_ready, sln_ready, sexp_in, sexp_ready, srec_ready = (
            sem("rows_moved"), sem("saz_ready"), sem("sln_ready"), sem("sexp_in"), sem("sexp_ready"), sem("srec_ready"))
        hs_moved, emos_ready, shT_done = sem("hs_moved"), sem("emos_ready"), sem("shT_done")
        gates_ready = sem("gates_ready")
        csc_done, pcx_ready, pcx_exp, pc_ready = sem("csc_done"), sem("pcx_ready"), sem("pcx_exp"), sem("pc_ready")
        qk_done, mx_ready, p_exp, p_ready, t_done = sem("qk_done"), sem("mx_ready"), sem("p_exp"), sem("p_ready"), sem("t_done")
        pt_act, pt_dve, pv_done, o_evac = sem("pt_act"), sem("pt_dve"), sem("pv_done"), sem("o_evac")
        pool_ready, pool_mm = sem("pool_ready"), sem("pool_mm")
        snew_done, wsc_done, wsc_evac, w_moved, sgate_moved, sg_exp = (sem("snew_done"), sem("wsc_done"), sem("wsc_evac"),
                                                                       sem("w_moved"), sem("sgate_moved"), sem("sg_exp"))
        sx_in, sx_out, imp_in, imp_done, sp_ready, spT_done, spT_evac = (
            sem("sx_in"), sem("sx_out"), sem("imp_in"), sem("imp_done"), sem("sp_ready"), sem("spT_done"), sem("spT_evac"))
        spv_done, mix_ready = sem("spv_done"), sem("mix_ready")
        y_ready, silu_in, silu_out, x_ready, out_ready = (sem("y_ready"), sem("silu_in"), sem("silu_out"), sem("x_ready"),
                                                          sem("out_ready"))
        dve_step = sem("dve_step")

        SLOT0 = [0]
        for item in PART1 + PART2:
            SLOT0.append(SLOT0[-1] + item[2])
        NE = len([e for e in EVENTS if e[0] == "slc"])
        UNITS = [(hh, i) for hh in range(NH) for i in range(ST)]
        OFF = [0, 512, 896, 1152]

        block = ctx.enter_context(nc.Block())

        @block.sync
        def _(sp):
            for k in range(KD):
                sp.dma_start(x[:, k, :], xT[:, k, :]).then_inc(x_landed, 16)
            sp.dma_start(con[:, :], con_d).then_inc(con_landed, 16)
            sp.dma_start(par[:, :], par_d).then_inc(par_landed, 16)
            for n in range(RING):
                sp.dma_start(ring[:, n, :, :], wst[n, :, :].rearrange("p (k n) -> p k n", k=KD)).then_inc(slot_landed[n], 16)
            rounds = NSLOT // RING
            with sp.Fori(1, rounds) as r:
                for s in range(RING):
                    sp.wait_ge(slot_done, r * RING + (s + 1 - RING))
                    sp.dma_start(ring[:, s, :, :], wst[bass.ds(r * RING + s, 1), :, :].rearrange("a p (k n) -> (a p) k n", k=KD))\
                      .then_inc(slot_landed[s], 16)
            for n in range(rounds * RING, NSLOT):
                sp.wait_ge(slot_done, n + 1 - RING)
                sp.dma_start(ring[:, n % RING, :, :], wst[n, :, :].rearrange("p (k n) -> p k n", k=KD))\
                  .then_inc(slot_landed[n % RING], 16)

        @block.gpsimd
        def _(pool):
            pool.dma_start(ptt[:, :], pt_d).then_inc(table_landed, 16)
            nc.gpsimd.memset(qs[:, :, :], 0.0).then_inc(memset_done, 1)
            nc.gpsimd.memset(vm[:, :, :, HD:HD + 1], 1.0).then_inc(memset_done, 1)
            pool.wait_ge(table_landed, 16)

            def load_half(b, s):
                for j in range(HALF):
                    pg = pool.value_load(ptt[0:1, bass.ds(b * NPG + s * HALF + j, 1)], min_val=0, max_val=NPHYS - 1)
                    pool.dma_start(pages[:, s, j, :], cacheA[bass.ds(pg, 1), :, :].rearrange("a p n -> (a p) n"))\
                        .then_inc(cache_landed[s], 16)

            load_half(0, 0)
            load_half(0, 1)
            pool.dma_start(zs[:, :, :, 0:15], plst).then_inc(rec_landed, 16)
            with pool.Fori(1, NB) as b:
                for s in range(2):
                    pool.wait_ge(comp_done, b * 2 + (s - 1))
                    pool.wait_ge(slc_scored, b * 2 + (s - 1))
                    load_half(b, s)

            pool.wait_ge(evac_act, len(PART1))
            pool.dma_start(o_fm, pT[:, T_KC:T_MK, :]).then_inc(early_out, 16)
            pool.dma_start(o_vn, vn[:, :, :]).then_inc(early_out, 16)
            pool.dma_start(o_st, sT[:, :, :]).then_inc(early_out, 16)
            pool.dma_start(o_pool, pT[:, T_PU:T_PU + 2, S - 15:S]).then_inc(early_out, 16)
            pool.wait_ge(comp_done, 2 * NB)
            pool.wait_ge(slc_scored, 2 * NB)

            def load_values(b):
                with pool.Fori(0, NPG) as j:
                    pg = pool.value_load(ptt[0:1, bass.ds(j + b * NPG, 1)], min_val=0, max_val=NPHYS - 1)
                    pool.dma_start(vpages[:, b % 3, bass.ds(j, 1), :],
                                   cacheV[bass.ds(pg, 1), :, :].rearrange("a p n -> p a n")).then_inc(vcache_landed[b % 3], 16)

            pool.wait_ge(sn_evac, 1)
            for e in range(4):
                for hh in range(4):
                    r = slice(e * 32 + hh * 8, e * 32 + hh * 8 + 8)
                    pool.dma_start(smr[r, 0:128].rearrange("p (t d) -> p t d", t=2),
                                   sn[0:8, 0:512].rearrange("p (t h d) -> p t h d", t=2, h=4)[:, :, hh, :]).then_inc(rows_moved, 16)
                    pool.dma_start(smr[r, 128:144], sn[0:8, 512 + hh * 64 + e * 16:512 + hh * 64 + e * 16 + 16])\
                        .then_inc(rows_moved, 16)
                    pool.dma_start(smr[r, 144:146], sn[0:8, 768 + hh:768 + hh + 33:32], allow_slow_non_contiguous=True)\
                        .then_inc(rows_moved, 16)
            pool.dma_start(cst[:, :], mC).then_inc(rec_landed, 16)
            for b in range(NB):
                pool.dma_start(sg[b * 8:b * 8 + 8, 0:3], sn[b:b + 1, 768 + 64:768 + 88].rearrange("p (h r) -> p h r", h=8))\
                    .then_inc(sgate_moved, 16)
            for b in range(3):
                load_values(b)
            pool.wait_ge(srec_ready, 1)
            for e in range(4):
                for hh in range(4):
                    pool.dma_start(hs8[0:8, hh * 64 + e * 16:hh * 64 + e * 16 + 16], shh[e * 32 + hh * 8:e * 32 + hh * 8 + 8, :])\
                        .then_inc(hs_moved, 16)
            pool.dma_start(o_sC, cst[:, :]).then_inc(state_out, 16)
            pool.dma_start(o_sn, smr[0:32, 146:210]).then_inc(state_out, 16)
            pool.dma_start(o_sm, mv[0:32, 3:4]).then_inc(state_out, 16)
            pool.wait_ge(mmix_ready, 1)
            pool.dma_start(o_C, cout[0:HD, :, :]).then_inc(state_out, 16)
            pool.dma_start(o_m, mout[0:4, 0:1]).then_inc(state_out, 16)
            pool.wait_ge(pool_ready, 1)
            pool.dma_start(o_spool, zs[:, :, :, 1:16]).then_inc(state_out, 16)
            pool.wait_ge(early_out, 64)
            pool.wait_ge(pv_done, len(UNITS))
            pool.dma_start(kwin, winK).then_inc(win_landed, 16)
            pool.dma_start(vwin, winV).then_inc(win_landed, 16)
            pool.wait_ge(win_landed, 32)
            pool.dma_start(o_wk, kwin[:, :, 1:512]).then_inc(state_out, 16)
            pool.dma_start(o_wv, vwin).then_inc(state_out, 16)
            for b in range(3, NB):
                pool.wait_ge(spv_done, b - 2)
                load_values(b)
            pool.wait_ge(mix_ready, 1)
            pool.dma_start(ffst_t, ffst).then_inc(ffst_landed, 16)
            pool.wait_ge(evac_dve, KD + 2 * FC)
            pool.dma_start(o_ffp, ffo_p).then_inc(end_out, 16)
            pool.dma_start(o_ffs, ffo_s).then_inc(end_out, 16)
            pool.wait_ge(out_ready, 1)
            pool.dma_start(o_y, h[:, :, :]).then_inc(end_out, 16)
            pool.wait_ge(early_out, 64)
            pool.wait_ge(state_out, 16 * 8)
            pool.wait_ge(end_out, 48)

        @block.tensor
        def _(pe):
            mm = nc.tensor.matmul

            def norm_sums(n):
                for k in range(KD):
                    pe.wait_ge(sq_ready, n * KD + k + 1)
                    mm(ps[:, 4, :], con_("mean"), sq[:, k % 2, 0:S], start=(k == 0), stop=(k == KD - 1))
                    mm(ps[:, 5, 0:NB], con_("mean"), sq[:, k % 2, S:T], start=(k == 0), stop=(k == KD - 1)).then_inc(sq_used, 1)

            def product(n, kind, t, slots):
                bank, bank8 = ps[:, n % 2, :], ps[:, 2 + n % 2, 0:NB]
                src = fT if kind == "down" else h
                chunks = FC if kind == "down" else KD
                for s in range(slots):
                    g = SLOT0[n] + s
                    pe.wait_ge(slot_landed[g % RING], 16 * (g // RING + 1))
                    w = ring[:, g % RING, :, :]
                    ks = range(s * KD, min((s + 1) * KD, chunks))
                    for k in ks:
                        one = dict(start=(k == 0), stop=(k == chunks - 1))
                        if kind == "ada":
                            last = mm(ps[:, 2 + n % 2, 0:9], w[:, k, :], sc[:, k, :], **one)
                        else:
                            if kind == "in" and t == 0:
                                pe.wait_ge(h_prompt, k + 1)
                                pe.wait_ge(h_sample, k + 1)
                            if kind == "up" and t == 0:
                                pe.wait_ge(h_prompt, KD + k + 1)
                                pe.wait_ge(h_sample, KD + k + 1)
                            if kind == "down" and t == 0 and k >= FC - 1:
                                pe.wait_ge(evac_dve, KD + 2 * FC)
                            if not (kind == "in" and t >= N_FM):
                                mm(bank, w[:, k - s * KD, :], src[:, k, 0:S], **one)
                                last = mm(bank8, w[:, k - s * KD, :], src[:, k, S:T], **one)
                    if kind == "in" and t >= N_FM:
                        for i in range(ST):
                            for k in ks:
                                mm(bank[:, i * P:(i + 1) * P], h[:, k, i * P:(i + 1) * P], w[:, k, :],
                                   start=(k == 0), stop=(k == KD - 1))
                        for k in ks:
                            last = mm(bank8, w[:, k, :], h[:, k, S:T], start=(k == 0), stop=(k == KD - 1))
                    last.then_inc(slot_done, 1)

            pe.wait_ge(con_landed, 16)
            pe.wait_ge(par_landed, 16)
            norm_sums(0)
            pe.wait_ge(silu_ready, 1)
            e = 0
            for ev in EVENTS:
                if ev[0] == "lin":
                    n = ev[1]
                    if n >= 2:
                        pe.wait_ge(evac_act, n - 1)
                    product(n, *PART1[n])
                elif ev[0] == "slc":
                    _, b, s = ev
                    pe.wait_ge(cache_landed[s], 16 * HALF * (b + 1))
                    pe.wait_ge(qs_ready, 1)
                    if e:
                        pe.wait_ge(slc_evac, e)
                    e += 1
                    for j in range(2):
                        last = mm(ps[0:NH, 6 + j, :].rearrange("p (j n) -> p j n", j=4), qs[:, b, :],
                                  pages[:, s, 4 * j:4 * j + 4, P:2 * P], start=True, stop=True)
                    last.then_inc(slc_scored, 1)
                elif ev[0] == "blocks":
                    b = ev[1]
                    pe.wait_ge(pooled_ready, b + 1)
                    if b:
                        pe.wait_ge(blocks_evac, b)
                        pe.wait_ge(cmp_evac, b)
                    else:
                        pe.wait_ge(var_ready, 1)
                    mm(ps[:, 4, 0:NCB], par_("cw", 0, P), pooled[:, 0, 0:NCB], start=True, stop=True)
                    mm(ps[0:NCB, 5, 0:P], pooled[:, 1, 0:NCB], par_("cw", P, 2 * P), start=True, stop=False)
                    mm(ps[0:NCB, 5, 0:P], con_("ones", 0, NCB, 1), par_("bv", hi=1), start=False, stop=True)\
                        .then_inc(blocks_done, 1)
                else:
                    b = ev[1]
                    pe.wait_ge(blocks_evac, b + 1)
                    mm(ps[0:NH, 4, 0:NCB], qs[:, b, :], kct[:, 0:NCB], start=True, stop=True).then_inc(cmp_scored, 1)

            pe.wait_ge(evac_act, len(PART1))
            pe.wait_ge(blocks_evac, NB)
            pe.wait_ge(cmp_evac, NB)
            pe.wait_ge(slc_evac, NE)
            for t in range(2):
                for i in range(ST):
                    last = nc.tensor.transpose(ps[:, 4 + t, i * P:(i + 1) * P], pT[:, T_MK + t, i * P:(i + 1) * P], ident)
            last.then_inc(kn_T, 1)
            for c, t in enumerate([T_MQ, T_MQ + 1, T_MK, T_MK + 1, T_MV, T_MV + 1, T_G, T_VS, T_VW]):
                last = nc.tensor.transpose(ps[0:NB, c // 4, (c % 4) * P:(c % 4 + 1) * P], sT[:, t, :], ident)
            last.then_inc(sn_T, 1)
            for i in range(ST):
                last = nc.tensor.transpose(ps[:, 3, i * P:(i + 1) * P], pT[:, T_G, i * P:(i + 1) * P], ident)
            last.then_inc(g_T, 1)
            pe.wait_ge(pooled_ready, NB + 1)
            mm(ps[:, 6, 0:NCP], par_("cw", 0, P), pooled[:, 0, 0:NCP], start=True, stop=True)
            mm(ps[0:NCP, 7, 0:P], pooled[:, 1, 0:NCP], par_("cw", P, 2 * P), start=True, stop=False)
            mm(ps[0:NCP, 7, 0:P], con_("ones", 0, NCP, 1), par_("bv", hi=1), start=False, stop=True).then_inc(blocks_done, 1)
            pe.wait_ge(rows_ready, 1)
            pe.wait_ge(sn_evac, 1)
            for i in range(ST):
                last = nc.tensor.transpose(ps[:, 0, i * 36:(i + 1) * 36], r36[0:36, i * P:(i + 1) * P], ident[0:36, 0:36])
            last.then_inc(r_T, 1)

            pe.wait_ge(kn_evac, 1)
            pe.wait_ge(g_exp, 1)
            pe.wait_ge(blocks_evac, NB + 1)
            for hh in range(4):
                rows, t = hr[hh % 2], hh // 2
                if hh:
                    pe.wait_ge(w_done, 4 * hh)
                mm(ps[:, 7, :], con_("hot", hh * P, (hh + 1) * P, 4), mro[0:4, :], start=True, stop=True).then_inc(bc_done, 1)
                for j in range(ST):
                    q = 4 * hh + j
                    if q >= 2:
                        pe.wait_ge(w_done, q - 1)
                    mm(ps[:, 4 + q % 2, 0:S - j * P], pT[rows, T_MK + t, j * P:(j + 1) * P], pT[rows, T_MQ + t, j * P:S],
                       start=True, stop=True).then_inc(mscore_done, 1)
                pe.wait_ge(w_done, 4 * hh + 4)
                if hh:
                    pe.wait_ge(num_evac, hh)
                for i in range(ST):
                    for j in range(i + 1):
                        at = OFF[j] + (i - j) * P
                        mm(ps[:, 6, i * 65:i * 65 + 65], wj[:, at:at + P], vm[:, j, hh, :], start=(j == 0), stop=(j == i))
                for j in range(ST):
                    last = mm(ps[0:HD, 3, hh * 65:hh * 65 + 65], wk[:, j, :], vm[:, j, hh, :], start=(j == 0), stop=(j == ST - 1))
                last.then_inc(num_done, 1)
            pe.wait_ge(num_evac, 4)
            for t in range(2):
                for i in range(ST):
                    last = nc.tensor.transpose(ps[:, 1 + t, i * P:(i + 1) * P], hN[:, i, t * P:(t + 1) * P], ident)
            last.then_inc(hT_done, 1)

            pe.wait_ge(mmix_ready, 1)
            pe.wait_ge(rt_evac, 1)
            for u, (hh, i) in enumerate(UNITS):
                rows = hr[hh // G]
                last = mm(ps[:, u // 16, (u % 16) * 32:(u % 16) * 32 + NCP], pT[rows, hh % G, i * P:(i + 1) * P], kct[rows, 0:NCP],
                          start=True, stop=True)
            last.then_inc(csc_done, 1)

            def scores(u):
                hh, i = UNITS[u]
                rows, n = hr[hh // G], (i + 1) * P
                if u >= 2:
                    pe.wait_ge(p_exp, u - 1)
                elif u == 0:
                    pe.wait_ge(pcx_ready, 1)
                for r, t in enumerate((T_KS, T_KW)):
                    last = mm(ps[:, 2 * (u % 2) + r, 0:n], pT[rows, hh % G, i * P:(i + 1) * P], pT[rows, t, 0:n],
                              start=True, stop=True)
                last.then_inc(qk_done, 1)

            def flip(u):
                hh, i = UNITS[u]
                pe.wait_ge(p_ready, u + 1)
                if u == 0:
                    pe.wait_ge(pc_ready, 1)
                else:
                    pe.wait_ge(pt_act, u)
                    pe.wait_ge(pt_dve, u)
                for r in range(2):
                    for c in range(i + 1):
                        nc.tensor.transpose(ps[:, 4 + r, c * P:(c + 1) * P], pr[:, u % 2, r, c * P:(c + 1) * P], ident)
                nc.tensor.transpose(ps[0:NCP, 6, 0:P], pc[:, u, 0:NCP], ident).then_inc(t_done, 1)

            def values(u):
                hh, i = UNITS[u]
                rows = hr[hh // G]
                pe.wait_ge(pt_act, u + 1)
                pe.wait_ge(pt_dve, u + 1)
                if u:
                    pe.wait_ge(o_evac, u)
                out = ps[rows, 7, 0:P]
                for r in range(2):
                    for c in range(i + 1):
                        mm(out, vn[:, c, r * P + rows.start:r * P + rows.stop], prT[:, u % 2, r, c * P:(c + 1) * P],
                           start=(r == 0 and c == 0), stop=False)
                mm(out, vcp[0:NCP, rows], pcT[0:NCP, u % 2, :], start=False, stop=True).then_inc(pv_done, 1)

            NU = len(UNITS)
            for u in range(NU + 2):
                if u < NU:
                    scores(u)
                if 1 <= u <= NU:
                    flip(u - 1)
                if u >= 2:
                    values(u - 2)

            pe.wait_ge(o_evac, NU)
            mm(ps[0:64, 0, 0:NB], qs[:, :, :], sT[:, T_KS, :], start=True, stop=True)
            mm(ps[0:64, 0, NB:2 * NB], qs[:, :, :], sT[:, T_KW, :], start=True, stop=True).then_inc(snew_done, 1)
            pe.wait_ge(pool_ready, 1)
            for t in range(2):
                mm(ps[:, 4 + t, :], par_("pw", t * P, (t + 1) * P), md[:, t, :], start=True, stop=True)
                last = mm(ps[:, 6, t * NB:(t + 1) * NB], par_("pw", t * P, (t + 1) * P), mds[:, t, :], start=True, stop=True)
            last.then_inc(pool_mm, 1)
            pe.wait_ge(hs_moved, 16 * 16)
            for t in range(2):
                last = nc.tensor.transpose(ps[:, 7, t * NB:(t + 1) * NB], hs8[0:NB, t * P:(t + 1) * P], ident[0:NB, 0:NB])
            last.then_inc(shT_done, 1)
            pe.wait_ge(win_landed, 32)
            for b in range(NB):
                if b >= 2:
                    pe.wait_ge(wsc_evac, b - 1)
                mm(ps[0:NH, 1 + b % 2, :], qs[:, b, :], kwin[:, b, :], start=True, stop=True).then_inc(wsc_done, 1)
            pe.wait_ge(imp_in, 1)
            mm(ps[0:64, 3, 0:NCB], con_("grp", rows=64), scm[:, 0:NCB], start=True, stop=True).then_inc(imp_done, 1)
            pe.wait_ge(sp_ready, 1)
            for c in range(NPG):
                nc.tensor.transpose(ps[:, 4 + c // 8, (c % 8) * 64:(c % 8 + 1) * 64], sall[:, c * P:(c + 1) * P], ident[0:64, 0:64])
            for c in range(ST):
                nc.tensor.transpose(ps[:, 6, c * 64:(c + 1) * 64], swin[0:64, c * P:(c + 1) * P], ident[0:64, 0:64])
            nc.tensor.transpose(ps[0:NCB, 0, 0:64], scm[:, 0:NCB], ident[0:64, 0:64])
            nc.tensor.transpose(ps[0:NB, 1, 0:64], sall[:, NPG * P:NPG * P + NB], ident[0:64, 0:64])
            nc.tensor.transpose(ps[0:NB, 2, 0:64], swin[0:64, S:S + NB], ident[0:64, 0:64]).then_inc(spT_done, 1)
            pe.wait_ge(spT_evac, 1)
            for b in range(NB):
                pe.wait_ge(vcache_landed[b % 3], 16 * NPG * (b // 3 + 1))
                out, cols = ps[:, 7, b * 8:(b + 1) * 8], slice(b * 8, (b + 1) * 8)
                for c in range(NPG):
                    mm(out, vpages[:, b % 3, c, :], ptS[:, c, cols], start=(c == 0), stop=False)
                for c in range(ST):
                    mm(out, vwin[:, b, c, :], ptS[:, NPG + c, cols], start=False, stop=False)
                mm(out, vc[0:NCB, b, :], ptS[0:NCB, 20, cols], start=False, stop=False)
                mm(out, sn[0:NB, 7 * P:8 * P], ptS[0:NB, 21, cols], start=False, stop=False)
                mm(out, sn[0:NB, 8 * P:9 * P], ptS[0:NB, 22, cols], start=False, stop=True).then_inc(spv_done, 1)

            pe.wait_ge(mix_ready, 1)
            for m, (kind, t, slots) in enumerate(PART2):
                if m >= 2:
                    pe.wait_ge(evac_dve, m - 1)
                if m == KD:
                    norm_sums(1)
                product(len(PART1) + m, kind, t, slots)
            norm_sums(2)

        @block.scalar
        def _(act):
            A = nc.scalar.activation
            chain = [0]

            def link(ins):
                chain[0] += 1
                ins.then_inc(act_step, 1)
                act.wait_ge(act_step, chain[0])

            def squares(n, k):
                if n * KD + k >= 2:
                    act.wait_ge(sq_used, n * KD + k - 1)
                A(sq[:, k % 2, :], x[:, k, :], ACT.Square).then_inc(sq_ready, 1)

            def normed(n, shift):
                for k in range(KD):
                    act.wait_ge(xn_ready, n * KD + k + 1)
                    A(h[:, k, 0:S], h[:, k, 0:S], ACT.Identity, bias=mod[:, shift + k, 0:1], scale=ab[:, k, 0:1])\
                        .then_inc(h_prompt, 1)

            act.wait_ge(par_landed, 16)
            A(sc2[:, :, :], par_("c").rearrange("p (k n) -> p k n", k=KD), ACT.Exp, scale=-1.0).then_inc(silu_exp, 1)
            for k in range(KD):
                act.wait_ge(x_landed, 16 * KD)
                squares(0, k)
            act.wait_ge(var_ready, 1)
            A(rstd[:, :], rstd[:, :], ACT.Sqrt).then_inc(root_ready, 1)
            e = 0
            for ev in EVENTS:
                if ev[0] == "lin":
                    n = ev[1]
                    kind, t, _ = PART1[n]
                    act.wait_ge(slot_done, SLOT0[n + 1])
                    if kind == "ada":
                        A(mod[:, t, :], ps[:, 2 + n % 2, 0:9], ACT.Identity, bias=par_("ada_b", t, t + 1)).then_inc(evac_act, 1)
                        if t == 15:
                            normed(0, 0)
                        continue
                    scale = SCALE if T_MK <= t < T_MK + 2 else 1.0
                    A(sT[:, t, :], ps[:, 2 + n % 2, 0:NB], ACT.Identity, scale=scale)
                    if t < N_FM:
                        A(pT[:, t, :], ps[:, n % 2, :], ACT.Identity, scale=scale).then_inc(evac_act, 1)
                    elif t < T_MV:
                        A(vn[:, :, (t - T_VS) * P:(t - T_VS + 1) * P], ps[:, n % 2, :].rearrange("p (i n) -> p i n", i=ST),
                          ACT.Identity).then_inc(evac_act, 1)
                    else:
                        if t == T_MV:
                            act.wait_ge(memset_done, 2)
                        v = ps[:, n % 2, :].rearrange("p (i a d) -> p i a d", i=ST, a=2)
                        A(vm[:, :, 2 * (t - T_MV):2 * (t - T_MV) + 2, 0:HD], v, ACT.Identity).then_inc(evac_act, 1)
                    if t == 3:
                        act.wait_ge(evac_act, n + 1)
                        act.wait_ge(memset_done, 2)
                        for hh in range(NH):
                            rows = hr[hh // G]
                            last = A(qs[rows, :, hh], sT[rows, hh % G, :], ACT.Identity)
                        last.then_inc(qs_ready, 1)
                elif ev[0] == "slc":
                    _, b, s = ev
                    e += 1
                    act.wait_ge(slc_scored, e)
                    if b and s == 0:
                        act.wait_ge(sst_moved, 32 * b)
                    for j in range(2):
                        at = (2 * s + j) * 512
                        last = A(sst[0:NH, at:at + 512], ps[0:NH, 6 + j, :], ACT.Identity)
                    last.then_inc(slc_evac, 1)
                elif ev[0] == "blocks":
                    act.wait_ge(blocks_done, ev[1] + 1)
                    A(kct[:, 0:NCB], ps[:, 4, 0:NCB], ACT.Identity, bias=par_("bk"))
                    A(vc[0:NCB, ev[1], :], ps[0:NCB, 5, 0:P], ACT.Identity).then_inc(blocks_evac, 1)
                else:
                    b = ev[1]
                    act.wait_ge(cmp_scored, b + 1)
                    A(sst[0:NH, 2048:2048 + NCB], ps[0:NH, 4, 0:NCB], ACT.Identity).then_inc(cmp_evac, 1)
                    act.wait_ge(cmp_evac, b + 1)
                    act.wait_ge(slc_evac, 2 * b + 2)
                    act.dma_start(sall[8 * b:8 * b + 8, 0:2048], sst[0:NH, 0:2048]).then_inc(sst_moved, 16)
                    act.dma_start(scm[8 * b:8 * b + 8, 0:NCB], sst[0:NH, 2048:2048 + NCB]).then_inc(sst_moved, 16)

            act.wait_ge(kn_T, 1)
            act.wait_ge(sst_moved, 32 * NB)
            act.wait_ge(pooled_ready, NB + 1)
            for t in range(2):
                last = A(kN[:, t, :, :], ps[:, 4 + t, :].rearrange("p (i n) -> p i n", i=ST), ACT.Identity)
            last.then_inc(kn_evac, 1)
            act.wait_ge(sn_T, 1)
            for c in range(3):
                n = min(512, 1152 - 512 * c)
                last = A(sn[0:NB, 512 * c:512 * c + n], ps[0:NB, c, 0:n], ACT.Identity)
            last.then_inc(sn_evac, 1)
            act.wait_ge(g_T, 1)
            A(gN[:, :, :], ps[:, 3, :].rearrange("p (i n) -> p i n", i=ST)[:, :, 64:88], ACT.Exp, scale=-1.0).then_inc(g_exp, 1)
            act.wait_ge(blocks_done, NB + 1)
            A(kct[:, 0:NCP], ps[:, 6, 0:NCP], ACT.Identity, bias=par_("bk"))
            A(vcp[0:NCP, :], ps[0:NCP, 7, 0:P], ACT.Identity).then_inc(blocks_evac, 1)
            act.wait_ge(az_ready, 1)
            link(A(lfo[0:4, :], lfo[0:4, :], ACT.Exp, scale=-1.0))
            A(lfo[0:4, :], lfo[0:4, :], ACT.Ln, bias=1.0).then_inc(ln_ready, 1)
            act.wait_ge(r_T, 1)
            r4 = ps[:, 0, 0:ST * 36].rearrange("p (i n) -> p i n", i=ST)
            A(rT[:, :, :], r4, ACT.Identity)
            A(enm[:, :, :], r4[:, :, 32:36], ACT.Exp, scale=-1.0).then_inc(rt_evac, 1)
            act.wait_ge(rt_evac, 1)
            for q in range(16):
                hh, j = q // 4, q % 4
                act.wait_ge(dmask_done, q + 1)
                last = A(dt_[:, q % 2, 0:P], dt_[:, q % 2, 0:P], ACT.Exp, bias=rT[:, j, hh:hh + 1])
                if j < 3:
                    last = A(dt_[:, q % 2, P:S - j * P], ps[:, 7, (j + 1) * P:S], ACT.Exp, bias=rT[:, j, hh:hh + 1])
                last.then_inc(dt_done, 1)
            act.wait_ge(w_done, 16)
            A(emos[:, :, :], sT[:, T_MO:T_MO + 2, :], ACT.Exp, scale=-1.0)
            A(dt_[:, :, :], pT[:, T_MO:T_MO + 2, :], ACT.Exp, scale=-1.0).then_inc(emo_ready, 1)
            act.wait_ge(saz_ready, 1)
            link(A(mv[:, 4:5], mv[:, 4:5], ACT.Exp, scale=-1.0))
            A(mv[:, 4:5], mv[:, 4:5], ACT.Ln, bias=1.0).then_inc(sln_ready, 1)
            act.wait_ge(sexp_in, 1)
            A(mv[:, 8:11], mv[:, 8:11], ACT.Exp).then_inc(sexp_ready, 1)
            act.wait_ge(pcx_ready, 1)
            A(pc[:, :, 0:NCP], pc[:, :, 0:NCP], ACT.Exp, scale=SCALE).then_inc(pcx_exp, 1)
            NU = len(UNITS)
            for u in range(NU + 1):
                if u < NU:
                    hh, i = UNITS[u]
                    act.wait_ge(mx_ready, u + 1)
                    if u >= 2:
                        act.wait_ge(t_done, u - 1)
                    for r in range(2):
                        last = A(pr[:, u % 2, r, 0:(i + 1) * P], ps[:, 2 * (u % 2) + r, 0:(i + 1) * P], ACT.Exp,
                                 bias=nmx[:, u % 2, r:r + 1], scale=SCALE, accum_out=sm[:, u % 2, r:r + 1])
                    last.then_inc(p_exp, 1)
                if u >= 1:
                    v = u - 1
                    n = (UNITS[v][1] + 1) * P
                    act.wait_ge(t_done, v + 1)
                    if v >= 2:
                        act.wait_ge(pv_done, v - 1)
                    A(prT[:, v % 2, 0, 0:n], ps[:, 4, 0:n], ACT.Identity).then_inc(pt_act, 1)
            act.wait_ge(o_evac, NU)
            for b in range(NB):
                act.wait_ge(wsc_done, b + 1)
                if b:
                    act.wait_ge(w_moved, 16 * b)
                A(sst2[0:NH, :], ps[0:NH, 1 + b % 2, :], ACT.Identity).then_inc(wsc_evac, 1)
                act.wait_ge(wsc_evac, b + 1)
                act.dma_start(swin[8 * b:8 * b + 8, 0:S], sst2[0:NH, :]).then_inc(w_moved, 16)
            act.wait_ge(sgate_moved, 16 * NB)
            A(sg[:, 0:3], sg[:, 0:3], ACT.Exp, scale=-1.0).then_inc(sg_exp, 1)
            act.wait_ge(sx_in, 1)
            A(scm[:, 0:NCB], scm[:, 0:NCB], ACT.Exp, bias=ssx[:, 1:2], scale=SCALE, accum_out=ssx[:, 2:3]).then_inc(sx_out, 1)
            act.wait_ge(sx_in, 2)
            A(swin[0:64, 0:T], swin[0:64, 0:T], ACT.Exp, bias=ssx[:, 4:5], scale=SCALE, accum_out=ssx[:, 5:6]).then_inc(sx_out, 1)
            act.wait_ge(sx_in, 3)
            A(sall[:, :], sall[:, :], ACT.Exp, bias=ssx[:, 7:8], scale=SCALE, accum_out=ssx[:, 8:9]).then_inc(sx_out, 1)
            for k in range(KD):
                act.wait_ge(x_ready, k + 1)
                squares(1, k)
            act.wait_ge(var_ready, 2)
            A(rstd[:, :], rstd[:, :], ACT.Sqrt).then_inc(root_ready, 1)
            normed(1, 24)
            for m in range(2 * FC):
                n = N_UP0 + m
                t = PART2[KD + m][1]
                act.wait_ge(slot_done, SLOT0[n + 1])
                if m >= 2:
                    act.wait_ge(silu_in if m % 2 == 0 else evac_dve, m // 2 if m % 2 == 0 else KD + m - 1)
                if m % 2 == 0 and m >= 2:
                    act.wait_ge(silu_out, m // 2)
                cw = par_("conv_w", 3 * t + 2, 3 * t + 3)
                A(yab[:, m % 2, 0:S], ps[:, n % 2, :], ACT.Identity, bias=par_("conv_b", t, t + 1), scale=cw).then_inc(y_ready, 1)
                if m % 2 == 0:
                    act.wait_ge(silu_in, m // 2 + 1)
                    if m >= 2:
                        act.wait_ge(evac_dve, KD + m)
                    A(sil[:, :], yab[:, 0, :], ACT.Silu).then_inc(silu_out, 1)
            for k in range(KD):
                act.wait_ge(x_ready, KD + k + 1)
                squares(2, k)
            act.wait_ge(var_ready, 3)
            A(rstd[:, :], rstd[:, :], ACT.Sqrt).then_inc(root_ready, 1)

        @block.vector
        def _(dve):
            V = nc.vector
            chain = [0]

            def link(ins):
                chain[0] += 1
                ins.then_inc(dve_step, 1)
                dve.wait_ge(dve_step, chain[0])

            def root(n):
                dve.wait_ge(sq_used, (n + 1) * KD)
                V.tensor_scalar(rstd[:, 0:S], ps[:, 4, :], EPS, None, ALU.add)
                V.tensor_scalar(rstd[:, S:T], ps[:, 5, 0:NB], EPS, None, ALU.add).then_inc(var_ready, 1)
                dve.wait_ge(root_ready, n + 1)
                link(V.reciprocal(rstd[:, :], rstd[:, :]))

            def normed(n, gain, scale, shift):
                link(V.scalar_tensor_tensor(ab[:, :, :], mod[:, scale:scale + KD, :], 1.0,
                                            par_(gain).unsqueeze(2).broadcast_to([P, KD, 9]), ALU.add, ALU.mult))
                for k in range(KD):
                    V.tensor_tensor(h[:, k, :], x[:, k, :], rstd[:, :], ALU.mult).then_inc(xn_ready, 1)
                    dve.wait_ge(xn_ready, n * KD + k + 1)
                    link(V.tensor_tensor(h[:, k, S:T], h[:, k, S:T], ab[:, k, 1:9], ALU.mult))
                    V.tensor_tensor(h[:, k, S:T], h[:, k, S:T], mod[:, shift + k, 1:9], ALU.add).then_inc(h_sample, 1)

            def compress(src_k, src_v, nseg, at, seg4):
                for kv, src in enumerate((src_k, src_v)):
                    for half, dst in enumerate((poolA, poolB)):
                        w = par_("wpos", 32 * kv + 16 * half, 32 * kv + 16 * half + 16)
                        if seg4:
                            o = tmp[:, 0:nseg * 16].rearrange("p (a n j) -> p a n j", a=HALF, j=16)
                            ww = w.unsqueeze(1).unsqueeze(1).broadcast_to([P, HALF, 8, 16])
                        else:
                            o = tmp[:, 0:nseg * 16].rearrange("p (n j) -> p n j", j=16)
                            ww = w.unsqueeze(1).broadcast_to([P, nseg, 16])
                        link(V.tensor_tensor(o, src, ww, ALU.mult))
                        last = V.tensor_reduce(dst[:, kv, at:at + nseg],
                                               tmp[:, 0:nseg * 16].rearrange("p (n j) -> p n j", j=16), AX, ALU.add)
                        if not (kv and half):
                            link(last)
                return last

            dve.wait_ge(silu_exp, 1)
            link(V.tensor_scalar(sc2[:, :, :], sc2[:, :, :], 1.0, None, ALU.add))
            link(V.reciprocal(sc2[:, :, :], sc2[:, :, :]))
            V.tensor_tensor(sc[:, :, :], sc2[:, :, :], par_("c").rearrange("p (k n) -> p k n", k=KD), ALU.mult).then_inc(silu_ready, 1)
            root(0)
            dve.wait_ge(evac_act, 16)
            dve.wait_ge(x_landed, 16 * KD)
            normed(0, "g1", 8, 0)

            nb = 0
            for b in range(NB):
                for s in range(2):
                    dve.wait_ge(cache_landed[s], 16 * HALF * (b + 1))
                    pg = pages[:, s, :, :]
                    compress(pg[:, :, 0:P].rearrange("p a (n j) -> p a n j", j=16),
                             pg[:, :, 2 * P:3 * P].rearrange("p a (n j) -> p a n j", j=16), 64, 64 * s, True).then_inc(comp_done, 1)
                    dve.wait_ge(comp_done, 2 * b + s + 1)
                if b:
                    dve.wait_ge(blocks_done, b)
                V.tensor_tensor(pooled[:, :, 0:NCB], poolA[:, :, 0:NCB], poolB[:, :, 1:NCB + 1], ALU.add).then_inc(pooled_ready, 1)
                dve.wait_ge(pooled_ready, b + 1)

            dve.wait_ge(evac_act, len(PART1))
            link(compress(pT[:, T_KC, :].rearrange("p (n j) -> p n j", j=16),
                          pT[:, T_VC, :].rearrange("p (n j) -> p n j", j=16), S // 16, 0, False))
            dve.wait_ge(blocks_done, NB)
            V.tensor_tensor(pooled[:, :, 0:NCP], poolA[:, :, 0:NCP], poolB[:, :, 1:NCP + 1], ALU.add).then_inc(pooled_ready, 1)

            dve.wait_ge(pooled_ready, NB + 1)
            link(V.memset(r36[0:36, :], 0.0))
            link(V.memset(zro[0:4, :], 0.0))
            link(V.tensor_scalar(r36[0:4, :], pT[0:4, T_G, :], par_("gate_b", hi=4), None, ALU.add))
            link(V.tensor_scalar(bro[0:4, :], pT[32:36, T_G, :], par_("gate_b", lo=32, hi=36), None, ALU.add))
            V.scalar_tensor_tensor(lfo[0:4, :], bro[0:4, :], -1.0, bro[0:4, :], ALU.mult, ALU.max).then_inc(az_ready, 1)
            dve.wait_ge(ln_ready, 1)
            link(V.scalar_tensor_tensor(lfo[0:4, :], bro[0:4, :], 0.0, lfo[0:4, :], ALU.min, ALU.subtract))
            link(V.tensor_tensor_scan(bro[0:4, :], lfo[0:4, :], zro[0:4, :], 0.0, ALU.add, ALU.add))
            link(V.tensor_tensor(r36[0:4, :], r36[0:4, :], bro[0:4, :], ALU.subtract))
            link(V.tensor_tensor_scan(mro[0:4, :], r36[0:4, :], zro[0:4, :], 0.0, ALU.max, ALU.max))
            link(V.tensor_tensor(r36[32:36, :], bro[0:4, :], mro[0:4, :], ALU.add))
            link(V.tensor_copy(mout[0:4, 0:1], r36[32:36, S - 1:S]))
            V.tensor_scalar(mro[0:4, :], mro[0:4, :], -1.0, None, ALU.mult).then_inc(rows_ready, 1)

            dve.wait_ge(rt_evac, 1)
            dve.wait_ge(kn_evac, 1)
            for hh in range(4):
                dve.wait_ge(bc_done, hh + 1)
                for j in range(ST):
                    q = 4 * hh + j
                    V.tensor_tensor(dt_[:, q % 2, 0:P], ps[:, 7, j * P:(j + 1) * P], con_("ct"), ALU.add).then_inc(dmask_done, 1)
                    dve.wait_ge(dt_done, q + 1)
                    dve.wait_ge(mscore_done, q + 1)
                    if hh and j == 0:
                        dve.wait_ge(num_done, hh)
                    n = S - j * P
                    V.tensor_tensor(wj[:, OFF[j]:OFF[j] + n], ps[:, 4 + q % 2, 0:n], dt_[:, q % 2, 0:n], ALU.mult)
                    if j == 0 and hh:
                        dve.wait_ge(num_evac, hh)
                    V.tensor_scalar(wk[:, j, :], kN[:, hh // 2, j, (hh % 2) * HD:(hh % 2 + 1) * HD], dt_[:, q % 2, n - 1:n], None,
                                    ALU.mult).then_inc(w_done, 1)
                    dve.wait_ge(w_done, q + 1)
                dve.wait_ge(num_done, hh + 1)
                num = ps[:, 6, 0:4 * 65].rearrange("p (i n) -> p i n", i=ST)
                link(V.tensor_copy(d4[:, 0:4], num[:, :, HD]))
                link(V.scalar_tensor_tensor(d4[:, 4:8], d4[:, 0:4], -1.0, d4[:, 0:4], ALU.mult, ALU.max))
                link(V.tensor_tensor(d4[:, 4:8], d4[:, 4:8], enm[:, :, hh], ALU.max))
                link(V.reciprocal(d4[:, 4:8], d4[:, 4:8]))
                V.tensor_tensor(hN[:, :, hh * HD:(hh + 1) * HD], num[:, :, 0:HD], d4[:, 4:8].unsqueeze(2).broadcast_to([P, ST, HD]),
                                ALU.mult).then_inc(num_evac, 1)
            link(V.tensor_copy(cout[0:HD, :, :], ps[0:HD, 3, 0:260].rearrange("p (h n) -> p h n", h=4)))
            dve.wait_ge(emo_ready, 1)
            link(V.tensor_scalar(dt_[:, :, :], dt_[:, :, :], 1.0, None, ALU.add))
            link(V.reciprocal(dt_[:, :, :], dt_[:, :, :]))
            dve.wait_ge(hT_done, 1)
            V.tensor_tensor(h[:, 4:6, 0:S], ps[:, 1:3, :], dt_[:, :, :], ALU.mult).then_inc(mmix_ready, 1)

            dve.wait_ge(rows_moved, 16 * 48)
            dve.wait_ge(rec_landed, 32)
            q_, k_, v_ = smr[:, 0:64], smr[:, 64:128], smr[:, 128:144]
            link(V.tensor_tensor(mv[:, 0:1], smr[:, 144:145], par_("igb"), ALU.add))
            link(V.tensor_tensor(mv[:, 1:2], smr[:, 145:146], par_("fgb"), ALU.add))
            V.scalar_tensor_tensor(mv[:, 4:5], mv[:, 1:2], -1.0, mv[:, 1:2], ALU.mult, ALU.max).then_inc(saz_ready, 1)
            dve.wait_ge(sln_ready, 1)
            link(V.scalar_tensor_tensor(mv[:, 1:2], mv[:, 1:2], 0.0, mv[:, 4:5], ALU.min, ALU.subtract))
            link(V.tensor_tensor(mv[:, 2:3], mv[:, 1:2], par_("mm"), ALU.add))
            link(V.tensor_tensor(mv[:, 3:4], mv[:, 2:3], mv[:, 0:1], ALU.max))
            V.tensor_tensor(mv[:, 8:9], mv[:, 0:1], mv[:, 3:4], ALU.subtract)
            V.tensor_tensor(mv[:, 9:10], mv[:, 2:3], mv[:, 3:4], ALU.subtract)
            V.tensor_scalar(mv[:, 10:11], mv[:, 3:4], -1.0, None, ALU.mult).then_inc(sexp_in, 1)
            c_de = cst[:, :].rearrange("p (d e) -> p d e", e=16)
            t_ed = ctmp[:, :].rearrange("p (e d) -> p e d", d=64)
            t_de = ctmp[:, :].rearrange("p (d e) -> p d e", e=16)
            link(V.tensor_tensor(t_ed, c_de.rearrange("p d e -> p e d"), q_.unsqueeze(1).broadcast_to([P, 16, 64]), ALU.mult))
            link(V.tensor_reduce(qc[:, :], t_ed, AX, ALU.add))
            link(V.tensor_tensor(ctmp[:, 0:64], q_, k_, ALU.mult))
            link(V.tensor_reduce(mv[:, 11:12], ctmp[:, 0:64], AX, ALU.add))
            link(V.tensor_tensor(ctmp[:, 0:64], q_, par_("mn"), ALU.mult))
            link(V.tensor_reduce(mv[:, 12:13], ctmp[:, 0:64], AX, ALU.add))
            dve.wait_ge(sexp_ready, 1)
            link(V.tensor_tensor(mv[:, 11:12], mv[:, 11:12], mv[:, 8:9], ALU.mult))
            link(V.scalar_tensor_tensor(mv[:, 13:14], mv[:, 12:13], mv[:, 9:10], mv[:, 11:12], ALU.mult, ALU.add))
            link(V.scalar_tensor_tensor(mv[:, 14:15], mv[:, 13:14], -1.0, mv[:, 13:14], ALU.mult, ALU.max))
            link(V.tensor_tensor(mv[:, 14:15], mv[:, 14:15], mv[:, 10:11], ALU.max))
            link(V.reciprocal(mv[:, 14:15], mv[:, 14:15]))
            link(V.tensor_scalar(qc[:, :], qc[:, :], mv[:, 9:10], None, ALU.mult))
            link(V.scalar_tensor_tensor(shh[:, :], v_, mv[:, 11:12], qc[:, :], ALU.mult, ALU.add))
            link(V.tensor_scalar(shh[:, :], shh[:, :], mv[:, 14:15], None, ALU.mult))
            link(V.tensor_copy(t_de, k_.unsqueeze(2).broadcast_to([P, 64, 16])))
            link(V.scalar_tensor_tensor(t_de, t_de, mv[:, 8:9], v_.unsqueeze(1).broadcast_to([P, 64, 16]), ALU.mult, ALU.mult))
            link(V.scalar_tensor_tensor(cst[:, :], cst[:, :], mv[:, 9:10], ctmp[:, :], ALU.mult, ALU.add))
            link(V.tensor_scalar(smr[:, 146:210], k_, mv[:, 8:9], None, ALU.mult))
            V.scalar_tensor_tensor(smr[:, 146:210], par_("mn"), mv[:, 9:10], smr[:, 146:210], ALU.mult, ALU.add)\
                .then_inc(srec_ready, 1)
            dve.wait_ge(srec_ready, 1)

            dve.wait_ge(g_exp, 1)
            link(V.tensor_scalar(gN[:, :, :], gN[:, :, :], 1.0, None, ALU.add))
            link(V.reciprocal(gN[:, :, :], gN[:, :, :]))

            for t in range(2):
                link(V.memset(zp[:, 0, 0:15], 0.0))
                buf = [zp[:, 0, :], zp[:, 1, :]]
                link(V.tensor_copy(zp[:, 0, 15:15 + S], pT[:, T_PU + t, :]))
                lo, cur = 0, 0
                for w in (1, 2, 4, 8)[:2 * t + 2]:
                    lo += w
                    top = w == (2, 8)[t]
                    if top:
                        link(V.tensor_copy(md[hr[0], t, :], buf[cur][hr[0], 15:15 + S]))
                    r = slice(HD, P) if top else slice(0, P)
                    link(V.tensor_tensor(buf[1 - cur][r, lo:15 + S], buf[cur][r, lo:15 + S], buf[cur][r, lo - w:15 + S - w], ALU.add))
                    cur = 1 - cur
                link(V.tensor_copy(md[hr[1], t, :], buf[cur][hr[1], 15:15 + S]))
                link(V.tensor_tensor(zp[:, 1, 15:31], md[:, t, 0:16], con_("rcnt", 16 * t, 16 * t + 16), ALU.mult))
                link(V.tensor_tensor(md[:, t, 0:16], zp[:, 1, 15:31], pT[:, T_PU + t, 0:16], ALU.subtract))
                link(V.scalar_tensor_tensor(md[:, t, 16:S], md[:, t, 16:S], con_("rw", t, t + 1), pT[:, T_PU + t, 16:S],
                                            ALU.mult, ALU.subtract))
                link(V.tensor_copy(zs[:, t, :, 15], sT[:, T_PU + t, :]))
                for g in range(2):
                    w = (2, 4, 8, 16)[2 * t + g]
                    link(V.tensor_reduce(zsum[hr[g], t, :], zs[hr[g], t, :, 16 - w:16], AX, ALU.add))
                last = V.scalar_tensor_tensor(mds[:, t, :], zsum[:, t, :], con_("rw", t, t + 1), sT[:, T_PU + t, :],
                                              ALU.mult, ALU.subtract)
            last.then_inc(pool_ready, 1)
            dve.wait_ge(pool_ready, 1)

            dve.wait_ge(csc_done, 1)
            for half in range(2):
                s4 = ps[:, half, :].rearrange("p (a i n) -> p a i n", a=4, i=ST)[:, :, :, 0:NCP]
                p4 = pc[:, 16 * half:16 * half + 16, :].rearrange("p (a i) n -> p a i n", a=4)[:, :, :, 0:NCP]
                madd = con_("cadd").rearrange("p (i n) -> p i n", i=ST).unsqueeze(1).broadcast_to([P, 4, ST, NCP])
                link(V.tensor_tensor(p4, s4, madd, ALU.add))
            link(V.tensor_reduce(mx[:, 0, :], pc[:, :, 0:NCP], AX, ALU.max))
            V.tensor_tensor(pc[:, :, 0:NCP], pc[:, :, 0:NCP], mx[:, 0, :].unsqueeze(2).broadcast_to([P, 32, NCP]), ALU.subtract)\
                .then_inc(pcx_ready, 1)
            dve.wait_ge(pcx_exp, 1)
            for half in range(2):
                p4 = pc[:, 16 * half:16 * half + 16, :].rearrange("p (a i) n -> p a i n", a=4)[:, :, :, 0:NCP]
                mmul = con_("cmul").rearrange("p (i n) -> p i n", i=ST).unsqueeze(1).broadcast_to([P, 4, ST, NCP])
                link(V.tensor_tensor(p4, p4, mmul, ALU.mult))
            link(V.tensor_reduce(mx[:, 1, :], pc[:, :, 0:NCP], AX, ALU.add))
            link(V.tensor_scalar(mx[:, 1, :], mx[:, 1, :], float(np.finfo(np.float32).tiny), None, ALU.max))
            link(V.reciprocal(mx[:, 2, :], mx[:, 1, :]))
            g0 = gN[:, :, 0:22:3].rearrange("p i h -> p h i")
            link(V.tensor_tensor(mx[:, 3, :].rearrange("p (h i) -> p h i", h=NH), mx[:, 2, :].rearrange("p (h i) -> p h i", h=NH),
                                 g0, ALU.mult))
            V.tensor_tensor(pc[:, :, 0:NCP], pc[:, :, 0:NCP], mx[:, 3, :].unsqueeze(2).broadcast_to([P, 32, NCP]), ALU.mult)\
                .then_inc(pc_ready, 1)

            NU = len(UNITS)
            for u in range(NU + 2):
                if u < NU:
                    hh, i = UNITS[u]
                    a = u % 2
                    two = ps[:, 2 * a:2 * a + 2, :]
                    dve.wait_ge(qk_done, u + 1)
                    d = two[:, :, i * P:(i + 1) * P]
                    link(V.tensor_tensor(d, d, con_("cq").unsqueeze(1).broadcast_to([P, 2, P]), ALU.add))
                    link(V.tensor_reduce(nmx[:, a, :], two[:, :, 0:(i + 1) * P], AX, ALU.max))
                    V.tensor_scalar(nmx[:, a, :], nmx[:, a, :], -SCALE, None, ALU.mult).then_inc(mx_ready, 1)
                if 1 <= u <= NU:
                    v = u - 1
                    n = (UNITS[v][1] + 1) * P
                    dve.wait_ge(t_done, v + 1)
                    if v >= 2:
                        dve.wait_ge(pv_done, v - 1)
                    V.tensor_copy(prT[:, v % 2, 1, 0:n], ps[:, 5, 0:n])
                    V.tensor_copy(pcT[0:NCP, v % 2, :], ps[0:NCP, 6, 0:P]).then_inc(pt_dve, 1)
                    dve.wait_ge(pt_dve, v + 1)
                if u < NU:
                    dve.wait_ge(p_exp, u + 1)
                    link(V.reciprocal(fac[:, a, :], sm[:, a, :]))
                    link(V.tensor_tensor(fac[:, a, :], fac[:, a, :], gN[:, i, 3 * hh + 1:3 * hh + 3], ALU.mult))
                    for r in range(2):
                        last = V.tensor_scalar(pr[:, a, r, 0:(i + 1) * P], pr[:, a, r, 0:(i + 1) * P], fac[:, a, r:r + 1], None,
                                               ALU.mult)
                    last.then_inc(p_ready, 1)
                if u >= 2:
                    hh, i = UNITS[u - 2]
                    rows = hr[hh // G]
                    dve.wait_ge(pv_done, u - 1)
                    V.tensor_copy(h[rows, hh % G, i * P:(i + 1) * P], ps[rows, 7, 0:P]).then_inc(o_evac, 1)

            dve.wait_ge(pool_mm, 1)
            for t in range(2):
                V.tensor_scalar(h[:, 6 + t, 0:S], ps[:, 4 + t, :], par_("pool_s", t, t + 1), None, ALU.mult)
                link(V.tensor_scalar(h[:, 6 + t, S:T], ps[:, 6, t * NB:(t + 1) * NB], par_("pool_s", t, t + 1), None, ALU.mult))
            link(V.tensor_scalar(emos[:, :, :], emos[:, :, :], 1.0, None, ALU.add))
            link(V.reciprocal(emos[:, :, :], emos[:, :, :]))
            dve.wait_ge(shT_done, 1)
            link(V.tensor_tensor(h[:, 4:6, S:T], ps[:, 7, 0:2 * NB].rearrange("p (t b) -> p t b", t=2), emos[:, :, :], ALU.mult))

            dve.wait_ge(snew_done, 1)
            dve.wait_ge(sst_moved, 32 * NB)
            link(V.tensor_tensor(sall[:, NPG * P:NPG * P + NB], ps[0:64, 0, 0:NB], con_("newm", rows=64), ALU.add))
            link(V.tensor_tensor(swin[0:64, S:T], ps[0:64, 0, NB:2 * NB], con_("newm", rows=64), ALU.add))
            link(V.tensor_reduce(ssx[:, 0:1], scm[:, 0:NCB], AX, ALU.max))
            V.tensor_scalar(ssx[:, 1:2], ssx[:, 0:1], -SCALE, None, ALU.mult).then_inc(sx_in, 1)
            dve.wait_ge(sg_exp, 1)
            link(V.tensor_scalar(sg[:, 0:3], sg[:, 0:3], 1.0, None, ALU.add))
            link(V.reciprocal(sg[:, 0:3], sg[:, 0:3]))
            dve.wait_ge(sx_out, 1)
            link(V.reciprocal(ssx[:, 9:10], ssx[:, 2:3]))
            V.tensor_scalar(scm[:, 0:NCB], scm[:, 0:NCB], ssx[:, 9:10], None, ALU.mult).then_inc(imp_in, 1)
            dve.wait_ge(w_moved, 16 * NB)
            link(V.memset(swin[0:64, 0:1], NEG))
            link(V.tensor_reduce(ssx[:, 3:4], swin[0:64, 0:T], AX, ALU.max))
            V.tensor_scalar(ssx[:, 4:5], ssx[:, 3:4], -SCALE, None, ALU.mult).then_inc(sx_in, 1)
            link(V.memset(simp[0:64, :], 0.0))
            dve.wait_ge(imp_done, 1)
            link(V.tensor_copy(simp[0:64, 1:1 + NCB], ps[0:64, 3, 0:NCB]))
            link(V.tensor_reduce(sel[:, 0, 0:NSB], simp[0:64, 0:132].rearrange("p (n r) -> p n r", r=4), AX, ALU.add))
            link(V.tensor_tensor(sel[:, 0, 0:NSB], sel[:, 0, 0:NSB], simp[0:64, 4:133:4], ALU.add))
            link(V.memset(sel[:, 0, 0:1], 1e6))
            link(V.memset(sel[:, 0, NSB - 2:NSB], 1e6))
            s_i = sel[:, 0, 0:NSB].unsqueeze(1).broadcast_to([64, NSB, NSB])
            s_j = sel[:, 0, 0:NSB].unsqueeze(2).broadcast_to([64, NSB, NSB])
            rk = rank[0:64, :].rearrange("p (j i) -> p j i", j=NSB)
            te = tie[0:64, :].rearrange("p (j i) -> p j i", j=NSB)
            link(V.tensor_tensor(rk, s_i, s_j, ALU.is_gt))
            link(V.tensor_tensor(te, s_i, s_j, ALU.is_equal))
            link(V.tensor_tensor(tie[0:64, :], tie[0:64, :], con_("ltri", rows=64), ALU.mult))
            link(V.tensor_tensor(rank[0:64, :], rank[0:64, :], tie[0:64, :], ALU.add))
            link(V.tensor_reduce(sel[:, 1, 0:NSB], rk, AX, ALU.add))
            link(V.tensor_scalar(sel[:, 2, 0:NSB], sel[:, 1, 0:NSB], float(NSEL) - 0.5, NEG, ALU.is_gt, ALU.mult))
            s3 = sall[:, 0:NPG * P].rearrange("p (n k) -> p n k", k=64)
            link(V.tensor_tensor(s3, s3, sel[:, 2, 0:32].unsqueeze(2).broadcast_to([64, 32, 64]), ALU.add))
            link(V.tensor_reduce(ssx[:, 6:7], sall[:, :], AX, ALU.max))
            V.tensor_scalar(ssx[:, 7:8], ssx[:, 6:7], -SCALE, None, ALU.mult).then_inc(sx_in, 1)
            link(V.tensor_scalar(scm[:, 0:NCB], scm[:, 0:NCB], sg[:, 0:1], None, ALU.mult))
            dve.wait_ge(sx_out, 3)
            for r, (n, buf) in enumerate(((8, sall[:, :]), (5, swin[0:64, 0:T]))):
                link(V.reciprocal(ssx[:, 10 + r:11 + r], ssx[:, n:n + 1]))
                link(V.tensor_tensor(ssx[:, 12 + r:13 + r], ssx[:, 10 + r:11 + r], sg[:, 1 + r:2 + r], ALU.mult))
                last = V.tensor_scalar(buf, buf, ssx[:, 12 + r:13 + r], None, ALU.mult)
            last.then_inc(sp_ready, 1)
            dve.wait_ge(spT_done, 1)
            V.tensor_copy(ptS[:, 0:NPG, :].rearrange("p (a c) r -> p a (c r)", a=2), ps[:, 4:6, :])
            V.tensor_copy(ptS[:, NPG:NPG + ST, :].rearrange("p c r -> p (c r)"), ps[:, 6, 0:256])
            V.tensor_copy(ptS[0:NCB, 20, :], ps[0:NCB, 0, 0:64])
            V.tensor_copy(ptS[0:NB, 21, :], ps[0:NB, 1, 0:64])
            V.tensor_copy(ptS[0:NB, 22, :], ps[0:NB, 2, 0:64]).then_inc(spT_evac, 1)
            dve.wait_ge(spv_done, NB)
            for hh in range(NH):
                rows = hr[hh // G]
                last = V.tensor_copy(h[rows, hh % G, S:T], ps[rows, 7, 0:64].rearrange("p (b r) -> p b r", b=NB)[:, :, hh])
            last.then_inc(mix_ready, 1)

            def residual(n, m, gate, done):
                dve.wait_ge(slot_done, SLOT0[n + 1])
                link(V.tensor_tensor(t8[:, :], ps[:, 2 + n % 2, 0:NB], mod[:, gate + m, 1:9], ALU.mult))
                V.scalar_tensor_tensor(x[:, m, 0:S], ps[:, n % 2, :], mod[:, gate + m, 0:1], x[:, m, 0:S], ALU.mult, ALU.add)\
                    .then_inc(evac_dve, 1)
                V.tensor_tensor(x[:, m, S:T], x[:, m, S:T], t8[:, :], ALU.add).then_inc(x_ready, 1)
                dve.wait_ge(x_ready, done)

            for m in range(KD):
                residual(len(PART1) + m, m, 16, m + 1)
            root(1)
            normed(1, "g2", 32, 24)

            dve.wait_ge(ffst_landed, 16)
            dve.wait_ge(state_out, 16 * 8)
            link(V.tensor_copy(ffo_s[:, :, 0, :], ffst_t[:, :, 1, :]))
            for m in range(2 * FC):
                n = N_UP0 + m
                t = PART2[KD + m][1]
                w = [par_("conv_w", 3 * t + c, 3 * t + c + 1) for c in range(3)]
                y, y8 = yab[:, m % 2, :], yab[:, m % 2, S:T]
                bank, bank8 = ps[:, n % 2, :], ps[:, 2 + n % 2, 0:NB]
                dve.wait_ge(y_ready, m + 1)
                V.tensor_copy(ffo_p[:, t, :], bank[:, S - 2:S])
                V.tensor_copy(ffo_s[:, t, 1, :], bank8)
                link(V.tensor_scalar(y8, bank8, w[2], par_("conv_b", t, t + 1), ALU.mult, ALU.add))
                link(V.scalar_tensor_tensor(y8, ffst_t[:, t, 1, :], w[1], y8, ALU.mult, ALU.add))
                V.scalar_tensor_tensor(y8, ffst_t[:, t, 0, :], w[0], y8, ALU.mult, ALU.add)
                link(V.scalar_tensor_tensor(y[:, 1:S], bank[:, 0:S - 1], w[1], y[:, 1:S], ALU.mult, ALU.add))
                last = V.scalar_tensor_tensor(y[:, 2:S], bank[:, 0:S - 2], w[0], y[:, 2:S], ALU.mult, ALU.add)
                if m % 2 == 0:
                    last.then_inc(silu_in, 1)
                    dve.wait_ge(silu_in, m // 2 + 1)
                    V.tensor_copy(t8[:, 0:1], y[:, 0:1]).then_inc(evac_dve, 1)
                    dve.wait_ge(evac_dve, KD + m + 1)
                else:
                    link(last)
                    dve.wait_ge(silu_out, m // 2 + 1)
                    V.tensor_tensor(fT[:, m // 2, :], sil[:, :], y, ALU.mult).then_inc(evac_dve, 1)
                    dve.wait_ge(evac_dve, KD + m + 1)
            for m in range(KD):
                residual(N_DOWN0 + m, m, 40, KD + m + 1)
            root(2)
            for k in range(KD):
                link(V.tensor_tensor(x[:, k, :], x[:, k, :], rstd[:, :], ALU.mult))
                last = V.tensor_scalar(h[:, k, :], x[:, k, :], par_("gf", k, k + 1), None, ALU.mult)
            last.then_inc(out_ready, 1)


def _constants():
    c = np.zeros((P, NCON), np.float32)

    def put(name, a, rows=P):
        at, n = CON[name]
        c[:rows, at:at + n] = a.reshape(rows, n)

    put("ident", np.eye(P))
    put("ones", np.ones((P, P)))
    put("mean", np.full((P, P), 1.0 / D))
    i = np.arange(P)
    put("cq", np.where(i[None, :] <= i[:, None], 0.0, NEG))
    put("ct", np.where(i[None, :] >= i[:, None], 0.0, NEG))
    pos = (np.arange(ST)[None, :] * P + i[:, None])[:, :, None]
    seen = 16 * np.arange(NCP)[None, None, :] + 31 <= pos
    put("cadd", np.where(seen, 0.0, NEG))
    put("cmul", np.where(seen, 1.0, 0.0))
    win = np.array([[2, 8], [4, 16]], np.float32)[(i >= HD).astype(int)]
    put("rw", 1.0 / win)
    put("rcnt", 1.0 / np.minimum(win[:, :, None], np.arange(1, 17)[None, None, :]))
    put("hot", np.repeat(np.eye(4), P, axis=1), 4)
    r = np.arange(64)
    put("grp", (r[:, None] // 4 == r[None, :] // 4) * 1.0, 64)
    put("newm", np.where(r[:, None] // 8 == np.arange(NB)[None, :], 0.0, NEG), 64)
    n = np.arange(NSB)
    put("ltri", np.broadcast_to((n[None, :] < n[:, None]) * 1.0, (64, NSB, NSB)), 64)
    return c


def _chunks(w):
    return w.reshape(-1, P, w.shape[1]).transpose(1, 0, 2)


def _stream(w):
    ada, w_in, w_out, up, down = (np.asarray(w[n])[0] for n in ("ada_w", "w_in", "w_out", "ffn_w_up", "ffn_w_down"))
    q, kv, ng, mq, mk, mv_, mif, mo, pu = np.split(w_in, np.cumsum([512, 768, 24, 256, 256, 256, 8, 256]), axis=1)
    q = q.reshape(D, 2, G, HD).transpose(0, 2, 1, 3).reshape(D, 512)
    gates = np.zeros((D, P), np.float32)
    gates[:, 0:4], gates[:, 32:36], gates[:, 64:88] = mif[:, :4], mif[:, 4:], ng
    kc, vc, ks, vs, kw, vw = np.split(kv, 6, axis=1)
    cols = np.concatenate([q, kc, vc, ks, kw, mk, mq, mo, pu, gates, vs, vw, mv_], axis=1)
    rows = np.concatenate([w_out[:512].reshape(2, G, HD, D).transpose(1, 0, 2, 3).reshape(512, D), w_out[512:]])
    src = {"ada": _chunks(ada), "in": _chunks(cols), "out": _chunks(rows), "up": _chunks(up), "down": _chunks(down)}
    out = np.zeros((NSLOT, P, KD, P), np.float32)
    n = 0
    for kind, t, slots in PART1 + PART2:
        for s in range(slots):
            a = src[kind][:, s * KD:(s + 1) * KD, t * P:(t + 1) * P]
            out[n, :, :a.shape[1], :] = a
            n += 1
    return out.reshape(NSLOT, P, KD * P)


def _params(w):
    p = np.zeros((P, NPAR), np.float32)

    def put(name, a, rows=slice(0, P)):
        at, n = PAR[name]
        p[rows, at:at + n] = np.asarray(a).reshape(-1, n)

    col = lambda a: np.asarray(a).reshape(-1, P).T
    put("g1", col(w["norm1_g"][0]))
    put("g2", col(w["norm2_g"][0]))
    put("gf", col(w["final_g"]))
    put("ada_b", col(w["ada_b"][0]))
    put("conv_w", np.asarray(w["ffn_conv_w"])[0].reshape(3, 2 * FC, P).transpose(2, 1, 0))
    put("conv_b", col(w["ffn_conv_b"][0]))
    put("pool_s", col(w["pool_scale"][0]))
    wpos = np.asarray(w["nsa_cmp_pos"])[0].transpose(2, 0, 1)
    put("wpos", np.concatenate([wpos, wpos]))
    b = np.asarray(w["nsa_cmp_b"])[0]
    put("bk", np.concatenate([b[0], b[0]]))
    put("bv", np.concatenate([b[1], b[1]]), slice(0, 1))
    gb = np.asarray(w["mlstm_gate_b"])[0]
    put("gate_b", gb[:4], slice(0, 4))
    put("gate_b", gb[4:], slice(32, 36))
    put("igb", np.tile(np.repeat(gb[:4], NB), 4))
    put("fgb", np.tile(np.repeat(gb[4:], NB), 4))
    c = np.concatenate([np.asarray(w["c_prompt"]), np.asarray(w["c_sample"])])
    put("c", c.reshape(9, KD, P).transpose(2, 1, 0))
    cw = np.zeros((P, 2, P), np.float32)
    pw = np.zeros((P, 2, P), np.float32)
    for t in range(2):
        for g in range(2):
            r = slice(g * HD, (g + 1) * HD)
            cw[r, t, r] = np.asarray(w["nsa_cmp_w"])[0, t]
            pw[r, t, r] = np.asarray(w["pool_w"])[0, 2 * t + g]
    put("cw", cw)
    put("pw", pw)
    put("mn", np.tile(np.asarray(w["state_mlstm_n"])[0].transpose(1, 0, 2).reshape(32, HD), (4, 1)))
    put("mm", np.tile(np.asarray(w["state_mlstm_m"])[0].T.reshape(32, 1), (4, 1)))
    return p


def kernel(**w):
    import concourse.bacc as bacc
    from concourse.bass_utils import run_bass_kernel_spmd

    f = {n: np.asarray(a) for n, a in w.items()}
    tokens = np.concatenate([f["x_prompt"][0], f["x_sample"][:, 0]])
    ck = f["cache_k"][0].reshape(NPHYS, PAGE, 2, P)
    cv = f["cache_v"][0].reshape(NPHYS, PAGE, 2, P)
    fm = lambda a: a.transpose(0, 2, 1)
    ins = {
        "xT": tokens.T.reshape(KD, P, T).transpose(1, 0, 2),
        "weights": _stream(w),
        "params": _params(w),
        "constants": _constants(),
        "page_table": f["page_table"].reshape(1, NB * NPG),
        "cache_keys": np.concatenate([fm(ck[:, :, 0]), fm(ck[:, :, 1]), fm(cv[:, :, 0])], axis=2),
        "cache_values": cv[:, :, 1],
        "win_keys": f["cache_win_k"][0].reshape(NB, S, P).transpose(2, 0, 1),
        "win_values": f["cache_win_v"][0].reshape(NB, ST, P, P).transpose(2, 0, 1, 3),
        "mlstm_C": f["state_mlstm_C"][0].reshape(NB, 4, HD, 4, 16).transpose(3, 1, 0, 2, 4).reshape(P, HD * 16),
        "mlstm_m": f["state_mlstm_m"][0],
        "pool_state": f["state_pool"][0].reshape(NB, 15, 2, P).transpose(3, 2, 0, 1),
        "ffn_state": f["state_ffn_conv"][0].reshape(NB, 2, 2 * FC, P).transpose(3, 2, 1, 0),
    }
    outs = {
        "y": (P, KD, T), "kv_fm": (P, 4, S), "v_tm": (P, ST, 2 * P), "sample_proj": (P, N_IN, NB),
        "wk": (P, NB, S - 1), "wv": (P, NB, ST, P), "C": (HD, 4, HD + 1), "m": (4, 1), "pool": (P, 2, 15),
        "sC": (P, HD * 16), "sn": (32, HD), "sm": (32, 1), "spool": (P, 2, NB, 15), "ffp": (P, 2 * FC, 2),
        "ffs": (P, 2 * FC, 2, NB),
    }
    nc = bacc.Bacc("TRN2", target_bir_lowering=False, num_devices=1)
    arrays = {n: np.ascontiguousarray(a) for n, a in ins.items()}
    args = [nc.dram_tensor(n, a.shape, I32 if n == "page_table" else F32, kind="ExternalInput").ap() for n, a in arrays.items()]
    args += [nc.dram_tensor("out_" + n, s, F32, kind="ExternalOutput").ap() for n, s in outs.items()]
    trunk_kernel(nc, *args)
    res = run_bass_kernel_spmd(nc, [arrays], core_ids=[0]).results[0]
    o = {n: res["out_" + n] for n in outs}

    y = o["y"].transpose(2, 1, 0).reshape(T, D)
    heads = lambda a: a.reshape(a.shape[:-1] + (2, HD))
    kc, vc, ks, kw = (heads(o["kv_fm"][:, i].T) for i in range(4))
    vt = o["v_tm"].transpose(1, 0, 2).reshape(S, 2 * P)
    vs, vw = heads(vt[:, :P]), heads(vt[:, P:])
    s = lambda t: o["sample_proj"][:, t].T
    new = lambda a, b: np.stack([a, b], axis=1)
    swk = np.concatenate([o["wk"].transpose(1, 2, 0), s(T_KW)[:, None]], axis=1)
    wv = o["wv"].transpose(1, 2, 0, 3).reshape(NB, S, P)
    swv = np.concatenate([wv[:, 1:], s(T_VW)[:, None]], axis=1)
    C = o["C"].transpose(1, 0, 2)
    sC = o["sC"].reshape(4, 4, NB, HD, 16).transpose(2, 1, 3, 0, 4).reshape(NB, 4, HD, HD)
    return (
        y[:S][None], y[S:][:, None],
        new(kc, ks)[None, None], new(vc, vs)[None, None], kw[None, None], vw[None, None],
        np.ascontiguousarray(C[:, :, :HD])[None, None], np.ascontiguousarray(C[:, :, HD])[None, None], o["m"].reshape(1, 1, 4),
        o["pool"].transpose(2, 1, 0).reshape(1, 1, 15, 2 * P), o["ffp"].transpose(2, 1, 0).reshape(1, 1, 2, 2 * FF),
        new(heads(s(T_KC)), heads(s(T_KS)))[None, :, None], new(heads(s(T_VC)), heads(s(T_VS)))[None, :, None],
        heads(swk)[None], heads(swv)[None],
        sC[None], o["sn"].reshape(4, NB, HD).transpose(1, 0, 2)[None], o["sm"].reshape(4, NB).T[None],
        o["spool"].transpose(2, 3, 1, 0).reshape(1, NB, 15, 2 * P),
        o["ffs"].transpose(3, 2, 1, 0).reshape(1, NB, 2, 2 * FF),
    )
```

```python
from contextlib import ExitStack

import numpy as np
import concourse.bass as bass
from concourse import mybir

F32 = mybir.dt.float32
F32R = mybir.dt.float32r
I32 = mybir.dt.int32
ALU = mybir.AluOpType
ACT = mybir.ActivationFunctionType
AX = mybir.AxisListType.X

P = 128
D = 1024
KD = D // P
S = 512
NB = 8
T = S + NB
ST = S // P
HD = 64
G = 4
NH = 8
PAGE = 128
NPG = 16
NPHYS = 160
HALF = NPG // 2
NCB = 127
NCP = S // 16 - 1
NSB = 33
NSEL = 16
FF = 2816
FC = FF // P
SCALE = HD ** -0.5
NEG = -1e30
EPS = 1e-6

(T_Q, T_KC, T_VC, T_KS, T_KW, T_MK, T_MQ, T_MO, T_PU, T_G, T_VS, T_VW, T_MV) = (0, 4, 5, 6, 7, 8, 10, 12, 14, 16, 17, 18, 19)
N_IN = 21
N_FM = 17

TH = T // 2
RAW = 3
FH = FC // 2

def _layout(parts):
    at, out = 0, {}
    for name, n in parts:
        out[name] = (at, n)
        at += n
    return out, at

PAR, NPAR = _layout([("g1", 8), ("g2", 8), ("gf", 8), ("ada_b", 48), ("conv_w", 132), ("conv_b", 44), ("pool_s", 2),
                     ("wpos", 64), ("bk", 1), ("gate_b", 1), ("igb", 1), ("fgb", 1), ("c", 72),
                     ("cw", 256), ("bv", 128), ("pw", 256), ("mn", 64), ("mm", 1)])
CON, NCON = _layout([("ident", 128), ("ones", 128), ("mean", 128), ("cq", 128), ("ct", 128), ("cadd", 124), ("cmul", 124),
                     ("rw", 2), ("rcnt", 32), ("grp", 64), ("newm", 8)])
HOT = 4 * P


def plan():
    part1 = [("ada", t, KD) for t in range(16)]
    done = 16
    for t in range(N_IN):
        part1.append(("in", t, KD))
        while done < 16 + (32 * (t + 1)) // N_IN:
            part1.append(("ada", done, KD))
            done += 1
    part2 = [("out", m, KD) for m in range(KD)]
    for half in range(2):
        for j in range(half * FH, (half + 1) * FH):
            part2 += [("up", j, KD), ("up", FC + j, KD)]
        part2 += [(f"down{half}", m, FH) for m in range(KD)]
    return part1, part2


PART1, PART2 = plan()
ITEMS = PART1 + PART2
CHUNK0 = [sum(i[2] for i in ITEMS[:n]) for n in range(len(ITEMS) + 1)]
NSLOT = CHUNK0[-1] // KD
SPLIT = [g for g in range(NSLOT) if g >= len(PART1) or PART1[g][0] == "in"]
PART2_AT = {(kind, t): m for m, (kind, t, _) in enumerate(PART2)}


def events():
    out, pend = [], []
    for n, (kind, t, _) in enumerate(PART1):
        out.append(("lin", n))
        out += pend
        pend = [("turn", n)] if kind == "ada" else []
        if kind == "in" and 4 <= t < 4 + 2 * NB:
            b = (t - 4) // 2
            out.append(("slc", b, t % 2))
            if t % 2:
                out.append(("blocks", b))
                pend.append(("cmp", b))
        if n == 15:
            out += pend
            pend = []
    return out + pend


EVENTS = events()


def trunk_kernel(nc, xT, wst, par_d, con_d, hot_d, ltri_d, pt_d, cacheA, cacheV, winK, winV, mC, mst, plst, ffst,
                 o_y, o_fm, o_vn, o_st, o_snv, o_wk, o_wv, o_C, o_m, o_pool, o_sC, o_sn, o_sm, o_spool, o_ffp, o_ffs):
    with ExitStack() as ctx:
        def sb(name, shape, dt=F32):
            return ctx.enter_context(nc.sbuf_tensor(name, shape, dt))

        def sem(name):
            return ctx.enter_context(nc.semaphore(name))

        base = -(-nc.sbuf_base // 32) * 32
        arena = sb("arena", [P, 30210])

        def at(name, col, shape, dt=F32):
            return nc.alloc_sbuf_tensor_at(name, shape, dt, offset=base + 4 * col)

        mix = arena[:, 0:4160].rearrange("p (k n) -> p k n", k=KD)
        hR = at("hR", 4160, [P, 2, KD, T], F32R)
        fR = at("fR", 12480, [P, 2, FH, T], F32R)
        big = arena[:, 12480:27464]
        pT = big[:, 0:17 * T].rearrange("p (t n) -> p t n", t=17)
        pages = big[:, 17 * T:17 * T + 2 * HALF * 384].rearrange("p (s j n) -> p s j n", s=2, j=HALF)
        vpages = big[:, 17 * T:17 * T + 3 * NPG * P].rearrange("p (s j n) -> p s j n", s=3, j=NPG)
        kwin = big[:, 0:4096].rearrange("p (b n) -> p b n", b=NB)
        vwin = big[:, 4096:8192].rearrange("p (b c n) -> p b c n", b=NB, c=ST)
        x = sb("x", [P, KD, T])
        raw = sb("raw", [P, RAW, KD, P])
        wR = sb("wR", [P, 2, 2, KD, P], F32R)
        vn = sb("vn", [P, ST, 2 * P])
        vm = sb("vm", [P, ST, 4, HD + 1])
        par = sb("par", [P, NPAR])
        con = sb("con", [P, NCON])
        sT = sb("sT", [P, N_FM, NB])
        mod = sb("mod", [P, 48, 9])
        sc = sb("sc", [P, KD, 9])
        sc2 = sb("sc2", [P, KD, 9])
        ab = sb("ab", [P, KD, 9])
        sq = sb("sq", [P, 2, T])
        rstd = sb("rstd", [P, T])
        t8 = sb("t8", [P, NB])
        qs = sb("qs", [P, NB, NH])
        sall = sb("sall", [64, NPG * P + NB])
        scm = sb("scm", [64, P])
        vc = sb("vc", [P, NB, P])
        ptt = sb("ptt", [1, NB * NPG], I32)

        def lay(at, parts):
            out = []
            for n in parts:
                out.append(arena[:, at:at + n])
                at += n
            return out

        tmp, poolA, poolB, sst, modn = lay(0, [1024, 256, 256, 2176, 256])
        poolA = poolA.rearrange("p (k n) -> p k n", k=2)
        poolB = poolB.rearrange("p (k n) -> p k n", k=2)
        modn = modn.rearrange("p (a n) -> p a n", a=2)
        sn, gN, cout, smr, cst = lay(27464, [1152, 96, 260, 214, 1024])
        gN = gN.rearrange("p (i n) -> p i n", i=ST)
        cout = cout.rearrange("p (h n) -> p h n", h=4)
        KEEP = 4160
        ctmp, kN, wj, dt_, wk, hN, r36, mro, hot = lay(KEEP, [1024, 1024, 1280, 1024, 256, 1024, 512, 512, HOT])
        kN = kN.rearrange("p (t i n) -> p t i n", t=2, i=ST)
        dt_ = dt_.rearrange("p (a n) -> p a n", a=2)
        wk = wk.rearrange("p (j n) -> p j n", j=ST)
        hN = hN.rearrange("p (i n) -> p i n", i=ST)
        lfo, zro, bro = sq[:, 0, 0:S], sq[:, 1, 0:S], rstd[:, 0:S]
        pr, prT, pc, md, mds = lay(KEEP, [2048, 2048, 1024, 1024, 16])
        pr = pr.rearrange("p (a r n) -> p a r n", a=2, r=2)
        prT = prT.rearrange("p (a r n) -> p a r n", a=2, r=2)
        pc = pc.rearrange("p (u n) -> p u n", n=32)
        md = md.rearrange("p (t n) -> p t n", t=2)
        mds = mds.rearrange("p (t n) -> p t n", t=2)
        zp = lay(KEEP + 2048, [2 * (15 + S)])[0].rearrange("p (t n) -> p t n", t=2)
        swin, ptS, simp, rank, tie, sst2, sel = lay(KEEP, [520, (NPG + ST + 3) * 64, 136, 1089, 1089, 512, 4 * 34])
        sel = sel[0:64, :].rearrange("p (a n) -> p a n", a=4)
        ltri = lay(KEEP + 6160, [NSB * NSB])[0]
        ptS = ptS.rearrange("p (c r) -> p c r", r=64)
        yab, sil, ffst_t = lay(0, [2 * T, T, 704])
        ffo_s, ffo_p, zb = lay(23920, [704, 88, 2 * (T + 2)])
        yab = yab.rearrange("p (a n) -> p a n", a=2)
        zb = zb.rearrange("p (a n) -> p a n", a=2)
        ffst_t = ffst_t.rearrange("p (c j b) -> p c j b", c=2 * FC, j=2)
        ffo_s = ffo_s.rearrange("p (c j b) -> p c j b", c=2 * FC, j=2)
        ffo_p = ffo_p.rearrange("p (c j) -> p c j", j=2)

        kct = sb("kct", [P, P])
        pcT = sb("pcT", [P, 2, P])
        vcp = sb("vcp", [P, P])
        pooled = sb("pooled", [P, 2, P])
        rT = sb("rT", [P, ST, 36])
        enm = sb("enm", [P, ST, 4])
        d4 = sb("d4", [P, 8])
        mx = sb("mx", [P, 4, 32])
        sm = sb("sm", [P, 2, 2])
        nmx = sb("nmx", [P, 2, 2])
        fac = sb("fac", [P, 2, 2])
        zs = sb("zs", [P, 2, NB, 16])
        zsum = sb("zsum", [P, 2, NB])
        mout = sb("mout", [4, 2])
        mv = sb("mv", [P, 32])
        qc = sb("qc", [P, 16])
        shh = sb("shh", [P, 16])
        hs8 = sb("hs8", [NB, 4 * HD])
        emos = sb("emos", [P, 2, NB])
        sg = sb("sg", [64, 4])
        ssx = sb("ssx", [64, 16])

        ps = ctx.enter_context(nc.psum_tensor("ps", [P, 8, 512], F32))

        def con_(name, a=0, b=None, rows=P):
            at, n = CON[name]
            return con[0:rows, at + a:at + (n if b is None else b)]

        def par_(name, a=0, b=None, lo=0, hi=P):
            at, n = PAR[name]
            return par[lo:hi, at + a:at + (n if b is None else b)]

        ident = con_("ident")
        hr = [slice(0, HD), slice(HD, P)]

        x_landed, par_landed, con_landed = sem("x_landed"), sem("par_landed"), sem("con_landed")
        raw_landed = [sem(f"raw_landed{i}") for i in range(RAW)]
        hi_ready, lo_ready = sem("hi_ready"), sem("lo_ready")
        slot_done = sem("slot_done")
        item_done = sem("item_done")
        turn_done, turn_evac = sem("turn_done"), sem("turn_evac")
        h_hi, h_lo = sem("h_hi"), sem("h_lo")
        hot_landed, ltri_landed = sem("hot_landed"), sem("ltri_landed")
        f_ready, f_hi, f_lo = sem("f_ready"), sem("f_hi"), sem("f_lo")
        y_used, zero_done = sem("y_used"), sem("zero_done")
        table_landed = sem("table_landed")
        cache_landed = [sem(f"cache_landed{i}") for i in range(2)]
        vcache_landed = [sem(f"vcache_landed{i}") for i in range(3)]
        win_landed = sem("win_landed")
        rec_landed = sem("rec_landed")
        ffst_landed = sem("ffst_landed")
        memset_done = sem("memset_done")
        early_out, state_out, end_out = sem("early_out"), sem("state_out"), sem("end_out")
        sq_ready, sq_used, var_ready, root_ready = sem("sq_ready"), sem("sq_used"), sem("var_ready"), sem("root_ready")
        silu_exp, silu_ready = sem("silu_exp"), sem("silu_ready")
        xn_ready, h_prompt, h_sample = sem("xn_ready"), sem("h_prompt"), sem("h_sample")
        evac_act, evac_dve = sem("evac_act"), sem("evac_dve")
        qs_ready = sem("qs_ready")
        slc_scored, slc_evac = sem("slc_scored"), sem("slc_evac")
        comp_done, pooled_ready = sem("comp_done"), sem("pooled_ready")
        blocks_done, blocks_evac = sem("blocks_done"), sem("blocks_evac")
        cmp_scored, cmp_evac, sst_moved = sem("cmp_scored"), sem("cmp_evac"), sem("sst_moved")
        kn_T, sn_T, g_T, kn_evac, sn_evac, g_exp = (sem("kn_T"), sem("sn_T"), sem("g_T"), sem("kn_evac"),
                                                    sem("sn_evac"), sem("g_exp"))
        az_ready, ln_ready, rows_ready, r_T, rt_evac = (sem("az_ready"), sem("ln_ready"), sem("rows_ready"), sem("r_T"),
                                                        sem("rt_evac"))
        act_step = sem("act_step")
        bc_done, mscore_done, dmask_done, dt_done, w_done = (sem("bc_done"), sem("mscore_done"), sem("dmask_done"),
                                                             sem("dt_done"), sem("w_done"))
        num_done, num_evac, hT_done, emo_ready, mmix_ready = (sem("num_done"), sem("num_evac"), sem("hT_done"),
                                                              sem("emo_ready"), sem("mmix_ready"))
        rows_moved, saz_ready, sln_ready, sexp_in, sexp_ready, srec_ready = (
            sem("rows_moved"), sem("saz_ready"), sem("sln_ready"), sem("sexp_in"), sem("sexp_ready"), sem("srec_ready"))
        hs_moved, emos_ready, shT_done = sem("hs_moved"), sem("emos_ready"), sem("shT_done")
        gates_ready = sem("gates_ready")
        csc_done, pcx_ready, pcx_exp, pc_ready = sem("csc_done"), sem("pcx_ready"), sem("pcx_exp"), sem("pc_ready")
        qk_done, mx_ready, p_exp, p_ready, t_done = sem("qk_done"), sem("mx_ready"), sem("p_exp"), sem("p_ready"), sem("t_done")
        pt_act, pt_dve, pv_done, o_evac = sem("pt_act"), sem("pt_dve"), sem("pv_done"), sem("o_evac")
        pool_ready, pool_mm = sem("pool_ready"), sem("pool_mm")
        snew_done, wsc_done, wsc_evac, w_moved, sgate_moved, sg_exp = (sem("snew_done"), sem("wsc_done"), sem("wsc_evac"),
                                                                       sem("w_moved"), sem("sgate_moved"), sem("sg_exp"))
        sx_in, sx_out, imp_in, imp_done, sp_ready, spT_done, spT_evac = (
            sem("sx_in"), sem("sx_out"), sem("imp_in"), sem("imp_done"), sem("sp_ready"), sem("spT_done"), sem("spT_evac"))
        spv_done, mix_ready = sem("spv_done"), sem("mix_ready")
        y_ready, silu_in, silu_out, x_ready, out_ready = (sem("y_ready"), sem("silu_in"), sem("silu_out"), sem("x_ready"),
                                                          sem("out_ready"))
        dve_step = sem("dve_step")

        def item_ready(eng, n):
            c = CHUNK0[n + 1]
            if c % KD == 0:
                eng.wait_ge(slot_done, c // KD)
            else:
                eng.wait_ge(item_done, sum(CHUNK0[i + 1] % KD != 0 for i in range(n + 1)))

        NE = len([e for e in EVENTS if e[0] == "slc"])
        UNITS = [(hh, i) for hh in range(NH) for i in range(ST)]
        OFF = [0, 512, 896, 1152]

        block = ctx.enter_context(nc.Block())

        @block.sync
        def _(sp):
            def load_slot(g):
                old = g - RAW
                if old >= 0 and old in SPLIT:
                    sp.wait_ge(lo_ready, SPLIT.index(old) + 1)
                elif old >= 0:
                    sp.wait_ge(slot_done, old + 1)
                sp.dma_start(raw[:, g % RAW, :, :], wst[g, :, :].rearrange("p (k n) -> p k n", k=KD))\
                  .then_inc(raw_landed[g % RAW], 16)

            page_regs = [sp.alloc_register(f"page{j}") for j in range(HALF)]

            def page_numbers(i):
                sp.load(page_regs, ptt[0:1, i * HALF:(i + 1) * HALF])
                return [sp.snap(reg, min_val=0, max_val=NPHYS - 1) for reg in page_regs]

            def load_half(i):
                b, s = i // 2, i % 2
                if i >= 2:
                    sp.wait_ge(comp_done, i - 1)
                    sp.wait_ge(slc_scored, i - 1)
                for j, pg in enumerate(page_numbers(i)):
                    sp.dma_start(pages[:, s, j, :], cacheA[bass.ds(pg, 1), :, :].rearrange("a p n -> (a p) n"))\
                      .then_inc(cache_landed[s], 16)

            for k in range(KD):
                sp.dma_start(x[:, k, :], xT[:, k, :]).then_inc(x_landed, 16)
                if k == 1:
                    sp.dma_start(par[:, :], par_d).then_inc(par_landed, 16)
                    sp.dma_start(con[:, :], con_d).then_inc(con_landed, 16)
            sp.wait_ge(table_landed, 16)
            half = 0
            for g in range(len(PART1)):
                load_slot(g)
                if g in (8, 15) or (half >= 2 and half < 2 * NB and g - 4 >= 0 and g - 4 in SPLIT
                                    and SPLIT.index(g - 4) >= half + 2):
                    load_half(half)
                    half += 1
            while half < 2 * NB:
                load_half(half)
                half += 1
            for g in range(len(PART1), len(PART1) + RAW):
                load_slot(g)

            sp.wait_ge(evac_act, len(PART1))
            sp.dma_start(hot[0:4, :], hot_d).then_inc(hot_landed, 16)
            sp.wait_ge(sn_evac, 1)
            sp.dma_start(cst[:, :], mC).then_inc(rec_landed, 16)
            sp.dma_start(zs[:, :, :, 0:15], plst).then_inc(rec_landed, 16)
            for e in range(4):
                for hh in range(4):
                    r = slice(e * 32 + hh * 8, e * 32 + hh * 8 + 8)
                    sp.dma_start(smr[r, 0:128].rearrange("p (t d) -> p t d", t=2),
                                 sn[0:8, 0:512].rearrange("p (t h d) -> p t h d", t=2, h=4)[:, :, hh, :]).then_inc(rows_moved, 16)
                    sp.dma_start(smr[r, 128:144], sn[0:8, 512 + hh * 64 + e * 16:512 + hh * 64 + e * 16 + 16])\
                      .then_inc(rows_moved, 16)
                    sp.dma_start(smr[r, 144:146], sn[0:8, 768 + hh:768 + hh + 33:32], allow_slow_non_contiguous=True)\
                      .then_inc(rows_moved, 16)
            for b in range(NB):
                sp.dma_start(sg[b * 8:b * 8 + 8, 0:3], sn[b:b + 1, 768 + 64:768 + 88].rearrange("p (h r) -> p h r", h=8))\
                  .then_inc(sgate_moved, 16)
            sp.dma_start(o_fm, pT[:, T_KC:T_MK, 0:S]).then_inc(early_out, 16)
            sp.dma_start(o_vn, vn[:, :, :]).then_inc(early_out, 16)
            sp.dma_start(o_st, sT[:, :, :]).then_inc(early_out, 16)
            sp.dma_start(o_snv, sn[0:NB, 7 * P:9 * P]).then_inc(early_out, 16)
            sp.dma_start(o_pool, pT[:, T_PU:T_PU + 2, S - 15:S]).then_inc(early_out, 16)

            sp.wait_ge(comp_done, 2 * NB)
            sp.wait_ge(slc_scored, 2 * NB)

            def load_values(b):
                for half in range(2):
                    for j, pg in enumerate(page_numbers(2 * b + half)):
                        sp.dma_start(vpages[:, b % 3, half * HALF + j, :],
                                     cacheV[bass.ds(pg, 1), :, :].rearrange("a p n -> (a p) n")).then_inc(vcache_landed[b % 3], 16)

            for b in range(3):
                load_values(b)
            sp.wait_ge(mmix_ready, 1)
            sp.dma_start(o_C, cout[0:HD, :, :]).then_inc(state_out, 16)
            sp.dma_start(o_m, mout[0:4, 0:1]).then_inc(state_out, 16)
            sp.dma_start(ltri[0:64, :], ltri_d).then_inc(ltri_landed, 16)
            sp.wait_ge(srec_ready, 1)
            for e in range(4):
                for hh in range(4):
                    sp.dma_start(hs8[0:8, hh * 64 + e * 16:hh * 64 + e * 16 + 16], shh[e * 32 + hh * 8:e * 32 + hh * 8 + 8, :])\
                      .then_inc(hs_moved, 16)
            sp.dma_start(o_sC, cst[:, :]).then_inc(state_out, 16)
            sp.dma_start(o_sn, smr[0:32, 146:210]).then_inc(state_out, 16)
            sp.dma_start(o_sm, mv[0:32, 3:4]).then_inc(state_out, 16)
            sp.wait_ge(pool_ready, 1)
            sp.dma_start(o_spool, zs[:, :, :, 1:16]).then_inc(state_out, 16)
            sp.wait_ge(early_out, 16 * 5)
            sp.wait_ge(qk_done, len(UNITS))
            sp.dma_start(kwin, winK).then_inc(win_landed, 16)
            sp.dma_start(vwin, winV).then_inc(win_landed, 16)
            sp.wait_ge(win_landed, 32)
            sp.dma_start(o_wk, kwin[:, :, 1:512]).then_inc(state_out, 16)
            sp.dma_start(o_wv, vwin).then_inc(state_out, 16)
            for b in range(3, NB):
                sp.wait_ge(spv_done, b - 2)
                load_values(b)
            g0 = len(PART1) + RAW
            for g in range(g0, g0 + 6):
                load_slot(g)
            sp.wait_ge(h_hi, 2 * KD)
            sp.wait_ge(h_lo, 2 * KD)
            sp.dma_start(ffst_t, ffst).then_inc(ffst_landed, 16)
            g0 += 6
            rounds = (NSLOT - g0) // RAW
            with sp.Fori(0, rounds) as q:
                for s in range(RAW):
                    sp.wait_ge(lo_ready, q * RAW + (SPLIT.index(g0 + s - RAW) + 1))
                    sp.dma_start(raw[:, (g0 + s) % RAW, :, :],
                                 wst[bass.ds(q * RAW + (g0 + s), 1), :, :].rearrange("a p (k n) -> (a p) k n", k=KD))\
                      .then_inc(raw_landed[(g0 + s) % RAW], 16)
            for g in range(g0 + rounds * RAW, NSLOT):
                load_slot(g)
            sp.wait_ge(f_lo, FC)
            sp.dma_start(o_ffp, ffo_p).then_inc(end_out, 16)
            sp.dma_start(o_ffs, ffo_s).then_inc(end_out, 16)
            for k in range(KD):
                sp.wait_ge(out_ready, k + 1)
                sp.dma_start(o_y[:, k, :], x[:, k, :]).then_inc(end_out, 16)
            sp.wait_ge(early_out, 16 * 5)
            sp.wait_ge(state_out, 16 * 8)
            sp.wait_ge(end_out, 16 * 10)

        @block.gpsimd
        def _(pool):
            pool.dma_start(ptt[:, :], pt_d).then_inc(table_landed, 16)
            nc.gpsimd.memset(qs[:, :, :], 0.0).then_inc(memset_done, 1)
            nc.gpsimd.memset(vm[:, :, :, HD:HD + 1], 1.0).then_inc(memset_done, 1)
            for i, g in enumerate(SPLIT):
                pool.wait_ge(hi_ready, i + 1)
                nc.gpsimd.tensor_tensor(wR[:, i % 2, 1, :, :], raw[:, g % RAW, :, :], wR[:, i % 2, 0, :, :].bitcast(F32),
                                        ALU.subtract).then_inc(lo_ready, 1)

        @block.tensor
        def _(pe):
            mm = nc.tensor.matmul

            def norm_sum(n, k):
                pe.wait_ge(sq_ready, n * KD + k + 1)
                mm(ps[:, 4, 0:TH], con_("mean"), sq[:, k % 2, 0:TH], start=(k == 0), stop=(k == KD - 1))
                mm(ps[:, 5, 0:TH], con_("mean"), sq[:, k % 2, TH:T], start=(k == 0), stop=(k == KD - 1)).then_inc(sq_used, 1)

            PASSES = [(0, 0), (0, 1), (1, 0)]

            def product(n):
                kind, t, chunks = ITEMS[n]
                a = 2 * (n % 2)
                if kind == "ada":
                    pe.wait_ge(raw_landed[n % RAW], 16 * (n // RAW + 1))
                    for k in range(KD):
                        last = mm(ps[0:9, a, 0:P], sc[:, k, :], raw[:, n % RAW, k, :], start=(k == 0), stop=(k == KD - 1))
                    last.then_inc(slot_done, 1)
                    return
                if kind == "in" and t >= N_FM:
                    i = SPLIT.index(n)
                    pe.wait_ge(lo_ready, i + 1)
                    for c in range(ST + 1):
                        cols = slice(c * P, (c + 1) * P) if c < ST else slice(S, T)
                        out = ps[:, a, cols] if c < ST else ps[0:NB, a + 1, 0:P]
                        for k in range(KD):
                            for q, (wp, hp) in enumerate(PASSES):
                                last = mm(out, hR[:, hp, k, cols], wR[:, i % 2, wp, k, :], start=(k == 0 and q == 0),
                                          stop=(k == KD - 1 and q == 2))
                    last.then_inc(slot_done, 1)
                    return
                for j in range(chunks):
                    g, k = (CHUNK0[n] + j) // KD, (CHUNK0[n] + j) % KD
                    i = SPLIT.index(g)
                    if j == 0 or k == 0:
                        pe.wait_ge(lo_ready, i + 1)
                    if (kind, t) in (("in", 0), ("out", 0), ("up", 0)):
                        v = ("in", "out", "up").index(kind)
                        pe.wait_ge(h_hi, v * KD + j + 1)
                        pe.wait_ge(h_lo, v * KD + j + 1)
                    if kind in ("down0", "down1") and t == 0:
                        pe.wait_ge(f_lo, FH * (kind == "down1") + j + 1)
                    src = fR if kind[:4] == "down" else hR
                    for q, (wp, hp) in enumerate(PASSES):
                        for half in range(2):
                            last = mm(ps[:, a + half, 0:TH], wR[:, i % 2, wp, k, :], src[:, hp, j, half * TH:(half + 1) * TH],
                                      start=(j == 0 and q == 0), stop=(j == chunks - 1 and q == 2))
                    if k == KD - 1:
                        last.then_inc(slot_done, 1)
                    elif j == chunks - 1:
                        last.then_inc(item_done, 1)

            pe.wait_ge(con_landed, 16)
            pe.wait_ge(par_landed, 16)
            for k in range(KD):
                norm_sum(0, k)
            pe.wait_ge(silu_ready, 1)
            e = turns = 0
            for ev in EVENTS:
                if ev[0] == "lin":
                    n = ev[1]
                    if n >= 2:
                        pe.wait_ge(evac_act, n - 1)
                        if PART1[n - 2][0] == "ada":
                            pe.wait_ge(turn_evac, sum(i[0] == "ada" for i in PART1[:n - 1]))
                    product(n)
                elif ev[0] == "turn":
                    n = ev[1]
                    pe.wait_ge(evac_act, n + 1)
                    nc.tensor.transpose(ps[:, 2 * (n % 2) + 1, 0:9], modn[0:9, turns % 2, :], ident[0:9, 0:9]).then_inc(turn_done, 1)
                    turns += 1
                elif ev[0] == "slc":
                    _, b, s = ev
                    pe.wait_ge(cache_landed[s], 16 * HALF * (b + 1))
                    pe.wait_ge(qs_ready, 1)
                    if e:
                        pe.wait_ge(slc_evac, e)
                    e += 1
                    for j in range(2):
                        last = mm(ps[0:NH, 6 + j, :].rearrange("p (j n) -> p j n", j=4), qs[:, b, :],
                                  pages[:, s, 4 * j:4 * j + 4, P:2 * P], start=True, stop=True)
                    last.then_inc(slc_scored, 1)
                elif ev[0] == "blocks":
                    b = ev[1]
                    pe.wait_ge(pooled_ready, b + 1)
                    if b:
                        pe.wait_ge(blocks_evac, b)
                        pe.wait_ge(cmp_evac, b)
                    mm(ps[:, 4, 0:NCB], par_("cw", 0, P), pooled[:, 0, 0:NCB], start=True, stop=True)
                    mm(ps[0:NCB, 5, 0:P], pooled[:, 1, 0:NCB], par_("cw", P, 2 * P), start=True, stop=False)
                    mm(ps[0:NCB, 5, 0:P], con_("ones", 0, NCB, 1), par_("bv", hi=1), start=False, stop=True)\
                        .then_inc(blocks_done, 1)
                else:
                    b = ev[1]
                    pe.wait_ge(blocks_evac, b + 1)
                    mm(ps[0:NH, 4, 0:NCB], qs[:, b, :], kct[:, 0:NCB], start=True, stop=True).then_inc(cmp_scored, 1)

            pe.wait_ge(evac_act, len(PART1))
            pe.wait_ge(turn_evac, 48)
            pe.wait_ge(blocks_evac, NB)
            pe.wait_ge(cmp_evac, NB)
            pe.wait_ge(slc_evac, NE)
            for t in range(2):
                for i in range(ST):
                    last = nc.tensor.transpose(ps[:, 4 + t, i * P:(i + 1) * P], pT[:, T_MK + t, i * P:(i + 1) * P], ident)
            last.then_inc(kn_T, 1)
            for c, t in enumerate([T_MQ, T_MQ + 1, T_MK, T_MK + 1, T_G]):
                last = nc.tensor.transpose(ps[0:NB, c // 4, (c % 4) * P:(c % 4 + 1) * P], sT[:, t, :], ident)
            last.then_inc(sn_T, 1)
            for i in range(ST):
                last = nc.tensor.transpose(ps[:, 3, i * P:(i + 1) * P], pT[:, T_G, i * P:(i + 1) * P], ident)
            last.then_inc(g_T, 1)
            pe.wait_ge(pooled_ready, NB + 1)
            mm(ps[:, 6, 0:NCP], par_("cw", 0, P), pooled[:, 0, 0:NCP], start=True, stop=True)
            mm(ps[0:NCP, 7, 0:P], pooled[:, 1, 0:NCP], par_("cw", P, 2 * P), start=True, stop=False)
            mm(ps[0:NCP, 7, 0:P], con_("ones", 0, NCP, 1), par_("bv", hi=1), start=False, stop=True).then_inc(blocks_done, 1)
            pe.wait_ge(rows_ready, 1)
            pe.wait_ge(sn_evac, 1)
            for i in range(ST):
                last = nc.tensor.transpose(ps[:, 0, i * 36:(i + 1) * 36], r36[0:36, i * P:(i + 1) * P], ident[0:36, 0:36])
            last.then_inc(r_T, 1)

            pe.wait_ge(kn_evac, 1)
            pe.wait_ge(g_exp, 1)
            pe.wait_ge(blocks_evac, NB + 1)
            pe.wait_ge(hot_landed, 16)
            for hh in range(4):
                rows, t = hr[hh % 2], hh // 2
                if hh:
                    pe.wait_ge(w_done, 4 * hh)
                mm(ps[:, 7, :], hot[0:4, hh * P:(hh + 1) * P], mro[0:4, :], start=True, stop=True).then_inc(bc_done, 1)
                for j in range(ST):
                    q = 4 * hh + j
                    if q >= 2:
                        pe.wait_ge(w_done, q - 1)
                    mm(ps[:, 4 + q % 2, 0:S - j * P], pT[rows, T_MK + t, j * P:(j + 1) * P], pT[rows, T_MQ + t, j * P:S],
                       start=True, stop=True).then_inc(mscore_done, 1)
                pe.wait_ge(w_done, 4 * hh + 4)
                if hh:
                    pe.wait_ge(num_evac, hh)
                for i in range(ST):
                    for j in range(i + 1):
                        at = OFF[j] + (i - j) * P
                        mm(ps[:, 6, i * 65:i * 65 + 65], wj[:, at:at + P], vm[:, j, hh, :], start=(j == 0), stop=(j == i))
                for j in range(ST):
                    last = mm(ps[0:HD, 3, hh * 65:hh * 65 + 65], wk[:, j, :], vm[:, j, hh, :], start=(j == 0), stop=(j == ST - 1))
                last.then_inc(num_done, 1)
            pe.wait_ge(num_evac, 4)
            for t in range(2):
                for i in range(ST):
                    last = nc.tensor.transpose(ps[:, 1 + t, i * P:(i + 1) * P], hN[:, i, t * P:(t + 1) * P], ident)
            last.then_inc(hT_done, 1)

            pe.wait_ge(mmix_ready, 1)
            pe.wait_ge(rt_evac, 1)
            for u, (hh, i) in enumerate(UNITS):
                rows = hr[hh // G]
                last = mm(ps[:, u // 16, (u % 16) * 32:(u % 16) * 32 + NCP], pT[rows, hh % G, i * P:(i + 1) * P], kct[rows, 0:NCP],
                          start=True, stop=True)
            last.then_inc(csc_done, 1)

            def scores(u):
                hh, i = UNITS[u]
                rows, n = hr[hh // G], (i + 1) * P
                if u >= 2:
                    pe.wait_ge(p_exp, u - 1)
                elif u == 0:
                    pe.wait_ge(pcx_ready, 1)
                for r, t in enumerate((T_KS, T_KW)):
                    last = mm(ps[:, 2 * (u % 2) + r, 0:n], pT[rows, hh % G, i * P:(i + 1) * P], pT[rows, t, 0:n],
                              start=True, stop=True)
                last.then_inc(qk_done, 1)

            def flip(u):
                hh, i = UNITS[u]
                pe.wait_ge(p_ready, u + 1)
                if u == 0:
                    pe.wait_ge(pc_ready, 1)
                else:
                    pe.wait_ge(pt_act, u)
                    pe.wait_ge(pt_dve, u)
                for r in range(2):
                    for c in range(i + 1):
                        nc.tensor.transpose(ps[:, 4 + r, c * P:(c + 1) * P], pr[:, u % 2, r, c * P:(c + 1) * P], ident)
                nc.tensor.transpose(ps[0:NCP, 6, 0:P], pc[:, u, 0:NCP], ident).then_inc(t_done, 1)

            def values(u):
                hh, i = UNITS[u]
                rows = hr[hh // G]
                pe.wait_ge(pt_act, u + 1)
                pe.wait_ge(pt_dve, u + 1)
                if u:
                    pe.wait_ge(o_evac, u)
                out = ps[rows, 7, 0:P]
                for r in range(2):
                    for c in range(i + 1):
                        mm(out, vn[:, c, r * P + rows.start:r * P + rows.stop], prT[:, u % 2, r, c * P:(c + 1) * P],
                           start=(r == 0 and c == 0), stop=False)
                mm(out, vcp[0:NCP, rows], pcT[0:NCP, u % 2, :], start=False, stop=True).then_inc(pv_done, 1)

            NU = len(UNITS)
            for u in range(NU + 2):
                if u < NU:
                    scores(u)
                if 1 <= u <= NU:
                    flip(u - 1)
                if u >= 2:
                    values(u - 2)

            pe.wait_ge(o_evac, NU)
            mm(ps[0:64, 0, 0:NB], qs[:, :, :], sT[:, T_KS, :], start=True, stop=True)
            mm(ps[0:64, 0, NB:2 * NB], qs[:, :, :], sT[:, T_KW, :], start=True, stop=True).then_inc(snew_done, 1)
            pe.wait_ge(pool_ready, 1)
            for t in range(2):
                mm(ps[:, 4 + t, :], par_("pw", t * P, (t + 1) * P), md[:, t, :], start=True, stop=True)
                last = mm(ps[:, 6, t * NB:(t + 1) * NB], par_("pw", t * P, (t + 1) * P), mds[:, t, :], start=True, stop=True)
            last.then_inc(pool_mm, 1)
            pe.wait_ge(hs_moved, 16 * 16)
            for t in range(2):
                last = nc.tensor.transpose(ps[:, 7, t * NB:(t + 1) * NB], hs8[0:NB, t * P:(t + 1) * P], ident[0:NB, 0:NB])
            last.then_inc(shT_done, 1)
            pe.wait_ge(win_landed, 32)
            for b in range(NB):
                if b >= 2:
                    pe.wait_ge(wsc_evac, b - 1)
                mm(ps[0:NH, 1 + b % 2, :], qs[:, b, :], kwin[:, b, :], start=True, stop=True).then_inc(wsc_done, 1)
            pe.wait_ge(imp_in, 1)
            mm(ps[0:64, 3, 0:NCB], con_("grp", rows=64), scm[:, 0:NCB], start=True, stop=True).then_inc(imp_done, 1)
            pe.wait_ge(sp_ready, 1)
            for c in range(NPG):
                nc.tensor.transpose(ps[:, 4 + c // 8, (c % 8) * 64:(c % 8 + 1) * 64], sall[:, c * P:(c + 1) * P], ident[0:64, 0:64])
            for c in range(ST):
                nc.tensor.transpose(ps[:, 6, c * 64:(c + 1) * 64], swin[0:64, c * P:(c + 1) * P], ident[0:64, 0:64])
            nc.tensor.transpose(ps[0:NCB, 0, 0:64], scm[:, 0:NCB], ident[0:64, 0:64])
            nc.tensor.transpose(ps[0:NB, 1, 0:64], sall[:, NPG * P:NPG * P + NB], ident[0:64, 0:64])
            nc.tensor.transpose(ps[0:NB, 2, 0:64], swin[0:64, S:S + NB], ident[0:64, 0:64]).then_inc(spT_done, 1)
            pe.wait_ge(spT_evac, 1)
            for b in range(NB):
                pe.wait_ge(vcache_landed[b % 3], 16 * NPG * (b // 3 + 1))
                out, cols = ps[:, 7, b * 8:(b + 1) * 8], slice(b * 8, (b + 1) * 8)
                for c in range(NPG):
                    mm(out, vpages[:, b % 3, c, :], ptS[:, c, cols], start=(c == 0), stop=False)
                for c in range(ST):
                    mm(out, vwin[:, b, c, :], ptS[:, NPG + c, cols], start=False, stop=False)
                mm(out, vc[0:NCB, b, :], ptS[0:NCB, 20, cols], start=False, stop=False)
                mm(out, sn[0:NB, 7 * P:8 * P], ptS[0:NB, 21, cols], start=False, stop=False)
                mm(out, sn[0:NB, 8 * P:9 * P], ptS[0:NB, 22, cols], start=False, stop=True).then_inc(spv_done, 1)

            pe.wait_ge(mix_ready, 1)
            for m, (kind, t, _) in enumerate(PART2):
                if m >= 2:
                    pe.wait_ge(evac_dve, m - 1)
                product(len(PART1) + m)
                if kind == "out" and t >= 2:
                    norm_sum(1, t - 2)
                if kind == "out" and t == KD - 1:
                    norm_sum(1, KD - 2)
                    norm_sum(1, KD - 1)
                if kind == "down1" and t >= 2:
                    norm_sum(2, t - 2)
            norm_sum(2, KD - 2)
            norm_sum(2, KD - 1)

        @block.scalar
        def _(act):
            A = nc.scalar.activation
            chain = [0]

            def link(ins):
                chain[0] += 1
                ins.then_inc(act_step, 1)
                act.wait_ge(act_step, chain[0])

            def squares(n, k):
                if n * KD + k >= 2:
                    act.wait_ge(sq_used, n * KD + k - 1)
                A(sq[:, k % 2, :], x[:, k, :], ACT.Square).then_inc(sq_ready, 1)

            def hi(i):
                g = SPLIT[i]
                act.wait_ge(raw_landed[g % RAW], 16 * (g // RAW + 1))
                if i >= 2:
                    act.wait_ge(slot_done, SPLIT[i - 2] + 1)
                A(wR[:, i % 2, 0, :, :], raw[:, g % RAW, :, :], ACT.Identity).then_inc(hi_ready, 1)

            def normed(n, shift):
                for k in range(KD):
                    act.wait_ge(xn_ready, n * KD + k + 1)
                    A(sq[:, k % 2, 0:S], sq[:, k % 2, 0:S], ACT.Identity, bias=mod[:, shift + k, 0:1], scale=ab[:, k, 0:1])\
                        .then_inc(h_prompt, 1)
                    act.wait_ge(h_prompt, n * KD + k + 1)
                    act.wait_ge(h_sample, n * KD + k + 1)
                    A(hR[:, 0, k, :], sq[:, k % 2, :], ACT.Identity).then_inc(h_hi, 1)

            act.wait_ge(par_landed, 16)
            A(sc2[:, :, :], par_("c").rearrange("p (k n) -> p k n", k=KD), ACT.Exp, scale=-1.0).then_inc(silu_exp, 1)
            for k in range(KD):
                act.wait_ge(x_landed, 16 * KD)
                squares(0, k)
            act.wait_ge(var_ready, 1)
            A(rstd[:, :], rstd[:, :], ACT.Sqrt).then_inc(root_ready, 1)
            e = adas = turns = 0
            for ev in EVENTS:
                if ev[0] == "turn":
                    act.wait_ge(turn_done, turns + 1)
                    t = PART1[ev[1]][1]
                    A(mod[:, t, :], ps[:, 2 * (ev[1] % 2) + 1, 0:9], ACT.Identity, bias=par_("ada_b", t, t + 1)).then_inc(turn_evac, 1)
                    turns += 1
                    if t == 15:
                        hi(0)
                        act.wait_ge(turn_evac, 16)
                        normed(0, 0)
                    continue
                if ev[0] == "lin":
                    n = ev[1]
                    kind, t, _ = PART1[n]
                    if kind == "in" and n < SPLIT[-1] and SPLIT.index(n) + 1 < N_IN:
                        hi(SPLIT.index(n) + 1)
                    item_ready(act, n)
                    if kind == "ada":
                        if adas >= 2:
                            act.wait_ge(turn_done, adas - 1)
                        A(modn[0:9, adas % 2, :], ps[0:9, 2 * (n % 2), 0:P], ACT.Identity).then_inc(evac_act, 1)
                        adas += 1
                        continue
                    scale = SCALE if T_MK <= t < T_MK + 2 else 1.0
                    two = ps[:, 2 * (n % 2):2 * (n % 2) + 2, 0:TH]
                    one = ps[:, 2 * (n % 2), :]
                    if t < N_FM:
                        A(sT[:, t, :], two[:, 1, TH - NB:TH], ACT.Identity, scale=scale)
                        A(pT[:, t, :].rearrange("p (a n) -> p a n", a=2), two, ACT.Identity, scale=scale).then_inc(evac_act, 1)
                    else:
                        c = {T_VS: 7, T_VW: 8, T_MV: 4, T_MV + 1: 5}[t]
                        A(sn[0:NB, c * P:(c + 1) * P], ps[0:NB, 2 * (n % 2) + 1, 0:P], ACT.Identity)
                    if N_FM <= t < T_MV:
                        A(vn[:, :, (t - T_VS) * P:(t - T_VS + 1) * P], one.rearrange("p (i n) -> p i n", i=ST),
                          ACT.Identity).then_inc(evac_act, 1)
                    elif t >= T_MV:
                        if t == T_MV:
                            act.wait_ge(memset_done, 2)
                        v = one.rearrange("p (i a d) -> p i a d", i=ST, a=2)
                        A(vm[:, :, 2 * (t - T_MV):2 * (t - T_MV) + 2, 0:HD], v, ACT.Identity).then_inc(evac_act, 1)
                    if t == 3:
                        act.wait_ge(evac_act, n + 1)
                        act.wait_ge(memset_done, 2)
                        for hh in range(NH):
                            rows = hr[hh // G]
                            last = A(qs[rows, :, hh], sT[rows, hh % G, :], ACT.Identity)
                        last.then_inc(qs_ready, 1)
                elif ev[0] == "slc":
                    _, b, s = ev
                    e += 1
                    act.wait_ge(slc_scored, e)
                    if b and s == 0:
                        act.wait_ge(sst_moved, 32 * b)
                    for j in range(2):
                        at = (2 * s + j) * 512
                        last = A(sst[0:NH, at:at + 512], ps[0:NH, 6 + j, :], ACT.Identity)
                    last.then_inc(slc_evac, 1)
                elif ev[0] == "blocks":
                    act.wait_ge(blocks_done, ev[1] + 1)
                    A(kct[:, 0:NCB], ps[:, 4, 0:NCB], ACT.Identity, bias=par_("bk"))
                    A(vc[0:NCB, ev[1], :], ps[0:NCB, 5, 0:P], ACT.Identity).then_inc(blocks_evac, 1)
                else:
                    b = ev[1]
                    act.wait_ge(cmp_scored, b + 1)
                    A(sst[0:NH, 2048:2048 + NCB], ps[0:NH, 4, 0:NCB], ACT.Identity).then_inc(cmp_evac, 1)
                    act.wait_ge(cmp_evac, b + 1)
                    act.wait_ge(slc_evac, 2 * b + 2)
                    act.dma_start(sall[8 * b:8 * b + 8, 0:2048], sst[0:NH, 0:2048]).then_inc(sst_moved, 16)
                    act.dma_start(scm[8 * b:8 * b + 8, 0:NCB], sst[0:NH, 2048:2048 + NCB]).then_inc(sst_moved, 16)

            act.wait_ge(kn_T, 1)
            act.wait_ge(sst_moved, 32 * NB)
            act.wait_ge(pooled_ready, NB + 1)
            for t in range(2):
                last = A(kN[:, t, :, :], ps[:, 4 + t, :].rearrange("p (i n) -> p i n", i=ST), ACT.Identity)
            last.then_inc(kn_evac, 1)
            act.wait_ge(sn_T, 1)
            A(sn[0:NB, 0:512], ps[0:NB, 0, :], ACT.Identity)
            last = A(sn[0:NB, 6 * P:7 * P], ps[0:NB, 1, 0:P], ACT.Identity)
            last.then_inc(sn_evac, 1)
            act.wait_ge(g_T, 1)
            A(gN[:, :, :], ps[:, 3, :].rearrange("p (i n) -> p i n", i=ST)[:, :, 64:88], ACT.Exp, scale=-1.0).then_inc(g_exp, 1)
            act.wait_ge(blocks_done, NB + 1)
            A(kct[:, 0:NCP], ps[:, 6, 0:NCP], ACT.Identity, bias=par_("bk"))
            A(vcp[0:NCP, :], ps[0:NCP, 7, 0:P], ACT.Identity).then_inc(blocks_evac, 1)
            act.wait_ge(az_ready, 1)
            link(A(lfo[0:4, :], lfo[0:4, :], ACT.Exp, scale=-1.0))
            A(lfo[0:4, :], lfo[0:4, :], ACT.Ln, bias=1.0).then_inc(ln_ready, 1)
            act.wait_ge(r_T, 1)
            r4 = ps[:, 0, 0:ST * 36].rearrange("p (i n) -> p i n", i=ST)
            A(rT[:, :, :], r4, ACT.Identity)
            A(enm[:, :, :], r4[:, :, 32:36], ACT.Exp, scale=-1.0).then_inc(rt_evac, 1)
            act.wait_ge(rt_evac, 1)
            for q in range(16):
                hh, j = q // 4, q % 4
                act.wait_ge(dmask_done, q + 1)
                last = A(dt_[:, q % 2, 0:P], dt_[:, q % 2, 0:P], ACT.Exp, bias=rT[:, j, hh:hh + 1])
                if j < 3:
                    last = A(dt_[:, q % 2, P:S - j * P], ps[:, 7, (j + 1) * P:S], ACT.Exp, bias=rT[:, j, hh:hh + 1])
                last.then_inc(dt_done, 1)
            act.wait_ge(w_done, 16)
            A(emos[:, :, :], sT[:, T_MO:T_MO + 2, :], ACT.Exp, scale=-1.0)
            A(dt_[:, :, :], pT[:, T_MO:T_MO + 2, 0:S], ACT.Exp, scale=-1.0).then_inc(emo_ready, 1)
            act.wait_ge(saz_ready, 1)
            link(A(mv[:, 4:5], mv[:, 4:5], ACT.Exp, scale=-1.0))
            A(mv[:, 4:5], mv[:, 4:5], ACT.Ln, bias=1.0).then_inc(sln_ready, 1)
            act.wait_ge(sexp_in, 1)
            A(mv[:, 8:11], mv[:, 8:11], ACT.Exp).then_inc(sexp_ready, 1)
            act.wait_ge(pcx_ready, 1)
            A(pc[:, :, 0:NCP], pc[:, :, 0:NCP], ACT.Exp, scale=SCALE).then_inc(pcx_exp, 1)
            NU = len(UNITS)
            for u in range(NU + 1):
                if u < NU:
                    hh, i = UNITS[u]
                    act.wait_ge(mx_ready, u + 1)
                    if u >= 2:
                        act.wait_ge(t_done, u - 1)
                    for r in range(2):
                        last = A(pr[:, u % 2, r, 0:(i + 1) * P], ps[:, 2 * (u % 2) + r, 0:(i + 1) * P], ACT.Exp,
                                 bias=nmx[:, u % 2, r:r + 1], scale=SCALE, accum_out=sm[:, u % 2, r:r + 1])
                    last.then_inc(p_exp, 1)
                if u >= 1:
                    v = u - 1
                    n = (UNITS[v][1] + 1) * P
                    act.wait_ge(t_done, v + 1)
                    if v >= 2:
                        act.wait_ge(pv_done, v - 1)
                    A(prT[:, v % 2, 0, 0:n], ps[:, 4, 0:n], ACT.Identity).then_inc(pt_act, 1)
            act.wait_ge(o_evac, NU)
            for b in range(NB):
                act.wait_ge(wsc_done, b + 1)
                if b:
                    act.wait_ge(w_moved, 16 * b)
                A(sst2[0:NH, :], ps[0:NH, 1 + b % 2, :], ACT.Identity).then_inc(wsc_evac, 1)
                act.wait_ge(wsc_evac, b + 1)
                act.dma_start(swin[8 * b:8 * b + 8, 0:S], sst2[0:NH, :]).then_inc(w_moved, 16)
            act.wait_ge(sgate_moved, 16 * NB)
            A(sg[:, 0:3], sg[:, 0:3], ACT.Exp, scale=-1.0).then_inc(sg_exp, 1)
            act.wait_ge(sx_in, 1)
            A(scm[:, 0:NCB], scm[:, 0:NCB], ACT.Exp, bias=ssx[:, 1:2], scale=SCALE, accum_out=ssx[:, 2:3]).then_inc(sx_out, 1)
            act.wait_ge(sx_in, 2)
            A(swin[0:64, 0:T], swin[0:64, 0:T], ACT.Exp, bias=ssx[:, 4:5], scale=SCALE, accum_out=ssx[:, 5:6]).then_inc(sx_out, 1)
            act.wait_ge(sx_in, 3)
            A(sall[:, :], sall[:, :], ACT.Exp, bias=ssx[:, 7:8], scale=SCALE, accum_out=ssx[:, 8:9]).then_inc(sx_out, 1)
            N2 = len(PART1)
            hi(N_IN)
            hi(N_IN + 1)
            for k in range(KD):
                if k == 0:
                    act.wait_ge(mix_ready, 1)
                A(hR[:, 0, k, :], mix[:, k, :], ACT.Identity).then_inc(h_hi, 1)
            nhi = N_IN + 2
            for m, (kind, t, _) in enumerate(PART2):
                n = N2 + m
                while SPLIT[nhi - 1] < (CHUNK0[n + 1] - 1) // KD:
                    hi(nhi)
                    nhi += 1
                item_ready(act, n)
                while nhi < len(SPLIT) and SPLIT[nhi - 2] < CHUNK0[n + 1] // KD:
                    hi(nhi)
                    nhi += 1
                if kind == "out":
                    act.wait_ge(x_ready, t + 1)
                    squares(1, t)
                    if t == KD - 1:
                        act.wait_ge(var_ready, 2)
                        A(rstd[:, :], rstd[:, :], ACT.Sqrt).then_inc(root_ready, 1)
                        normed(1, 24)
                elif kind == "up":
                    j, b = t % FC, t // FC
                    v = 2 * j + b
                    if v >= 2:
                        act.wait_ge(y_used, v - 1)
                    if v == 0:
                        act.wait_ge(zero_done, 1)
                    link(A(zb[:, b, 2:T + 2].rearrange("p (a n) -> p a n", a=2), ps[:, 2 * (n % 2):2 * (n % 2) + 2, 0:TH],
                           ACT.Identity))
                    A(yab[:, b, :], zb[:, b, 2:T + 2], ACT.Identity, bias=par_("conv_b", t, t + 1),
                      scale=par_("conv_w", 3 * t + 2, 3 * t + 3)).then_inc(y_ready, 1)
                    if b == 0:
                        act.wait_ge(silu_in, j + 1)
                        if j:
                            act.wait_ge(f_ready, j)
                        A(sil[:, :], yab[:, 0, :], ACT.Silu).then_inc(silu_out, 1)
                    else:
                        act.wait_ge(f_ready, j + 1)
                        if j == FH:
                            act.wait_ge(evac_dve, PART2_AT["down0", KD - 1] + 1)
                        A(fR[:, 0, j % FH, :], yab[:, 1, :], ACT.Identity).then_inc(f_hi, 1)
                elif kind == "down1":
                    act.wait_ge(x_ready, KD + t + 1)
                    squares(2, t)
            act.wait_ge(var_ready, 3)
            A(rstd[:, :], rstd[:, :], ACT.Sqrt).then_inc(root_ready, 1)

        @block.vector
        def _(dve):
            V = nc.vector
            chain = [0]

            def link(ins):
                chain[0] += 1
                ins.then_inc(dve_step, 1)
                dve.wait_ge(dve_step, chain[0])

            def root(n):
                dve.wait_ge(sq_used, (n + 1) * KD)
                V.tensor_scalar(rstd[:, :].rearrange("p (a n) -> p a n", a=2), ps[:, 4:6, 0:TH], EPS, None, ALU.add).then_inc(var_ready, 1)
                dve.wait_ge(root_ready, n + 1)
                link(V.reciprocal(rstd[:, :], rstd[:, :]))

            def normed(n, gain, scale, shift):
                link(V.scalar_tensor_tensor(ab[:, :, :], mod[:, scale:scale + KD, :], 1.0,
                                            par_(gain).unsqueeze(2).broadcast_to([P, KD, 9]), ALU.add, ALU.mult))
                for k in range(KD):
                    t = sq[:, k % 2, :]
                    if k >= 2:
                        dve.wait_ge(h_hi, n * 2 * KD + k - 1)
                    V.tensor_tensor(t, x[:, k, :], rstd[:, :], ALU.mult).then_inc(xn_ready, 1)
                    dve.wait_ge(xn_ready, n * KD + k + 1)
                    link(V.tensor_tensor(t[:, S:T], t[:, S:T], ab[:, k, 1:9], ALU.mult))
                    V.tensor_tensor(t[:, S:T], t[:, S:T], mod[:, shift + k, 1:9], ALU.add).then_inc(h_sample, 1)
                    for c in range(max(k - 1, 0), k + (k == KD - 1)):
                        dve.wait_ge(h_hi, n * 2 * KD + c + 1)
                        V.tensor_tensor(hR[:, 1, c, :], sq[:, c % 2, :], hR[:, 0, c, :].bitcast(F32), ALU.subtract)\
                            .then_inc(h_lo, 1)
                        dve.wait_ge(h_lo, n * 2 * KD + c + 1)

            def compress(src_k, src_v, nseg, at, seg4):
                for kv, src in enumerate((src_k, src_v)):
                    for half, dst in enumerate((poolA, poolB)):
                        w = par_("wpos", 32 * kv + 16 * half, 32 * kv + 16 * half + 16)
                        if seg4:
                            o = tmp[:, 0:nseg * 16].rearrange("p (a n j) -> p a n j", a=HALF, j=16)
                            ww = w.unsqueeze(1).unsqueeze(1).broadcast_to([P, HALF, 8, 16])
                        else:
                            o = tmp[:, 0:nseg * 16].rearrange("p (n j) -> p n j", j=16)
                            ww = w.unsqueeze(1).broadcast_to([P, nseg, 16])
                        link(V.tensor_tensor(o, src, ww, ALU.mult))
                        last = V.tensor_reduce(dst[:, kv, at:at + nseg],
                                               tmp[:, 0:nseg * 16].rearrange("p (n j) -> p n j", j=16), AX, ALU.add)
                        if not (kv and half):
                            link(last)
                return last

            dve.wait_ge(silu_exp, 1)
            link(V.tensor_scalar(sc2[:, :, :], sc2[:, :, :], 1.0, None, ALU.add))
            link(V.reciprocal(sc2[:, :, :], sc2[:, :, :]))
            V.tensor_tensor(sc[:, :, :], sc2[:, :, :], par_("c").rearrange("p (k n) -> p k n", k=KD), ALU.mult).then_inc(silu_ready, 1)
            root(0)
            dve.wait_ge(turn_evac, 16)
            dve.wait_ge(x_landed, 16 * KD)
            normed(0, "g1", 8, 0)

            for b in range(NB):
                for s in range(2):
                    dve.wait_ge(cache_landed[s], 16 * HALF * (b + 1))
                    pg = pages[:, s, :, :]
                    compress(pg[:, :, 0:P].rearrange("p a (n j) -> p a n j", j=16),
                             pg[:, :, 2 * P:3 * P].rearrange("p a (n j) -> p a n j", j=16), 64, 64 * s, True).then_inc(comp_done, 1)
                    dve.wait_ge(comp_done, 2 * b + s + 1)
                if b:
                    dve.wait_ge(blocks_done, b)
                V.tensor_tensor(pooled[:, :, 0:NCB], poolA[:, :, 0:NCB], poolB[:, :, 1:NCB + 1], ALU.add).then_inc(pooled_ready, 1)
                dve.wait_ge(pooled_ready, b + 1)

            dve.wait_ge(evac_act, len(PART1))
            link(compress(pT[:, T_KC, 0:S].rearrange("p (n j) -> p n j", j=16),
                          pT[:, T_VC, 0:S].rearrange("p (n j) -> p n j", j=16), S // 16, 0, False))
            dve.wait_ge(blocks_done, NB)
            V.tensor_tensor(pooled[:, :, 0:NCP], poolA[:, :, 0:NCP], poolB[:, :, 1:NCP + 1], ALU.add).then_inc(pooled_ready, 1)

            dve.wait_ge(pooled_ready, NB + 1)
            link(V.memset(r36[0:36, :], 0.0))
            link(V.memset(zro[0:4, :], 0.0))
            link(V.tensor_scalar(r36[0:4, :], pT[0:4, T_G, 0:S], par_("gate_b", hi=4), None, ALU.add))
            link(V.tensor_scalar(bro[0:4, :], pT[32:36, T_G, 0:S], par_("gate_b", lo=32, hi=36), None, ALU.add))
            V.scalar_tensor_tensor(lfo[0:4, :], bro[0:4, :], -1.0, bro[0:4, :], ALU.mult, ALU.max).then_inc(az_ready, 1)
            dve.wait_ge(ln_ready, 1)
            link(V.scalar_tensor_tensor(lfo[0:4, :], bro[0:4, :], 0.0, lfo[0:4, :], ALU.min, ALU.subtract))
            link(V.tensor_tensor_scan(bro[0:4, :], lfo[0:4, :], zro[0:4, :], 0.0, ALU.add, ALU.add))
            link(V.tensor_tensor(r36[0:4, :], r36[0:4, :], bro[0:4, :], ALU.subtract))
            link(V.tensor_tensor_scan(mro[0:4, :], r36[0:4, :], zro[0:4, :], 0.0, ALU.max, ALU.max))
            link(V.tensor_tensor(r36[32:36, :], bro[0:4, :], mro[0:4, :], ALU.add))
            link(V.tensor_copy(mout[0:4, 0:1], r36[32:36, S - 1:S]))
            V.tensor_scalar(mro[0:4, :], mro[0:4, :], -1.0, None, ALU.mult).then_inc(rows_ready, 1)

            dve.wait_ge(rt_evac, 1)
            dve.wait_ge(kn_evac, 1)
            for hh in range(4):
                dve.wait_ge(bc_done, hh + 1)
                for j in range(ST):
                    q = 4 * hh + j
                    V.tensor_tensor(dt_[:, q % 2, 0:P], ps[:, 7, j * P:(j + 1) * P], con_("ct"), ALU.add).then_inc(dmask_done, 1)
                    dve.wait_ge(dt_done, q + 1)
                    dve.wait_ge(mscore_done, q + 1)
                    if hh and j == 0:
                        dve.wait_ge(num_done, hh)
                    n = S - j * P
                    V.tensor_tensor(wj[:, OFF[j]:OFF[j] + n], ps[:, 4 + q % 2, 0:n], dt_[:, q % 2, 0:n], ALU.mult)
                    if j == 0 and hh:
                        dve.wait_ge(num_evac, hh)
                    V.tensor_scalar(wk[:, j, :], kN[:, hh // 2, j, (hh % 2) * HD:(hh % 2 + 1) * HD], dt_[:, q % 2, n - 1:n], None,
                                    ALU.mult).then_inc(w_done, 1)
                    dve.wait_ge(w_done, q + 1)
                dve.wait_ge(num_done, hh + 1)
                num = ps[:, 6, 0:4 * 65].rearrange("p (i n) -> p i n", i=ST)
                link(V.tensor_copy(d4[:, 0:4], num[:, :, HD]))
                link(V.scalar_tensor_tensor(d4[:, 4:8], d4[:, 0:4], -1.0, d4[:, 0:4], ALU.mult, ALU.max))
                link(V.tensor_tensor(d4[:, 4:8], d4[:, 4:8], enm[:, :, hh], ALU.max))
                link(V.reciprocal(d4[:, 4:8], d4[:, 4:8]))
                V.tensor_tensor(hN[:, :, hh * HD:(hh + 1) * HD], num[:, :, 0:HD], d4[:, 4:8].unsqueeze(2).broadcast_to([P, ST, HD]),
                                ALU.mult).then_inc(num_evac, 1)
            link(V.tensor_copy(cout[0:HD, :, :], ps[0:HD, 3, 0:260].rearrange("p (h n) -> p h n", h=4)))
            dve.wait_ge(emo_ready, 1)
            link(V.tensor_scalar(dt_[:, :, :], dt_[:, :, :], 1.0, None, ALU.add))
            link(V.reciprocal(dt_[:, :, :], dt_[:, :, :]))
            dve.wait_ge(hT_done, 1)
            V.tensor_tensor(mix[:, 4:6, 0:S], ps[:, 1:3, :], dt_[:, :, :], ALU.mult).then_inc(mmix_ready, 1)

            dve.wait_ge(rows_moved, 16 * 48)
            dve.wait_ge(rec_landed, 32)
            q_, k_, v_ = smr[:, 0:64], smr[:, 64:128], smr[:, 128:144]
            link(V.tensor_tensor(mv[:, 0:1], smr[:, 144:145], par_("igb"), ALU.add))
            link(V.tensor_tensor(mv[:, 1:2], smr[:, 145:146], par_("fgb"), ALU.add))
            V.scalar_tensor_tensor(mv[:, 4:5], mv[:, 1:2], -1.0, mv[:, 1:2], ALU.mult, ALU.max).then_inc(saz_ready, 1)
            dve.wait_ge(sln_ready, 1)
            link(V.scalar_tensor_tensor(mv[:, 1:2], mv[:, 1:2], 0.0, mv[:, 4:5], ALU.min, ALU.subtract))
            link(V.tensor_tensor(mv[:, 2:3], mv[:, 1:2], par_("mm"), ALU.add))
            link(V.tensor_tensor(mv[:, 3:4], mv[:, 2:3], mv[:, 0:1], ALU.max))
            V.tensor_tensor(mv[:, 8:9], mv[:, 0:1], mv[:, 3:4], ALU.subtract)
            V.tensor_tensor(mv[:, 9:10], mv[:, 2:3], mv[:, 3:4], ALU.subtract)
            V.tensor_scalar(mv[:, 10:11], mv[:, 3:4], -1.0, None, ALU.mult).then_inc(sexp_in, 1)
            c_de = cst[:, :].rearrange("p (d e) -> p d e", e=16)
            t_ed = ctmp[:, :].rearrange("p (e d) -> p e d", d=64)
            t_de = ctmp[:, :].rearrange("p (d e) -> p d e", e=16)
            link(V.tensor_tensor(t_ed, c_de.rearrange("p d e -> p e d"), q_.unsqueeze(1).broadcast_to([P, 16, 64]), ALU.mult))
            link(V.tensor_reduce(qc[:, :], t_ed, AX, ALU.add))
            link(V.tensor_tensor(ctmp[:, 0:64], q_, k_, ALU.mult))
            link(V.tensor_reduce(mv[:, 11:12], ctmp[:, 0:64], AX, ALU.add))
            link(V.tensor_tensor(ctmp[:, 0:64], q_, par_("mn"), ALU.mult))
            link(V.tensor_reduce(mv[:, 12:13], ctmp[:, 0:64], AX, ALU.add))
            dve.wait_ge(sexp_ready, 1)
            link(V.tensor_tensor(mv[:, 11:12], mv[:, 11:12], mv[:, 8:9], ALU.mult))
            link(V.scalar_tensor_tensor(mv[:, 13:14], mv[:, 12:13], mv[:, 9:10], mv[:, 11:12], ALU.mult, ALU.add))
            link(V.scalar_tensor_tensor(mv[:, 14:15], mv[:, 13:14], -1.0, mv[:, 13:14], ALU.mult, ALU.max))
            link(V.tensor_tensor(mv[:, 14:15], mv[:, 14:15], mv[:, 10:11], ALU.max))
            link(V.reciprocal(mv[:, 14:15], mv[:, 14:15]))
            link(V.tensor_scalar(qc[:, :], qc[:, :], mv[:, 9:10], None, ALU.mult))
            link(V.scalar_tensor_tensor(shh[:, :], v_, mv[:, 11:12], qc[:, :], ALU.mult, ALU.add))
            link(V.tensor_scalar(shh[:, :], shh[:, :], mv[:, 14:15], None, ALU.mult))
            link(V.tensor_copy(t_de, k_.unsqueeze(2).broadcast_to([P, 64, 16])))
            link(V.scalar_tensor_tensor(t_de, t_de, mv[:, 8:9], v_.unsqueeze(1).broadcast_to([P, 64, 16]), ALU.mult, ALU.mult))
            link(V.scalar_tensor_tensor(cst[:, :], cst[:, :], mv[:, 9:10], ctmp[:, :], ALU.mult, ALU.add))
            link(V.tensor_scalar(smr[:, 146:210], k_, mv[:, 8:9], None, ALU.mult))
            V.scalar_tensor_tensor(smr[:, 146:210], par_("mn"), mv[:, 9:10], smr[:, 146:210], ALU.mult, ALU.add)\
                .then_inc(srec_ready, 1)
            dve.wait_ge(srec_ready, 1)

            dve.wait_ge(g_exp, 1)
            link(V.tensor_scalar(gN[:, :, :], gN[:, :, :], 1.0, None, ALU.add))
            link(V.reciprocal(gN[:, :, :], gN[:, :, :]))

            for t in range(2):
                link(V.memset(zp[:, 0, 0:15], 0.0))
                buf = [zp[:, 0, :], zp[:, 1, :]]
                link(V.tensor_copy(zp[:, 0, 15:15 + S], pT[:, T_PU + t, 0:S]))
                lo, cur = 0, 0
                for w in (1, 2, 4, 8)[:2 * t + 2]:
                    lo += w
                    top = w == (2, 8)[t]
                    if top:
                        link(V.tensor_copy(md[hr[0], t, :], buf[cur][hr[0], 15:15 + S]))
                    r = slice(HD, P) if top else slice(0, P)
                    link(V.tensor_tensor(buf[1 - cur][r, lo:15 + S], buf[cur][r, lo:15 + S], buf[cur][r, lo - w:15 + S - w], ALU.add))
                    cur = 1 - cur
                link(V.tensor_copy(md[hr[1], t, :], buf[cur][hr[1], 15:15 + S]))
                link(V.tensor_tensor(zp[:, 1, 15:31], md[:, t, 0:16], con_("rcnt", 16 * t, 16 * t + 16), ALU.mult))
                link(V.tensor_tensor(md[:, t, 0:16], zp[:, 1, 15:31], pT[:, T_PU + t, 0:16], ALU.subtract))
                link(V.scalar_tensor_tensor(md[:, t, 16:S], md[:, t, 16:S], con_("rw", t, t + 1), pT[:, T_PU + t, 16:S],
                                            ALU.mult, ALU.subtract))
                link(V.tensor_copy(zs[:, t, :, 15], sT[:, T_PU + t, :]))
                for g in range(2):
                    w = (2, 4, 8, 16)[2 * t + g]
                    link(V.tensor_reduce(zsum[hr[g], t, :], zs[hr[g], t, :, 16 - w:16], AX, ALU.add))
                last = V.scalar_tensor_tensor(mds[:, t, :], zsum[:, t, :], con_("rw", t, t + 1), sT[:, T_PU + t, :],
                                              ALU.mult, ALU.subtract)
            last.then_inc(pool_ready, 1)
            dve.wait_ge(pool_ready, 1)

            dve.wait_ge(csc_done, 1)
            for half in range(2):
                s4 = ps[:, half, :].rearrange("p (a i n) -> p a i n", a=4, i=ST)[:, :, :, 0:NCP]
                p4 = pc[:, 16 * half:16 * half + 16, :].rearrange("p (a i) n -> p a i n", a=4)[:, :, :, 0:NCP]
                madd = con_("cadd").rearrange("p (i n) -> p i n", i=ST).unsqueeze(1).broadcast_to([P, 4, ST, NCP])
                link(V.tensor_tensor(p4, s4, madd, ALU.add))
            link(V.tensor_reduce(mx[:, 0, :], pc[:, :, 0:NCP], AX, ALU.max))
            V.tensor_tensor(pc[:, :, 0:NCP], pc[:, :, 0:NCP], mx[:, 0, :].unsqueeze(2).broadcast_to([P, 32, NCP]), ALU.subtract)\
                .then_inc(pcx_ready, 1)
            dve.wait_ge(pcx_exp, 1)
            for half in range(2):
                p4 = pc[:, 16 * half:16 * half + 16, :].rearrange("p (a i) n -> p a i n", a=4)[:, :, :, 0:NCP]
                mmul = con_("cmul").rearrange("p (i n) -> p i n", i=ST).unsqueeze(1).broadcast_to([P, 4, ST, NCP])
                link(V.tensor_tensor(p4, p4, mmul, ALU.mult))
            link(V.tensor_reduce(mx[:, 1, :], pc[:, :, 0:NCP], AX, ALU.add))
            link(V.tensor_scalar(mx[:, 1, :], mx[:, 1, :], float(np.finfo(np.float32).tiny), None, ALU.max))
            link(V.reciprocal(mx[:, 2, :], mx[:, 1, :]))
            g0 = gN[:, :, 0:22:3].rearrange("p i h -> p h i")
            link(V.tensor_tensor(mx[:, 3, :].rearrange("p (h i) -> p h i", h=NH), mx[:, 2, :].rearrange("p (h i) -> p h i", h=NH),
                                 g0, ALU.mult))
            V.tensor_tensor(pc[:, :, 0:NCP], pc[:, :, 0:NCP], mx[:, 3, :].unsqueeze(2).broadcast_to([P, 32, NCP]), ALU.mult)\
                .then_inc(pc_ready, 1)

            NU = len(UNITS)
            for u in range(NU + 2):
                if u < NU:
                    hh, i = UNITS[u]
                    a = u % 2
                    two = ps[:, 2 * a:2 * a + 2, :]
                    dve.wait_ge(qk_done, u + 1)
                    d = two[:, :, i * P:(i + 1) * P]
                    link(V.tensor_tensor(d, d, con_("cq").unsqueeze(1).broadcast_to([P, 2, P]), ALU.add))
                    link(V.tensor_reduce(nmx[:, a, :], two[:, :, 0:(i + 1) * P], AX, ALU.max))
                    V.tensor_scalar(nmx[:, a, :], nmx[:, a, :], -SCALE, None, ALU.mult).then_inc(mx_ready, 1)
                if 1 <= u <= NU:
                    v = u - 1
                    n = (UNITS[v][1] + 1) * P
                    dve.wait_ge(t_done, v + 1)
                    if v >= 2:
                        dve.wait_ge(pv_done, v - 1)
                    V.tensor_copy(prT[:, v % 2, 1, 0:n], ps[:, 5, 0:n])
                    V.tensor_copy(pcT[0:NCP, v % 2, :], ps[0:NCP, 6, 0:P]).then_inc(pt_dve, 1)
                    dve.wait_ge(pt_dve, v + 1)
                if u < NU:
                    dve.wait_ge(p_exp, u + 1)
                    link(V.reciprocal(fac[:, a, :], sm[:, a, :]))
                    link(V.tensor_tensor(fac[:, a, :], fac[:, a, :], gN[:, i, 3 * hh + 1:3 * hh + 3], ALU.mult))
                    for r in range(2):
                        last = V.tensor_scalar(pr[:, a, r, 0:(i + 1) * P], pr[:, a, r, 0:(i + 1) * P], fac[:, a, r:r + 1], None,
                                               ALU.mult)
                    last.then_inc(p_ready, 1)
                if u >= 2:
                    hh, i = UNITS[u - 2]
                    rows = hr[hh // G]
                    dve.wait_ge(pv_done, u - 1)
                    V.tensor_copy(mix[rows, hh % G, i * P:(i + 1) * P], ps[rows, 7, 0:P]).then_inc(o_evac, 1)

            dve.wait_ge(pool_mm, 1)
            for t in range(2):
                V.tensor_scalar(mix[:, 6 + t, 0:S], ps[:, 4 + t, :], par_("pool_s", t, t + 1), None, ALU.mult)
                link(V.tensor_scalar(mix[:, 6 + t, S:T], ps[:, 6, t * NB:(t + 1) * NB], par_("pool_s", t, t + 1), None, ALU.mult))
            link(V.tensor_scalar(emos[:, :, :], emos[:, :, :], 1.0, None, ALU.add))
            link(V.reciprocal(emos[:, :, :], emos[:, :, :]))
            dve.wait_ge(shT_done, 1)
            link(V.tensor_tensor(mix[:, 4:6, S:T], ps[:, 7, 0:2 * NB].rearrange("p (t b) -> p t b", t=2), emos[:, :, :], ALU.mult))

            dve.wait_ge(snew_done, 1)
            dve.wait_ge(sst_moved, 32 * NB)
            link(V.tensor_tensor(sall[:, NPG * P:NPG * P + NB], ps[0:64, 0, 0:NB], con_("newm", rows=64), ALU.add))
            link(V.tensor_tensor(swin[0:64, S:T], ps[0:64, 0, NB:2 * NB], con_("newm", rows=64), ALU.add))
            link(V.tensor_reduce(ssx[:, 0:1], scm[:, 0:NCB], AX, ALU.max))
            V.tensor_scalar(ssx[:, 1:2], ssx[:, 0:1], -SCALE, None, ALU.mult).then_inc(sx_in, 1)
            dve.wait_ge(sg_exp, 1)
            link(V.tensor_scalar(sg[:, 0:3], sg[:, 0:3], 1.0, None, ALU.add))
            link(V.reciprocal(sg[:, 0:3], sg[:, 0:3]))
            dve.wait_ge(sx_out, 1)
            link(V.reciprocal(ssx[:, 9:10], ssx[:, 2:3]))
            V.tensor_scalar(scm[:, 0:NCB], scm[:, 0:NCB], ssx[:, 9:10], None, ALU.mult).then_inc(imp_in, 1)
            dve.wait_ge(w_moved, 16 * NB)
            link(V.memset(swin[0:64, 0:1], NEG))
            link(V.tensor_reduce(ssx[:, 3:4], swin[0:64, 0:T], AX, ALU.max))
            V.tensor_scalar(ssx[:, 4:5], ssx[:, 3:4], -SCALE, None, ALU.mult).then_inc(sx_in, 1)
            link(V.memset(simp[0:64, :], 0.0))
            dve.wait_ge(imp_done, 1)
            link(V.tensor_copy(simp[0:64, 1:1 + NCB], ps[0:64, 3, 0:NCB]))
            link(V.tensor_reduce(sel[:, 0, 0:NSB], simp[0:64, 0:132].rearrange("p (n r) -> p n r", r=4), AX, ALU.add))
            link(V.tensor_tensor(sel[:, 0, 0:NSB], sel[:, 0, 0:NSB], simp[0:64, 4:133:4], ALU.add))
            link(V.memset(sel[:, 0, 0:1], 1e6))
            link(V.memset(sel[:, 0, NSB - 2:NSB], 1e6))
            s_i = sel[:, 0, 0:NSB].unsqueeze(1).broadcast_to([64, NSB, NSB])
            s_j = sel[:, 0, 0:NSB].unsqueeze(2).broadcast_to([64, NSB, NSB])
            rk = rank[0:64, :].rearrange("p (j i) -> p j i", j=NSB)
            te = tie[0:64, :].rearrange("p (j i) -> p j i", j=NSB)
            link(V.tensor_tensor(rk, s_i, s_j, ALU.is_gt))
            link(V.tensor_tensor(te, s_i, s_j, ALU.is_equal))
            dve.wait_ge(ltri_landed, 16)
            link(V.tensor_tensor(tie[0:64, :], tie[0:64, :], ltri[0:64, :], ALU.mult))
            link(V.tensor_tensor(rank[0:64, :], rank[0:64, :], tie[0:64, :], ALU.add))
            link(V.tensor_reduce(sel[:, 1, 0:NSB], rk, AX, ALU.add))
            link(V.tensor_scalar(sel[:, 2, 0:NSB], sel[:, 1, 0:NSB], float(NSEL) - 0.5, NEG, ALU.is_gt, ALU.mult))
            s3 = sall[:, 0:NPG * P].rearrange("p (n k) -> p n k", k=64)
            link(V.tensor_tensor(s3, s3, sel[:, 2, 0:32].unsqueeze(2).broadcast_to([64, 32, 64]), ALU.add))
            link(V.tensor_reduce(ssx[:, 6:7], sall[:, :], AX, ALU.max))
            V.tensor_scalar(ssx[:, 7:8], ssx[:, 6:7], -SCALE, None, ALU.mult).then_inc(sx_in, 1)
            link(V.tensor_scalar(scm[:, 0:NCB], scm[:, 0:NCB], sg[:, 0:1], None, ALU.mult))
            dve.wait_ge(sx_out, 3)
            for r, (n, buf) in enumerate(((8, sall[:, :]), (5, swin[0:64, 0:T]))):
                link(V.reciprocal(ssx[:, 10 + r:11 + r], ssx[:, n:n + 1]))
                link(V.tensor_tensor(ssx[:, 12 + r:13 + r], ssx[:, 10 + r:11 + r], sg[:, 1 + r:2 + r], ALU.mult))
                last = V.tensor_scalar(buf, buf, ssx[:, 12 + r:13 + r], None, ALU.mult)
            last.then_inc(sp_ready, 1)
            dve.wait_ge(spT_done, 1)
            V.tensor_copy(ptS[:, 0:NPG, :].rearrange("p (a c) r -> p a (c r)", a=2), ps[:, 4:6, :])
            V.tensor_copy(ptS[:, NPG:NPG + ST, :].rearrange("p c r -> p (c r)"), ps[:, 6, 0:256])
            V.tensor_copy(ptS[0:NCB, 20, :], ps[0:NCB, 0, 0:64])
            V.tensor_copy(ptS[0:NB, 21, :], ps[0:NB, 1, 0:64])
            V.tensor_copy(ptS[0:NB, 22, :], ps[0:NB, 2, 0:64]).then_inc(spT_evac, 1)
            dve.wait_ge(spv_done, NB)
            for hh in range(NH):
                rows = hr[hh // G]
                last = V.tensor_copy(mix[rows, hh % G, S:T], ps[rows, 7, 0:64].rearrange("p (b r) -> p b r", b=NB)[:, :, hh])
            last.then_inc(mix_ready, 1)

            for k in range(KD):
                dve.wait_ge(h_hi, KD + k + 1)
                V.tensor_tensor(hR[:, 1, k, :], mix[:, k, :], hR[:, 0, k, :].bitcast(F32), ALU.subtract).then_inc(h_lo, 1)

            def residual(m, gate, done):
                kind, t, _ = PART2[m]
                n = len(PART1) + m
                a = 2 * (n % 2)
                item_ready(dve, n)
                gp = mod[:, gate + t, 0:1]
                link(V.tensor_tensor(t8[:, :], ps[:, a + 1, TH - NB:TH], mod[:, gate + t, 1:9], ALU.mult))
                V.scalar_tensor_tensor(x[:, t, 0:TH], ps[:, a, 0:TH], gp, x[:, t, 0:TH], ALU.mult, ALU.add)
                V.scalar_tensor_tensor(x[:, t, TH:S], ps[:, a + 1, 0:TH - NB], gp, x[:, t, TH:S], ALU.mult, ALU.add)\
                    .then_inc(evac_dve, 1)
                last = V.tensor_tensor(x[:, t, S:T], x[:, t, S:T], t8[:, :], ALU.add)
                if done:
                    last.then_inc(x_ready, 1)
                    dve.wait_ge(x_ready, done)
                else:
                    link(last)

            for m, (kind, t, _) in enumerate(PART2):
                if kind == "out":
                    residual(m, 16, t + 1)
                    if t == KD - 1:
                        root(1)
                        normed(1, "g2", 32, 24)
                        V.memset(zb[:, :, 0:2], 0.0).then_inc(zero_done, 1)
                        dve.wait_ge(ffst_landed, 16)
                        dve.wait_ge(state_out, 16 * 8)
                        link(V.tensor_copy(ffo_s[:, :, 0, :], ffst_t[:, :, 1, :]))
                elif kind == "up":
                    j, b = t % FC, t // FC
                    v = 2 * j + b
                    w = [par_("conv_w", 3 * t + c, 3 * t + c + 1) for c in range(3)]
                    y, z = yab[:, b, :], zb[:, b, :]
                    dve.wait_ge(y_ready, v + 1)
                    nc.vector.tensor_copy(ffo_p[:, t, :], z[:, S:S + 2]).then_inc(evac_dve, 1)
                    V.tensor_copy(ffo_s[:, t, 1, :], z[:, S + 2:T + 2])
                    link(V.scalar_tensor_tensor(y[:, S:T], ffst_t[:, t, 1, :], w[1], y[:, S:T], ALU.mult, ALU.add))
                    link(V.scalar_tensor_tensor(y[:, S:T], ffst_t[:, t, 0, :], w[0], y[:, S:T], ALU.mult, ALU.add))
                    link(V.scalar_tensor_tensor(y[:, 0:S], z[:, 1:S + 1], w[1], y[:, 0:S], ALU.mult, ALU.add))
                    last = V.scalar_tensor_tensor(y[:, 0:S], z[:, 0:S], w[0], y[:, 0:S], ALU.mult, ALU.add)
                    if b == 0:
                        last.then_inc(silu_in, 1)
                        dve.wait_ge(silu_out, j + 1)
                        dve.sem_inc(y_used, 1)
                    else:
                        link(last)
                        V.tensor_tensor(y, sil[:, :], y, ALU.mult).then_inc(f_ready, 1)
                        dve.wait_ge(f_hi, j + 1)
                        V.tensor_tensor(fR[:, 1, j % FH, :], y, fR[:, 0, j % FH, :].bitcast(F32), ALU.subtract).then_inc(f_lo, 1)
                        dve.wait_ge(f_lo, j + 1)
                        dve.sem_inc(y_used, 1)
                else:
                    residual(m, 40, KD + t + 1 if kind == "down1" else 0)
            root(2)
            for k in range(KD):
                link(V.tensor_tensor(x[:, k, :], x[:, k, :], rstd[:, :], ALU.mult))
                V.tensor_scalar(x[:, k, :], x[:, k, :], par_("gf", k, k + 1), None, ALU.mult).then_inc(out_ready, 1)


def _constants():
    c = np.zeros((P, NCON), np.float32)

    def put(name, a, rows=P):
        at, n = CON[name]
        c[:rows, at:at + n] = a.reshape(rows, n)

    put("ident", np.eye(P))
    put("ones", np.ones((P, P)))
    put("mean", np.full((P, P), 1.0 / D))
    i = np.arange(P)
    put("cq", np.where(i[None, :] <= i[:, None], 0.0, NEG))
    put("ct", np.where(i[None, :] >= i[:, None], 0.0, NEG))
    pos = (np.arange(ST)[None, :] * P + i[:, None])[:, :, None]
    seen = 16 * np.arange(NCP)[None, None, :] + 31 <= pos
    put("cadd", np.where(seen, 0.0, NEG))
    put("cmul", np.where(seen, 1.0, 0.0))
    win = np.array([[2, 8], [4, 16]], np.float32)[(i >= HD).astype(int)]
    put("rw", 1.0 / win)
    put("rcnt", 1.0 / np.minimum(win[:, :, None], np.arange(1, 17)[None, None, :]))
    r = np.arange(64)
    put("grp", (r[:, None] // 4 == r[None, :] // 4) * 1.0, 64)
    put("newm", np.where(r[:, None] // 8 == np.arange(NB)[None, :], 0.0, NEG), 64)
    return c


def _chunks(w):
    return w.reshape(-1, P, w.shape[1]).transpose(1, 0, 2)


def _stream(w):
    ada, w_in, w_out, up, down = (np.asarray(w[n])[0] for n in ("ada_w", "w_in", "w_out", "ffn_w_up", "ffn_w_down"))
    q, kv, ng, mq, mk, mv_, mif, mo, pu = np.split(w_in, np.cumsum([512, 768, 24, 256, 256, 256, 8, 256]), axis=1)
    q = q.reshape(D, 2, G, HD).transpose(0, 2, 1, 3).reshape(D, 512)
    gates = np.zeros((D, P), np.float32)
    gates[:, 0:4], gates[:, 32:36], gates[:, 64:88] = mif[:, :4], mif[:, 4:], ng
    kc, vc, ks, vs, kw, vw = np.split(kv, 6, axis=1)
    cols = np.concatenate([q, kc, vc, ks, kw, mk, mq, mo, pu, gates, vs, vw, mv_], axis=1)
    rows = np.concatenate([w_out[:512].reshape(2, G, HD, D).transpose(1, 0, 2, 3).reshape(512, D), w_out[512:]])
    src = {"ada": _chunks(ada), "in": _chunks(cols), "out": _chunks(rows), "up": _chunks(up), "down": _chunks(down)}
    src["down0"], src["down1"] = src["down"][:, :FH], src["down"][:, FH:]
    stream = np.concatenate([src[kind][:, :, t * P:(t + 1) * P] for kind, t, _ in ITEMS], axis=1)
    return stream.reshape(P, NSLOT, KD * P).transpose(1, 0, 2)


def _params(w):
    p = np.zeros((P, NPAR), np.float32)

    def put(name, a, rows=slice(0, P)):
        at, n = PAR[name]
        p[rows, at:at + n] = np.asarray(a).reshape(-1, n)

    col = lambda a: np.asarray(a).reshape(-1, P).T
    put("g1", col(w["norm1_g"][0]))
    put("g2", col(w["norm2_g"][0]))
    put("gf", col(w["final_g"]))
    put("ada_b", col(w["ada_b"][0]))
    put("conv_w", np.asarray(w["ffn_conv_w"])[0].reshape(3, 2 * FC, P).transpose(2, 1, 0))
    put("conv_b", col(w["ffn_conv_b"][0]))
    put("pool_s", col(w["pool_scale"][0]))
    wpos = np.asarray(w["nsa_cmp_pos"])[0].transpose(2, 0, 1)
    put("wpos", np.concatenate([wpos, wpos]))
    b = np.asarray(w["nsa_cmp_b"])[0]
    put("bk", np.concatenate([b[0], b[0]]))
    put("bv", np.concatenate([b[1], b[1]]), slice(0, 1))
    gb = np.asarray(w["mlstm_gate_b"])[0]
    put("gate_b", gb[:4], slice(0, 4))
    put("gate_b", gb[4:], slice(32, 36))
    put("igb", np.tile(np.repeat(gb[:4], NB), 4))
    put("fgb", np.tile(np.repeat(gb[4:], NB), 4))
    c = np.concatenate([np.asarray(w["c_prompt"]), np.asarray(w["c_sample"])])
    put("c", c.reshape(9, KD, P).transpose(2, 1, 0))
    cw = np.zeros((P, 2, P), np.float32)
    pw = np.zeros((P, 2, P), np.float32)
    for t in range(2):
        for g in range(2):
            r = slice(g * HD, (g + 1) * HD)
            cw[r, t, r] = np.asarray(w["nsa_cmp_w"])[0, t]
            pw[r, t, r] = np.asarray(w["pool_w"])[0, 2 * t + g]
    put("cw", cw)
    put("pw", pw)
    put("mn", np.tile(np.asarray(w["state_mlstm_n"])[0].transpose(1, 0, 2).reshape(32, HD), (4, 1)))
    put("mm", np.tile(np.asarray(w["state_mlstm_m"])[0].T.reshape(32, 1), (4, 1)))
    return p


def kernel(**w):
    import concourse.bacc as bacc
    from concourse.bass_utils import run_bass_kernel_spmd

    f = {n: np.asarray(a) for n, a in w.items()}
    tokens = np.concatenate([f["x_prompt"][0], f["x_sample"][:, 0]])
    ck = f["cache_k"][0].reshape(NPHYS, PAGE, 2, P)
    cv = f["cache_v"][0].reshape(NPHYS, PAGE, 2, P)
    fm = lambda a: a.transpose(0, 2, 1)
    ins = {
        "xT": tokens.T.reshape(KD, P, T).transpose(1, 0, 2),
        "weights": _stream(w),
        "params": _params(w),
        "constants": _constants(),
        "hot": np.repeat(np.eye(4, dtype=np.float32), P, axis=1),
        "ltri": np.tile(np.tril(np.ones((NSB, NSB), np.float32), -1).reshape(1, -1), (64, 1)),
        "page_table": f["page_table"].reshape(1, NB * NPG),
        "cache_keys": np.concatenate([fm(ck[:, :, 0]), fm(ck[:, :, 1]), fm(cv[:, :, 0])], axis=2),
        "cache_values": cv[:, :, 1],
        "win_keys": f["cache_win_k"][0].reshape(NB, S, P).transpose(2, 0, 1),
        "win_values": f["cache_win_v"][0].reshape(NB, ST, P, P).transpose(2, 0, 1, 3),
        "mlstm_C": f["state_mlstm_C"][0].reshape(NB, 4, HD, 4, 16).transpose(3, 1, 0, 2, 4).reshape(P, HD * 16),
        "mlstm_m": f["state_mlstm_m"][0],
        "pool_state": f["state_pool"][0].reshape(NB, 15, 2, P).transpose(3, 2, 0, 1),
        "ffn_state": f["state_ffn_conv"][0].reshape(NB, 2, 2 * FC, P).transpose(3, 2, 1, 0),
    }
    outs = {
        "y": (P, KD, T), "kv_fm": (P, 4, S), "v_tm": (P, ST, 2 * P), "sample_proj": (P, N_FM, NB), "sample_v": (NB, 2 * P),
        "wk": (P, NB, S - 1), "wv": (P, NB, ST, P), "C": (HD, 4, HD + 1), "m": (4, 1), "pool": (P, 2, 15),
        "sC": (P, HD * 16), "sn": (32, HD), "sm": (32, 1), "spool": (P, 2, NB, 15), "ffp": (P, 2 * FC, 2),
        "ffs": (P, 2 * FC, 2, NB),
    }
    nc = bacc.Bacc("TRN2", target_bir_lowering=False, num_devices=1)
    arrays = {n: np.ascontiguousarray(a) for n, a in ins.items()}
    args = [nc.dram_tensor(n, a.shape, I32 if n == "page_table" else F32, kind="ExternalInput").ap() for n, a in arrays.items()]
    args += [nc.dram_tensor("out_" + n, s, F32, kind="ExternalOutput").ap() for n, s in outs.items()]
    trunk_kernel(nc, *args)
    res = run_bass_kernel_spmd(nc, [arrays], core_ids=[0]).results[0]
    o = {n: res["out_" + n] for n in outs}

    y = o["y"].transpose(2, 1, 0).reshape(T, D)
    heads = lambda a: a.reshape(a.shape[:-1] + (2, HD))
    kc, vc, ks, kw = (heads(o["kv_fm"][:, i].T) for i in range(4))
    vt = o["v_tm"].transpose(1, 0, 2).reshape(S, 2 * P)
    vs, vw = heads(vt[:, :P]), heads(vt[:, P:])
    s = lambda t: o["sample_proj"][:, t].T
    svs, svw = o["sample_v"][:, :P], o["sample_v"][:, P:]
    new = lambda a, b: np.stack([a, b], axis=1)
    swk = np.concatenate([o["wk"].transpose(1, 2, 0), s(T_KW)[:, None]], axis=1)
    wv = o["wv"].transpose(1, 2, 0, 3).reshape(NB, S, P)
    swv = np.concatenate([wv[:, 1:], svw[:, None]], axis=1)
    C = o["C"].transpose(1, 0, 2)
    sC = o["sC"].reshape(4, 4, NB, HD, 16).transpose(2, 1, 3, 0, 4).reshape(NB, 4, HD, HD)
    return (
        y[:S][None], y[S:][:, None],
        new(kc, ks)[None, None], new(vc, vs)[None, None], kw[None, None], vw[None, None],
        np.ascontiguousarray(C[:, :, :HD])[None, None], np.ascontiguousarray(C[:, :, HD])[None, None], o["m"].reshape(1, 1, 4),
        o["pool"].transpose(2, 1, 0).reshape(1, 1, 15, 2 * P), o["ffp"].transpose(2, 1, 0).reshape(1, 1, 2, 2 * FF),
        new(heads(s(T_KC)), heads(s(T_KS)))[None, :, None], new(heads(s(T_VC)), heads(svs))[None, :, None],
        heads(swk)[None], heads(swv)[None],
        sC[None], o["sn"].reshape(4, NB, HD).transpose(1, 0, 2)[None], o["sm"].reshape(4, NB).T[None],
        o["spool"].transpose(2, 3, 1, 0).reshape(1, NB, 15, 2 * P),
        o["ffs"].transpose(3, 2, 1, 0).reshape(1, NB, 2, 2 * FF),
    )
```

```python
from contextlib import ExitStack

import numpy as np
import concourse.bass as bass
from concourse import mybir

F32 = mybir.dt.float32
F32R = mybir.dt.float32r
I32 = mybir.dt.int32
ALU = mybir.AluOpType
ACT = mybir.ActivationFunctionType
AX = mybir.AxisListType.X

P = 128
D = 1024
KD = D // P
S = 512
NB = 8
T = S + NB
ST = S // P
HD = 64
G = 4
NH = 8
PAGE = 128
NPG = 16
NPHYS = 160
HALF = NPG // 2
NCB = 127
NCP = S // 16 - 1
NSB = 33
NSEL = 16
FF = 2816
FC = FF // P
SCALE = HD ** -0.5
NEG = -1e30
EPS = 1e-6

(T_Q, T_KC, T_VC, T_KS, T_KW, T_MK, T_MQ, T_MO, T_PU, T_G, T_VS, T_VW, T_MV) = (0, 4, 5, 6, 7, 8, 10, 12, 14, 16, 17, 18, 19)
N_IN = 21
N_FM = 17

TH = T // 2
EARLY = 16
WINDOWS_FIRST = 4
SAMPLE_AT = 1
EARLY_GROUP = [0, 1, 2, 2, 3, 3, 3, 3, 4, 4, 4, 4, 5, 5, 5, 5]
EXTRA = 3
RAW = 3
FH = FC // 2

def _layout(parts):
    at, out = 0, {}
    for name, n in parts:
        out[name] = (at, n)
        at += n
    return out, at

PAR, NPAR = _layout([("g1", 8), ("g2", 8), ("gf", 8), ("ada_b", 48), ("conv_w", 132), ("conv_b", 44), ("pool_s", 2),
                     ("wpos", 64), ("bk", 1), ("gate_b", 1), ("igb", 1), ("fgb", 1), ("c", 72),
                     ("cw", 256), ("bv", 128), ("pw", 256), ("mn", 64), ("mm", 1)])
CON, NCON = _layout([("ident", 128), ("ones", 128), ("mean", 128), ("cq", 128), ("ct", 128), ("cadd", 124), ("cmul", 124),
                     ("rw", 2), ("rcnt", 32), ("grp", 64), ("newm", 8)])
HOT = 4 * P


def plan():
    part1 = [("ada", t, KD) for t in range(16)] + [("in", t, KD) for t in range(N_IN)]
    part1 += [("ada", t, KD) for t in range(16, 40)]
    part2 = [("out", m, KD) for m in range(KD)]
    for half in range(2):
        for j in range(half * FH, (half + 1) * FH):
            part2 += [("up", j, KD), ("up", FC + j, KD)]
        part2 += [(f"down{half}", m, FH) for m in range(KD)]
    return part1, part2


PART1, PART2 = plan()
N_A = 16 + N_IN
LATE = [("ada", t, KD) for t in range(40, 48)]
ITEMS = PART1 + PART2 + LATE
CHUNK0 = [sum(i[2] for i in ITEMS[:n]) for n in range(len(ITEMS) + 1)]
NSLOT = CHUNK0[-1] // KD
NMAIN = NSLOT - len(LATE)
SPLIT = [g for g in range(NMAIN) if g >= len(PART1) or PART1[g][0] == "in"]
PART2_AT = {(kind, t): m for m, (kind, t, _) in enumerate(PART2)}


def places():
    out = []
    for g in range(NSLOT):
        turn = (g - N_A) % (RAW + EXTRA)
        if g < EARLY:
            out.append(("early", g))
        elif g >= NMAIN:
            out.append(("early", g - NMAIN))
        elif N_A <= g < len(PART1) and turn >= RAW:
            out.append(("extra", turn - RAW))
        elif N_A <= g < len(PART1):
            out.append(("raw", (N_A + turn) % RAW))
        else:
            out.append(("raw", g % RAW))
    return out


TOKEN_ITEMS = [n for n, (kind, t, _) in enumerate(PART1) if kind == "in" and t >= N_FM]
PLACE = places()
BEFORE = [max((o for o in range(g) if PLACE[o] == PLACE[g]), default=None) for g in range(NSLOT)]


def events(first, last):
    soft = {9: "slc_exp", 18: "flip"}
    out, pend = [], []
    for n in range(first, last):
        kind, t, _ = PART1[n]
        out.append(("lin", n))
        out += pend
        pend = [("turn", n)] if kind == "ada" else []
        if n - N_A in soft:
            out.append(("soft", soft[n - N_A]))
        if kind == "in" and 4 <= t < 4 + 2 * NB:
            b = (t - 4) // 2
            out.append(("slc", b, t % 2))
            if t % 2:
                out.append(("blocks", b))
                pend.append(("cmp", b))
        if kind == "in" and t >= N_FM:
            pend.append(("tokens", n))
        if n == 15:
            out += pend
            pend = []
    return out + pend


EVENTS_A, EVENTS_B = events(0, N_A), events(N_A, len(PART1))


def trunk_kernel(nc, xT, wst, par_d, con_d, hot_d, ltri_d, pt_d, cacheA, cacheV, winK, winV, mC, mst, plst, ffst,
                 o_y, o_fm, o_vn, o_st, o_snv, o_wk, o_wv, o_C, o_m, o_pool, o_sC, o_sn, o_sm, o_spool, o_ffp, o_ffs):
    with ExitStack() as ctx:
        def sb(name, shape, dt=F32):
            return ctx.enter_context(nc.sbuf_tensor(name, shape, dt))

        def sem(name):
            return ctx.enter_context(nc.semaphore(name))

        base = -(-nc.sbuf_base // 32) * 32
        arena = sb("arena", [P, 30210])

        def at(name, col, shape, dt=F32):
            return nc.alloc_sbuf_tensor_at(name, shape, dt, offset=base + 4 * col)

        mix = arena[:, 0:4160].rearrange("p (k n) -> p k n", k=KD)
        hR = at("hR", 4160, [P, 2, KD, T], F32R)
        fR = at("fR", 12480, [P, 2, FH, T], F32R)
        big = arena[:, 12480:27464]
        pT = big[:, 0:17 * T].rearrange("p (t n) -> p t n", t=17)
        pages = big[:, 17 * T:17 * T + 2 * HALF * 384].rearrange("p (s j n) -> p s j n", s=2, j=HALF)
        early = [v[:, g * D:(g + 1) * D] for v in (big, arena[:, 4160:12480]) for g in range(EARLY // 2)]
        extra = [arena[:, 4160 + at:4160 + at + D] for at in (1024, 2048, 6144)]
        kwin = big[:, 17 * T:17 * T + NB * S].rearrange("p (b n) -> p b n", b=NB)
        vpages = big[:, 17 * T:17 * T + 2 * NPG * P].rearrange("p (s j n) -> p s j n", s=2, j=NPG)
        x = sb("x", [P, KD, T])
        raw = sb("raw", [P, RAW, KD, P])
        wR = sb("wR", [P, 2, 2, KD, P], F32R)
        vn = sb("vn", [P, ST, 2 * P])
        vm = sb("vm", [P, ST, 4, HD + 1])
        par = sb("par", [P, NPAR])
        con = sb("con", [P, NCON])
        sT = sb("sT", [P, N_FM, NB])
        mod = sb("mod", [P, 48, 9])
        sc = sb("sc", [P, KD, 9])
        sc2 = sb("sc2", [P, KD, 9])
        ab = sb("ab", [P, KD, 9])
        sq = sb("sq", [P, 2, T])
        rstd = sb("rstd", [P, T])
        t8 = sb("t8", [P, NB])
        qs = sb("qs", [P, NB, NH])
        sall = sb("sall", [64, NPG * P + NB])
        scm = sb("scm", [64, P])
        vc = sb("vc", [P, NB, P])
        ptt = sb("ptt", [1, NB * NPG], I32)

        def lay(at, parts):
            out = []
            for n in parts:
                out.append(arena[:, at:at + n])
                at += n
            return out

        tmp, poolA, poolB, sst, modn = lay(0, [1024, 256, 256, 2176, 256])
        poolA = poolA.rearrange("p (k n) -> p k n", k=2)
        poolB = poolB.rearrange("p (k n) -> p k n", k=2)
        modn = modn.rearrange("p (a n) -> p a n", a=2)
        sn, gN, cout, smr, cst = lay(27464, [1152, 96, 260, 214, 1024])
        gN = gN.rearrange("p (i n) -> p i n", i=ST)
        cout = cout.rearrange("p (h n) -> p h n", h=4)
        tmpv = cst
        KEEP = 4160
        ctmp, kN, wj, dt_, wk, hN, r36, mro, hot = lay(KEEP, [1024, 1024, 1280, 1024, 256, 1024, 512, 512, HOT])
        mrow = arena[:, KEEP + 7168:KEEP + 8192].rearrange("p (a n) -> p a n", a=2)
        kN = kN.rearrange("p (t i n) -> p t i n", t=2, i=ST)
        dt_ = dt_.rearrange("p (a n) -> p a n", a=2)
        wj = (wj, arena[:, 0:1280])
        wk = [v.rearrange("p (j n) -> p j n", j=ST) for v in (wk, arena[:, 1280:1536])]
        hN = hN.rearrange("p (i n) -> p i n", i=ST)
        lfo, zro, bro = sq[:, 0, 0:S], sq[:, 1, 0:S], rstd[:, 0:S]
        pr, prT = lay(KEEP, [2048, 2048])
        md, pc = arena[:, KEEP + 5120:KEEP + 6144], arena[:, KEEP + 7168:KEEP + 7168 + 32 * NCP]
        mds = arena[:, KEEP + 8192:KEEP + 8208]
        pr = pr.rearrange("p (a r n) -> p a r n", a=2, r=2)
        prT = prT.rearrange("p (a r n) -> p a r n", a=2, r=2)
        pc = pc.rearrange("p (u n) -> p u n", n=NCP)
        md = md.rearrange("p (t n) -> p t n", t=2)
        mds = mds.rearrange("p (t n) -> p t n", t=2)
        zp = (arena[:, KEEP + 3072:KEEP + 3072 + 15 + S], arena[:, 1400:1400 + 15 + S])
        swin, ptS = lay(12480 + 17 * T + NB * S, [520, (NPG + ST + 3) * 64])
        rank, simp, sel = lay(0, [NSB * NSB, 136, 4 * 34])
        sel = sel[0:64, :].rearrange("p (a n) -> p a n", a=4)
        ltri, tie = arena[:, 3120:4144], arena[:, KEEP + 4096:KEEP + 5120]
        so8, vwin = arena[:, KEEP + 6144:KEEP + 7168], arena[:, KEEP + 4096:KEEP + 5120]
        vwin = vwin.rearrange("p (s c n) -> p s c n", s=2, c=ST)
        ptS = ptS.rearrange("p (c r) -> p c r", r=64)
        yab, sil, ffst_t = lay(0, [2 * T, T, 704])
        ffo_s, ffo_p, zb = lay(23920, [704, 88, 2 * (T + 2)])
        yab = yab.rearrange("p (a n) -> p a n", a=2)
        zb = zb.rearrange("p (a n) -> p a n", a=2)
        ffst_t = ffst_t.rearrange("p (c j b) -> p c j b", c=2 * FC, j=2)
        ffo_s = ffo_s.rearrange("p (c j b) -> p c j b", c=2 * FC, j=2)
        ffo_p = ffo_p.rearrange("p (c j) -> p c j", j=2)

        kct = sb("kct", [P, P])
        pcT = sb("pcT", [P, 2, P])
        vcp = sb("vcp", [P, P])
        pooled = sb("pooled", [P, 2, P])
        rT = sb("rT", [P, ST, 36])
        enm = sb("enm", [P, ST, 4])
        d4 = sb("d4", [P, 8])
        mx = sb("mx", [P, 4, 32])
        sm = sb("sm", [P, 2, 2])
        nmx = sb("nmx", [P, 2, 2])
        fac = sb("fac", [P, 2, 2])
        zs = sb("zs", [P, 2, NB, 16])
        zsum = sb("zsum", [P, 2, NB])
        mout = sb("mout", [4, 2])
        mv = sb("mv", [P, 32])
        qc = sb("qc", [P, 16])
        shh = sb("shh", [P, 16])
        hs8 = sb("hs8", [NB, 4 * HD])
        emos = sb("emos", [P, 2, NB])
        sg = sb("sg", [64, 4])
        ssx = sb("ssx", [64, 16])

        ps = ctx.enter_context(nc.psum_tensor("ps", [P, 8, 512], F32))

        def con_(name, a=0, b=None, rows=P):
            at, n = CON[name]
            return con[0:rows, at + a:at + (n if b is None else b)]

        def par_(name, a=0, b=None, lo=0, hi=P):
            at, n = PAR[name]
            return par[lo:hi, at + a:at + (n if b is None else b)]

        ident = con_("ident")
        hr = [slice(0, HD), slice(HD, P)]

        x_landed, par_landed, con_landed = sem("x_landed"), sem("par_landed"), sem("con_landed")
        raw_landed = [sem(f"raw_landed{i}") for i in range(RAW)]
        early_landed = [sem(f"early_landed{i}") for i in range(EARLY_GROUP[-1] + 1)]
        extra_landed = [sem(f"extra_landed{i}") for i in range(EXTRA)]
        hi_ready, lo_ready = sem("hi_ready"), sem("lo_ready")
        slot_done = sem("slot_done")
        item_done = sem("item_done")
        tokens_done, tokens_evac = sem("tokens_done"), sem("tokens_evac")
        turn_done, turn_evac = sem("turn_done"), sem("turn_evac")
        h_hi, h_lo, hs_hi = sem("h_hi"), sem("h_lo"), sem("hs_hi")
        hot_landed, ltri_landed = sem("hot_landed"), sem("ltri_landed")
        f_ready, f_hi, f_lo = sem("f_ready"), sem("f_hi"), sem("f_lo")
        y_used, zero_done = sem("y_used"), sem("zero_done")
        table_landed = sem("table_landed")
        cache_landed = [sem(f"cache_landed{i}") for i in range(2)]
        vcache_landed = [sem(f"vcache_landed{i}") for i in range(2)]
        win_landed, vwin_landed = sem("win_landed"), [sem(f"vwin_landed{i}") for i in range(2)]
        vmul_ready, vmul_used = sem("vmul_ready"), sem("vmul_used")
        rec_landed = sem("rec_landed")
        ffst_landed = sem("ffst_landed")
        memset_done = sem("memset_done")
        early_out, state_out, end_out = sem("early_out"), sem("state_out"), sem("end_out")
        late_done, late_evac, late_turned = sem("late_done"), sem("late_evac"), sem("late_turned")
        sum_ready, total_done = sem("sum_ready"), sem("total_done")
        sq_ready, sq_used, var_ready, root_ready = sem("sq_ready"), sem("sq_used"), sem("var_ready"), sem("root_ready")
        silu_exp, silu_ready = sem("silu_exp"), sem("silu_ready")
        xn_ready, h_sample = sem("xn_ready"), sem("h_sample")
        evac_act, evac_dve = sem("evac_act"), sem("evac_dve")
        qs_ready = sem("qs_ready")
        slc_scored, slc_evac = sem("slc_scored"), sem("slc_evac")
        comp_done, pooled_ready = sem("comp_done"), sem("pooled_ready")
        blocks_done, blocks_evac = sem("blocks_done"), sem("blocks_evac")
        cmp_scored, cmp_evac, sst_moved = sem("cmp_scored"), sem("cmp_evac"), sem("sst_moved")
        kn_T, sn_T, g_T, kn_evac, sn_evac, g_exp = (sem("kn_T"), sem("sn_T"), sem("g_T"), sem("kn_evac"),
                                                    sem("sn_evac"), sem("g_exp"))
        az_ready, ln_ready, rows_ready, r_T, rt_evac = (sem("az_ready"), sem("ln_ready"), sem("rows_ready"), sem("r_T"),
                                                        sem("rt_evac"))
        act_step = sem("act_step")
        bc_evac = sem("bc_evac")
        bc_done, mscore_done, dmask_done, dt_done, w_done = (sem("bc_done"), sem("mscore_done"), sem("dmask_done"),
                                                             sem("dt_done"), sem("w_done"))
        num_done, num_evac, hT_done, emo_ready, mmix_ready = (sem("num_done"), sem("num_evac"), sem("hT_done"),
                                                              sem("emo_ready"), sem("mmix_ready"))
        rows_moved, saz_ready, sln_ready, sexp_in, sexp_ready, srec_ready = (
            sem("rows_moved"), sem("saz_ready"), sem("sln_ready"), sem("sexp_in"), sem("sexp_ready"), sem("srec_ready"))
        hs_moved, emos_ready, shT_done = sem("hs_moved"), sem("emos_ready"), sem("shT_done")
        gates_ready = sem("gates_ready")
        csc_done, pcx_ready, pcx_exp, pc_ready = sem("csc_done"), sem("pcx_ready"), sem("pcx_exp"), sem("pc_ready")
        qk_done, mx_ready, p_exp, p_ready, t_done = sem("qk_done"), sem("mx_ready"), sem("p_exp"), sem("p_ready"), sem("t_done")
        pt_act, pt_dve, pv_done, o_evac = sem("pt_act"), sem("pt_dve"), sem("pv_done"), sem("o_evac")
        cout_ready = sem("cout_ready")
        pool_ready, pool_mm, side_mix = sem("pool_ready"), sem("pool_mm"), sem("side_mix")
        snew_done, wsc_done, wsc_evac, sgate_moved, sg_exp = (sem("snew_done"), sem("wsc_done"), sem("wsc_evac"),
                                                                       sem("sgate_moved"), sem("sg_exp"))
        w_moved = [sem(f"w_moved{i}") for i in range(4)]
        sx_in, sx_out, imp_in, imp_done, sp_ready, spT_done, spT_evac = (
            sem("sx_in"), sem("sx_out"), sem("imp_in"), sem("imp_done"), sem("sp_ready"), sem("spT_done"), sem("spT_evac"))
        spv_done, soT_done, mix_ready = sem("spv_done"), sem("soT_done"), sem("mix_ready")
        y_ready, silu_in, silu_out, x_ready, out_ready = (sem("y_ready"), sem("silu_in"), sem("silu_out"), sem("x_ready"),
                                                          sem("out_ready"))
        dve_step, pool_step = sem("dve_step"), sem("pool_step")

        def item_ready(eng, n):
            c = CHUNK0[n + 1]
            if c % KD == 0:
                eng.wait_ge(slot_done, c // KD)
            else:
                eng.wait_ge(item_done, sum(CHUNK0[i + 1] % KD != 0 for i in range(n + 1)))

        def raw_slot(g):
            kind, i = PLACE[g]
            return raw[:, i] if kind == "raw" else (early if kind == "early" else extra)[i].rearrange("p (k n) -> p k n", k=KD)

        def landed(g):
            kind, i = PLACE[g]
            if kind == "early":
                return early_landed[EARLY_GROUP[i]]
            return {"raw": raw_landed, "extra": extra_landed}[kind][i]

        def raw_wait(eng, g):
            kind, i = PLACE[g]
            shared = EARLY_GROUP.count(EARLY_GROUP[i]) if kind == "early" else 1
            eng.wait_ge(landed(g), 16 * shared * PLACE[:g + 1].count(PLACE[g]))

        def windows_moved(eng):
            for done in w_moved:
                eng.wait_ge(done, 16 * NB // 4)

        def turned(n, i):
            return modn[0:9, i % 2, :] if n < 16 else sq[0:9, i % 2, 0:P]

        NE = 2 * NB
        UNITS = [(hh, i) for hh in range(NH) for i in range(ST)]
        OFF = [0, 512, 896, 1152]

        block = ctx.enter_context(nc.Block())

        @block.sync
        def _(sp):
            def load_slot(g):
                old = BEFORE[g]
                if old in SPLIT:
                    sp.wait_ge(lo_ready, SPLIT.index(old) + 1)
                elif old is not None:
                    sp.wait_ge(slot_done, old + 1)
                sp.dma_start(raw_slot(g), wst[g, :, :].rearrange("p (k n) -> p k n", k=KD)).then_inc(landed(g), 16)

            page_regs = [sp.alloc_register(f"page{j}") for j in range(HALF)]

            def page_numbers(i):
                sp.load(page_regs, ptt[0:1, i * HALF:(i + 1) * HALF])
                return [sp.snap(reg, min_val=0, max_val=NPHYS - 1) for reg in page_regs]

            def load_half(i):
                b, s = i // 2, i % 2
                if i >= 2:
                    sp.wait_ge(comp_done, i - 1)
                    sp.wait_ge(slc_scored, i - 1)
                for j, pg in enumerate(page_numbers(i)):
                    sp.dma_start(pages[:, s, j, :], cacheA[bass.ds(pg, 1), :, :].rearrange("a p n -> (a p) n"))\
                      .then_inc(cache_landed[s], 16)

            for k in range(KD):
                sp.dma_start(x[:, k, :], xT[:, k, :]).then_inc(x_landed, 16)
                if k == 1:
                    sp.dma_start(par[:, :], par_d).then_inc(par_landed, 16)
                    sp.dma_start(con[:, :], con_d).then_inc(con_landed, 16)
            sp.wait_ge(table_landed, 16)
            half = 0
            for g in range(N_A + RAW):
                load_slot(g)
                if g in (18, 19) or (half >= 2 and half < 2 * NB and g >= half + 22):
                    load_half(half)
                    half += 1

            sp.wait_ge(comp_done, 2 * NB)
            sp.wait_ge(slc_scored, 2 * NB)
            for b in range(0, NB, 4):
                sp.dma_start(kwin[:, b:b + 4, :], winK[:, b:b + 4, :]).then_inc(win_landed, 16)
            sp.wait_ge(evac_act, N_A)
            sp.dma_start(hot[0:4, :], hot_d).then_inc(hot_landed, 16)
            sp.wait_ge(sn_evac, 1)
            sp.dma_start(cst[:, :], mC).then_inc(rec_landed, 16)
            sp.dma_start(zs[:, :, :, 0:15], plst).then_inc(rec_landed, 16)
            for b in range(NB):
                sp.dma_start(sg[b * 8:b * 8 + 8, 0:3], sn[b:b + 1, 768 + 64:768 + 88].rearrange("p (h r) -> p h r", h=8))\
                  .then_inc(sgate_moved, 16)
            for e in range(4):
                for hh in range(4):
                    r = slice(e * 32 + hh * 8, e * 32 + hh * 8 + 8)
                    sp.dma_start(smr[r, 0:128].rearrange("p (t d) -> p t d", t=2),
                                 sn[0:8, 0:512].rearrange("p (t h d) -> p t h d", t=2, h=4)[:, :, hh, :]).then_inc(rows_moved, 16)
                    sp.dma_start(smr[r, 128:144], sn[0:8, 512 + hh * 64 + e * 16:512 + hh * 64 + e * 16 + 16])\
                      .then_inc(rows_moved, 16)
                    sp.dma_start(smr[r, 144:146], sn[0:8, 768 + hh:768 + hh + 33:32], allow_slow_non_contiguous=True)\
                      .then_inc(rows_moved, 16)

            def load_values(b):
                for half in range(2):
                    for j, pg in enumerate(page_numbers(2 * b + half)):
                        sp.dma_start(vpages[:, b % 2, half * HALF + j, :],
                                     cacheV[bass.ds(pg, 1), :, :].rearrange("a p n -> (a p) n")).then_inc(vcache_landed[b % 2], 16)

            def load_window(b):
                sp.dma_start(vwin[:, b % 2], winV[:, b]).then_inc(vwin_landed[b % 2], 16)

            windows_moved(sp)
            sp.dma_start(ltri[0:64, :], ltri_d).then_inc(ltri_landed, 16)
            sp.wait_ge(wsc_done, NB)
            load_values(0)
            load_values(1)
            sp.dma_start(o_fm, pT[:, T_KC:T_MK, 0:S]).then_inc(early_out, 16)
            sp.dma_start(o_vn, vn[:, :, :]).then_inc(early_out, 16)
            sp.dma_start(o_st, sT[:, :, :]).then_inc(early_out, 16)
            sp.dma_start(o_snv, sn[0:NB, 7 * P:9 * P]).then_inc(early_out, 16)
            sp.dma_start(o_pool, pT[:, T_PU:T_PU + 2, S - 15:S]).then_inc(early_out, 16)
            sp.wait_ge(mmix_ready, 1)
            sp.dma_start(o_C, cout[0:HD, :, :]).then_inc(state_out, 16)
            sp.dma_start(o_m, mout[0:4, 0:1]).then_inc(state_out, 16)
            sp.wait_ge(sx_in, 3)
            load_window(0)
            load_window(1)
            sp.wait_ge(srec_ready, 1)
            for e in range(4):
                for hh in range(4):
                    sp.dma_start(hs8[0:8, hh * 64 + e * 16:hh * 64 + e * 16 + 16], shh[e * 32 + hh * 8:e * 32 + hh * 8 + 8, :])\
                      .then_inc(hs_moved, 16)
            sp.dma_start(o_sC, cst[:, :]).then_inc(state_out, 16)
            sp.dma_start(o_sn, smr[0:32, 146:210]).then_inc(state_out, 16)
            sp.dma_start(o_sm, mv[0:32, 3:4]).then_inc(state_out, 16)
            sp.wait_ge(pool_ready, 1)
            sp.dma_start(o_spool, zs[:, :, :, 1:16]).then_inc(state_out, 16)
            sp.wait_ge(side_mix, 1)
            sp.dma_start(o_wk, winK[:, :, 1:512]).then_inc(state_out, 16)
            sp.dma_start(o_wv, winV).then_inc(state_out, 16)
            for b in range(2, NB):
                sp.wait_ge(spv_done, b - 1)
                load_values(b)
                load_window(b)
            g0 = len(PART1) + RAW
            for g in range(g0, g0 + 6):
                load_slot(g)
                if g == g0:
                    sp.wait_ge(early_out, 16 * 5)
                    sp.wait_ge(mix_ready, 1)
                    for late in range(NMAIN, NSLOT):
                        load_slot(late)
            sp.wait_ge(h_hi, 2 * KD)
            sp.wait_ge(h_lo, 2 * KD)
            sp.dma_start(ffst_t, ffst).then_inc(ffst_landed, 16)
            g0 += 6
            rounds = (NMAIN - g0) // RAW
            with sp.Fori(0, rounds) as q:
                for s in range(RAW):
                    sp.wait_ge(lo_ready, q * RAW + (SPLIT.index(g0 + s - RAW) + 1))
                    sp.dma_start(raw[:, (g0 + s) % RAW, :, :],
                                 wst[bass.ds(q * RAW + (g0 + s), 1), :, :].rearrange("a p (k n) -> (a p) k n", k=KD))\
                      .then_inc(raw_landed[(g0 + s) % RAW], 16)
            for g in range(g0 + rounds * RAW, NMAIN):
                load_slot(g)
            sp.wait_ge(f_lo, FC)
            sp.dma_start(o_ffp, ffo_p).then_inc(end_out, 16)
            sp.dma_start(o_ffs, ffo_s).then_inc(end_out, 16)
            for k in range(KD):
                sp.wait_ge(out_ready, k + 1)
                sp.dma_start(o_y[:, k, :], x[:, k, :]).then_inc(end_out, 16)
            sp.wait_ge(early_out, 16 * 5)
            sp.wait_ge(state_out, 16 * 8)
            sp.wait_ge(end_out, 16 * 10)

        @block.gpsimd
        def _(pool):
            G = nc.gpsimd
            pool.dma_start(ptt[:, :], pt_d).then_inc(table_landed, 16)
            nc.gpsimd.memset(qs[:, :, :], 0.0).then_inc(memset_done, 1)
            nc.gpsimd.memset(vm[:, :, :, HD:HD + 1], 1.0).then_inc(memset_done, 1)

            def value_products(h):
                b, s = h // 2, h % 2
                pool.wait_ge(cache_landed[s], 16 * HALF * (b + 1))
                for w in range(2):
                    if h or w:
                        pool.wait_ge(vmul_used, 2 * h + w)
                    nc.gpsimd.tensor_tensor(tmpv.rearrange("p (a n j) -> p a n j", a=HALF, j=16),
                                            pages[:, s, :, 2 * P:3 * P].rearrange("p a (n j) -> p a n j", j=16),
                                            par_("wpos", 32 + 16 * w, 48 + 16 * w).unsqueeze(1).unsqueeze(1).broadcast_to([P, HALF, 8, 16]),
                                            ALU.mult).then_inc(vmul_ready, 1)

            chain = [0]

            def link(ins):
                chain[0] += 1
                ins.then_inc(pool_step, 1)
                pool.wait_ge(pool_step, chain[0])

            def pool_heads():
                for t in range(2):
                    link(G.memset(zp[0][:, 0:15], 0.0))
                    buf = [zp[0][:, :], zp[1][:, :]]
                    link(G.tensor_copy(zp[0][:, 15:15 + S], pT[:, T_PU + t, 0:S]))
                    lo, cur = 0, 0
                    for w in (1, 2, 4, 8)[:2 * t + 2]:
                        lo += w
                        top = w == (2, 8)[t]
                        if top:
                            link(G.tensor_copy(md[hr[0], t, :], buf[cur][hr[0], 15:15 + S]))
                        r = slice(HD, P) if top else slice(0, P)
                        link(G.tensor_tensor(buf[1 - cur][r, lo:15 + S], buf[cur][r, lo:15 + S], buf[cur][r, lo - w:15 + S - w], ALU.add))
                        cur = 1 - cur
                    link(G.tensor_copy(md[hr[1], t, :], buf[cur][hr[1], 15:15 + S]))
                    link(G.tensor_tensor(zp[1][:, 15:31], md[:, t, 0:16], con_("rcnt", 16 * t, 16 * t + 16), ALU.mult))
                    link(G.tensor_tensor(md[:, t, 0:16], zp[1][:, 15:31], pT[:, T_PU + t, 0:16], ALU.subtract))
                    link(G.tensor_scalar(md[:, t, 16:S], md[:, t, 16:S], con_("rw", t, t + 1), None, ALU.mult))
                    link(G.tensor_tensor(md[:, t, 16:S], md[:, t, 16:S], pT[:, T_PU + t, 16:S], ALU.subtract))
                    link(G.tensor_copy(zs[:, t, :, 15], sT[:, T_PU + t, :]))
                    for g in range(2):
                        w = (2, 4, 8, 16)[2 * t + g]
                        link(G.tensor_tensor(zsum[hr[g], t, :], zs[hr[g], t, :, 15], zs[hr[g], t, :, 14], ALU.add))
                        for c in range(14 - 1, 15 - w, -1):
                            link(G.tensor_tensor(zsum[hr[g], t, :], zsum[hr[g], t, :], zs[hr[g], t, :, c], ALU.add))
                    link(G.tensor_scalar(zsum[:, t, :], zsum[:, t, :], con_("rw", t, t + 1), None, ALU.mult))
                    last = G.tensor_tensor(mds[:, t, :], zsum[:, t, :], sT[:, T_PU + t, :], ALU.subtract)
                last.then_inc(pool_ready, 1)

            pool.wait_ge(par_landed, 16)
            value_products(0)
            half = 1
            for i, g in enumerate(SPLIT):
                if i == N_IN:
                    pool.wait_ge(con_landed, 16)
                    pool.wait_ge(rec_landed, 32)
                    pool.wait_ge(mmix_ready, 1)
                    pool_heads()
                if i == 3 or (7 <= i < N_IN):
                    value_products(half)
                    half += 1
                pool.wait_ge(hi_ready, i + 1)
                nc.gpsimd.tensor_tensor(wR[:, i % 2, 1, :, :], raw[:, g % RAW, :, :], wR[:, i % 2, 0, :, :].bitcast(F32),
                                        ALU.subtract).then_inc(lo_ready, 1)

        @block.tensor
        def _(pe):
            mm = nc.tensor.matmul

            def norm_sum(k):
                pe.wait_ge(sq_ready, k + 1)
                mm(ps[:, 4, 0:TH], con_("mean"), sq[:, k % 2, 0:TH], start=(k == 0), stop=(k == KD - 1))
                mm(ps[:, 5, 0:TH], con_("mean"), sq[:, k % 2, TH:T], start=(k == 0), stop=(k == KD - 1)).then_inc(sq_used, 1)

            def norm_total(n):
                pe.wait_ge(sum_ready, n * (KD - 1))
                mm(ps[:, 4, 0:TH], con_("mean"), rstd[:, 0:TH], start=True, stop=True)
                mm(ps[:, 5, 0:TH], con_("mean"), rstd[:, TH:T], start=True, stop=True).then_inc(total_done, 1)

            PASSES = [(0, 0), (0, 1), (1, 0)]

            def product(n):
                kind, t, chunks = ITEMS[n]
                a = 2 * (n % 2)
                if kind == "ada":
                    raw_wait(pe, n)
                    for k in range(KD):
                        last = mm(ps[0:9, a, 0:P], sc[:, k, :], raw_slot(n)[:, k, :], start=(k == 0), stop=(k == KD - 1))
                    last.then_inc(slot_done, 1)
                    return
                for j in range(chunks):
                    g, k = (CHUNK0[n] + j) // KD, (CHUNK0[n] + j) % KD
                    i = SPLIT.index(g)
                    if j == 0 or k == 0:
                        pe.wait_ge(lo_ready, i + 1)
                    if (kind, t) in (("in", 0), ("out", 0), ("up", 0)):
                        v = ("in", "out", "up").index(kind)
                        pe.wait_ge(h_hi, v * KD + j + 1)
                        pe.wait_ge(h_lo, v * KD + j + 1)
                    if kind in ("down0", "down1") and t == 0:
                        pe.wait_ge(f_lo, FH * (kind == "down1") + j + 1)
                    src = fR if kind[:4] == "down" else hR
                    for q, (wp, hp) in enumerate(PASSES):
                        for half in range(2):
                            last = mm(ps[:, a + half, 0:TH], wR[:, i % 2, wp, k, :], src[:, hp, j, half * TH:(half + 1) * TH],
                                      start=(j == 0 and q == 0), stop=(j == chunks - 1 and q == 2))
                    if k == KD - 1:
                        last.then_inc(slot_done, 1)
                    elif j == chunks - 1:
                        last.then_inc(item_done, 1)

            pe.wait_ge(con_landed, 16)
            pe.wait_ge(par_landed, 16)
            for k in range(KD):
                norm_sum(k)
            pe.wait_ge(silu_ready, 1)
            count = {"slc": 0, "turn": 0}

            def step(ev):
                if ev[0] == "lin":
                    n = ev[1]
                    if n >= 2:
                        pe.wait_ge(evac_act, n - 1)
                        if n - 2 in TOKEN_ITEMS:
                            pe.wait_ge(tokens_evac, TOKEN_ITEMS.index(n - 2) + 1)
                        if PART1[n - 2][0] == "ada" and PART1[n][0] == "in":
                            pe.wait_ge(turn_evac, sum(i[0] == "ada" for i in PART1[:n - 1]))
                    if n == N_A + 1:
                        pe.wait_ge(pcx_ready, 1)
                        pe.wait_ge(cout_ready, 1)
                    product(n)
                elif ev[0] == "turn":
                    n = ev[1]
                    pe.wait_ge(evac_act, n + 1)
                    if count["turn"] >= 2:
                        pe.wait_ge(turn_evac, count["turn"] - 1)
                    nc.tensor.transpose(ps[:, 2 * (n % 2) + 1, 0:9], turned(n, count["turn"]), ident[0:9, 0:9]).then_inc(turn_done, 1)
                    count["turn"] += 1
                elif ev[0] == "tokens":
                    n = ev[1]
                    pe.wait_ge(evac_act, n + 1)
                    v = sq[:, n % 2, :]
                    for i in range(ST):
                        nc.tensor.transpose(ps[:, 2 * (n % 2), i * P:(i + 1) * P], v[:, i * P:(i + 1) * P], ident)
                    nc.tensor.transpose(ps[0:NB, 2 * (n % 2) + 1, 0:P], v[:, S:T], ident).then_inc(tokens_done, 1)
                elif ev[0] == "slc":
                    _, b, s = ev
                    pe.wait_ge(cache_landed[s], 16 * HALF * (b + 1))
                    pe.wait_ge(qs_ready, 1)
                    if count["slc"]:
                        pe.wait_ge(slc_evac, count["slc"])
                    count["slc"] += 1
                    for j in range(2):
                        last = mm(ps[0:NH, 6 + j, :].rearrange("p (j n) -> p j n", j=4), qs[:, b, :],
                                  pages[:, s, 4 * j:4 * j + 4, P:2 * P], start=True, stop=True)
                    last.then_inc(slc_scored, 1)
                elif ev == ("soft", "flip"):
                    pe.wait_ge(mmix_ready, 1)
                    pe.wait_ge(sp_ready, 1)
                    for c in range(NPG):
                        nc.tensor.transpose(ps[:, 4 + c // 8, (c % 8) * 64:(c % 8 + 1) * 64], sall[:, c * P:(c + 1) * P],
                                            ident[0:64, 0:64])
                    for c in range(ST):
                        nc.tensor.transpose(ps[:, 6, c * 64:(c + 1) * 64], swin[0:64, c * P:(c + 1) * P], ident[0:64, 0:64])
                    nc.tensor.transpose(ps[0:NCB, 7, 0:64], scm[:, 0:NCB], ident[0:64, 0:64])
                    nc.tensor.transpose(ps[0:NB, 7, 64:128], sall[:, NPG * P:NPG * P + NB], ident[0:64, 0:64])
                    nc.tensor.transpose(ps[0:NB, 7, 128:192], swin[0:64, S:S + NB], ident[0:64, 0:64]).then_inc(spT_done, 1)
                elif ev[0] == "blocks":
                    b = ev[1]
                    pe.wait_ge(pooled_ready, b + 1)
                    if b:
                        pe.wait_ge(blocks_evac, b)
                        pe.wait_ge(cmp_evac, b)
                    mm(ps[:, 4, 0:NCB], par_("cw", 0, P), pooled[:, 0, 0:NCB], start=True, stop=True)
                    mm(ps[0:NCB, 5, 0:P], pooled[:, 1, 0:NCB], par_("cw", P, 2 * P), start=True, stop=False)
                    mm(ps[0:NCB, 5, 0:P], con_("ones", 0, NCB, 1), par_("bv", hi=1), start=False, stop=True)\
                        .then_inc(blocks_done, 1)
                elif ev[0] == "cmp":
                    b = ev[1]
                    pe.wait_ge(blocks_evac, b + 1)
                    mm(ps[0:NH, 4, 0:NCB], qs[:, b, :], kct[:, 0:NCB], start=True, stop=True).then_inc(cmp_scored, 1)

            for ev in EVENTS_A:
                step(ev)

            pe.wait_ge(evac_act, N_A)
            pe.wait_ge(tokens_evac, len(TOKEN_ITEMS))
            pe.wait_ge(turn_evac, 16)
            pe.wait_ge(blocks_evac, NB)
            pe.wait_ge(cmp_evac, NB)
            pe.wait_ge(slc_evac, NE)
            for t in range(2):
                for i in range(ST):
                    last = nc.tensor.transpose(ps[:, 4 + t, i * P:(i + 1) * P], pT[:, T_MK + t, i * P:(i + 1) * P], ident)
            last.then_inc(kn_T, 1)
            for c, t in enumerate([T_MQ, T_MQ + 1, T_MK, T_MK + 1, T_G]):
                last = nc.tensor.transpose(ps[0:NB, c // 4, (c % 4) * P:(c % 4 + 1) * P], sT[:, t, :], ident)
            last.then_inc(sn_T, 1)
            for i in range(ST):
                last = nc.tensor.transpose(ps[:, 3, i * P:(i + 1) * P], pT[:, T_G, i * P:(i + 1) * P], ident)
            last.then_inc(g_T, 1)
            pe.wait_ge(pooled_ready, NB + 1)
            mm(ps[:, 6, 0:NCP], par_("cw", 0, P), pooled[:, 0, 0:NCP], start=True, stop=True)
            mm(ps[0:NCP, 6, P:2 * P], pooled[:, 1, 0:NCP], par_("cw", P, 2 * P), start=True, stop=False)
            mm(ps[0:NCP, 6, P:2 * P], con_("ones", 0, NCP, 1), par_("bv", hi=1), start=False, stop=True).then_inc(blocks_done, 1)
            def window_scores(b):
                if b == 0:
                    pe.wait_ge(win_landed, 32)
                else:
                    pe.wait_ge(wsc_evac, b)
                mm(ps[0:NH, 2, :], qs[:, b, :], kwin[:, b, :], start=True, stop=True).then_inc(wsc_done, 1)

            pe.wait_ge(sn_evac, 1)
            pe.wait_ge(blocks_evac, NB + 1)
            for c in range(4 * ST):
                if c % 4 == 0 and c // 4 < WINDOWS_FIRST:
                    window_scores(c // 4)
                r, i = c // ST, c % ST
                at = (c % 8) * 2 * NCP
                last = mm(ps[:, r // 2, at:at + 2 * NCP], pT[:, r, i * P:(i + 1) * P], kct[:, 64:64 + 2 * NCP],
                          start=True, stop=True)
            last.then_inc(csc_done, 1)
            pe.wait_ge(rows_ready, 1)
            pe.wait_ge(kn_evac, 1)
            for i in range(ST):
                last = nc.tensor.transpose(ps[:, 5, i * 36:(i + 1) * 36], r36[0:36, i * P:(i + 1) * P], ident[0:36, 0:36])
            last.then_inc(r_T, 1)

            pe.wait_ge(kn_evac, 1)
            pe.wait_ge(g_exp, 1)
            pe.wait_ge(blocks_evac, NB + 1)
            pe.wait_ge(hot_landed, 16)
            mm(ps[0:64, 6, 384:384 + NB], qs[:, :, :], sT[:, T_KS, :], start=True, stop=True)
            mm(ps[0:64, 6, 384 + NB:384 + 2 * NB], qs[:, :, :], sT[:, T_KW, :], start=True, stop=True).then_inc(snew_done, 1)

            def row_broadcast(hh):
                if hh:
                    pe.wait_ge(bc_evac, hh)
                mm(ps[:, 7, :], hot[0:4, hh * P:(hh + 1) * P], mro[0:4, :], start=True, stop=True).then_inc(bc_done, 1)

            def head_sums(hh, part):
                if part == 0:
                    pe.wait_ge(w_done, 4 * hh + 4)
                    if hh:
                        pe.wait_ge(num_evac, hh)
                for i in ((0, 1), (2,), (3,), ())[part]:
                    for j in range(i + 1):
                        at = OFF[j] + (i - j) * P
                        mm(ps[:, 6, i * 65:i * 65 + 65], wj[hh % 2][:, at:at + P], vm[:, j, hh, :], start=(j == 0), stop=(j == i))
                if part == 3:
                    for j in range(ST):
                        last = mm(ps[0:HD, 3, hh * 65:hh * 65 + 65], wk[hh % 2][:, j, :], vm[:, j, hh, :], start=(j == 0),
                                  stop=(j == ST - 1))
                    last.then_inc(num_done, 1)

            row_broadcast(0)
            pe.wait_ge(rt_evac, 1)
            for q in range(21):
                if q < 16:
                    hh, j = q // 4, q % 4
                    rows, t = hr[hh % 2], hh // 2
                    if q >= 2:
                        pe.wait_ge(w_done, q - 1)
                    mm(ps[:, 4 + q % 2, 0:S - j * P], pT[rows, T_MK + t, j * P:(j + 1) * P], pT[rows, T_MQ + t, j * P:S],
                       start=True, stop=True).then_inc(mscore_done, 1)
                    if j == 1 and hh < 3:
                        row_broadcast(hh + 1)
                    if WINDOWS_FIRST + q < NB:
                        window_scores(WINDOWS_FIRST + q)
                if q == 14:
                    pe.wait_ge(imp_in, 1)
                    pe.wait_ge(bc_evac, 4)
                    mm(ps[0:64, 7, 0:NCB], con_("grp", rows=64), scm[:, 0:NCB], start=True, stop=True).then_inc(imp_done, 1)
                if q >= 5:
                    head_sums((q - 5) // 4, (q - 5) % 4)
            pe.wait_ge(num_evac, 4)
            for t in range(2):
                for i in range(ST):
                    last = nc.tensor.transpose(ps[:, 4 + t, i * P:(i + 1) * P], hN[:, i, t * P:(t + 1) * P], ident)
            last.then_inc(hT_done, 1)

            pe.wait_ge(wsc_evac, NB)
            for ev in EVENTS_B:
                step(ev)
            pe.wait_ge(evac_act, len(PART1))
            pe.wait_ge(turn_evac, 40)
            pe.wait_ge(spT_evac, 1)
            pe.wait_ge(pool_ready, 1)
            for t in range(2):
                mm(ps[:, 4 + t, :], par_("pw", t * P, (t + 1) * P), md[:, t, :], start=True, stop=True)
                last = mm(ps[:, 6, t * NB:(t + 1) * NB], par_("pw", t * P, (t + 1) * P), mds[:, t, :], start=True, stop=True)
            last.then_inc(pool_mm, 1)

            def scores(u):
                hh, i = UNITS[u]
                rows, n = hr[hh // G], (i + 1) * P
                if u >= 2:
                    pe.wait_ge(p_exp, u - 1)
                for r, t in enumerate((T_KS, T_KW)):
                    last = mm(ps[:, 2 * (u % 2) + r, 0:n], pT[rows, hh % G, i * P:(i + 1) * P], pT[rows, t, 0:n],
                              start=True, stop=True)
                last.then_inc(qk_done, 1)

            def flip(u):
                hh, i = UNITS[u]
                pe.wait_ge(p_ready, u + 1)
                if u == 0:
                    pe.wait_ge(pc_ready, 1)
                    pe.wait_ge(side_mix, 1)
                else:
                    pe.wait_ge(pt_act, u)
                    pe.wait_ge(pt_dve, u)
                for r in range(2):
                    for c in range(i + 1):
                        nc.tensor.transpose(ps[:, 4 + r, c * P:(c + 1) * P], pr[:, u % 2, r, c * P:(c + 1) * P], ident)
                nc.tensor.transpose(ps[0:NCP, 6, 0:P], pc[:, u, 0:NCP], ident).then_inc(t_done, 1)

            def values(u):
                hh, i = UNITS[u]
                rows = hr[hh // G]
                pe.wait_ge(pt_act, u + 1)
                pe.wait_ge(pt_dve, u + 1)
                if u:
                    pe.wait_ge(o_evac, u)
                if i == SAMPLE_AT:
                    sample_values(u // ST)
                out = ps[rows, 7, 0:P]
                for r in range(2):
                    for c in range(i + 1):
                        mm(out, vn[:, c, r * P + rows.start:r * P + rows.stop], prT[:, u % 2, r, c * P:(c + 1) * P],
                           start=(r == 0 and c == 0), stop=False)
                mm(out, vcp[0:NCP, rows], pcT[0:NCP, u % 2, :], start=False, stop=True).then_inc(pv_done, 1)

            def sample_values(b):
                pe.wait_ge(vcache_landed[b % 2], 16 * NPG * (b // 2 + 1))
                pe.wait_ge(vwin_landed[b % 2], 16 * (b // 2 + 1))
                cols = slice(b * 8, (b + 1) * 8)
                parts = [(ptS[:, c, cols], vpages[:, b % 2, c, :]) for c in range(NPG)]
                parts += [(ptS[:, NPG + c, cols], vwin[:, b % 2, c, :]) for c in range(ST)]
                parts += [(ptS[0:NCB, 20, cols], vc[0:NCB, b, :]), (ptS[0:NB, 21, cols], sn[0:NB, 7 * P:8 * P]),
                          (ptS[0:NB, 22, cols], sn[0:NB, 8 * P:9 * P])]
                for c, (weights, vals) in enumerate(parts):
                    last = mm(ps[0:NH, 7, P:2 * P], weights, vals, start=(c == 0), stop=(c == len(parts) - 1))
                last.then_inc(spv_done, 1)

            NU = len(UNITS)
            for u in range(NU + 2):
                if u < NU:
                    scores(u)
                if 1 <= u <= NU:
                    flip(u - 1)
                if u >= 2:
                    values(u - 2)
            pe.wait_ge(hs_moved, 16 * 16)
            pe.wait_ge(o_evac, NU)
            for t in range(2):
                last = nc.tensor.transpose(ps[:, 7, t * NB:(t + 1) * NB], hs8[0:NB, t * P:(t + 1) * P], ident[0:NB, 0:NB])
            last.then_inc(shT_done, 1)
            for b in range(NB):
                last = nc.tensor.transpose(ps[:, 6, b * 8:(b + 1) * 8], so8[0:NH, b * P:(b + 1) * P], ident[0:NH, 0:NH])
            last.then_inc(soT_done, 1)

            pe.wait_ge(mix_ready, 1)
            for m, (kind, t, _) in enumerate(PART2):
                if m >= 2:
                    pe.wait_ge(evac_dve, m - 1)
                product(len(PART1) + m)
                if kind == "out" and t == KD - 1:
                    norm_total(1)
                    for i in range(len(LATE)):
                        raw_wait(pe, NMAIN + i)
                        for k in range(KD):
                            last = mm(ps[0:9, 6 + i // 4, (i % 4) * P:(i % 4 + 1) * P], sc[:, k, :], raw_slot(NMAIN + i)[:, k, :],
                                      start=(k == 0), stop=(k == KD - 1))
                    last.then_inc(late_done, 1)
                if kind == "up" and t == FC:
                    pe.wait_ge(late_evac, 1)
                    for i in range(len(LATE)):
                        last = nc.tensor.transpose(ps[:, 6, i * 9:(i + 1) * 9], sall[0:9, i * P:(i + 1) * P], ident[0:9, 0:9])
                    last.then_inc(late_turned, 1)
            norm_total(2)

        @block.scalar
        def _(act):
            A = nc.scalar.activation
            chain = [0]

            def link(ins):
                chain[0] += 1
                ins.then_inc(act_step, 1)
                act.wait_ge(act_step, chain[0])

            def load_weights(g):
                act.dma_start(raw_slot(g), wst[g, :, :].rearrange("p (k n) -> p k n", k=KD)).then_inc(landed(g), 16)

            def squares(n, k):
                if n == 0 and k >= 2:
                    act.wait_ge(sq_used, k - 1)
                if n and k >= 3:
                    act.wait_ge(sum_ready, (n - 1) * (KD - 1) + k - 2)
                A(rstd[:, :] if n and k == 0 else sq[:, k % 2, :], x[:, k, :], ACT.Square).then_inc(sq_ready, 1)

            def hi(i):
                g = SPLIT[i]
                raw_wait(act, g)
                if i >= 2:
                    act.wait_ge(slot_done, SPLIT[i - 2] + 1)
                A(wR[:, i % 2, 0, :, :], raw[:, g % RAW, :, :], ACT.Identity).then_inc(hi_ready, 1)

            def normed(n, shift):
                act.wait_ge(h_sample, n + 1)
                A(hR[:, 0, :, S:T], sc2[:, :, 0:NB], ACT.Identity).then_inc(hs_hi, 1)
                for k in range(KD):
                    act.wait_ge(xn_ready, n * KD + k + 1)
                    A(hR[:, 0, k, 0:S], sq[:, k % 2, 0:S], ACT.Identity, bias=mod[:, shift + k, 0:1]).then_inc(h_hi, 1)

            act.wait_ge(par_landed, 16)
            A(sc2[:, :, :], par_("c").rearrange("p (k n) -> p k n", k=KD), ACT.Exp, scale=-1.0).then_inc(silu_exp, 1)
            for k in range(KD):
                act.wait_ge(x_landed, 16 * KD)
                squares(0, k)
            act.wait_ge(var_ready, 1)
            A(rstd[:, :], rstd[:, :], ACT.Sqrt).then_inc(root_ready, 1)
            count = {"slc": 0, "ada": 0, "turn": 0}

            def step(ev):
                if ev[0] == "turn":
                    act.wait_ge(turn_done, count["turn"] + 1)
                    t = PART1[ev[1]][1]
                    A(mod[:, t, :], ps[:, 2 * (ev[1] % 2) + 1, 0:9], ACT.Identity, bias=par_("ada_b", t, t + 1)).then_inc(turn_evac, 1)
                    count["turn"] += 1
                    if t == 15:
                        hi(0)
                        act.wait_ge(turn_evac, 16)
                        normed(0, 0)
                    return
                if ev[0] == "lin":
                    n = ev[1]
                    kind, t, _ = PART1[n]
                    if kind == "in" and n < SPLIT[-1] and SPLIT.index(n) + 1 < N_IN:
                        hi(SPLIT.index(n) + 1)
                    item_ready(act, n)
                    if kind == "ada":
                        if n >= N_A and n in BEFORE:
                            load_weights(BEFORE.index(n))
                        if count["ada"] >= 2:
                            act.wait_ge(turn_done, count["ada"] - 1)
                        A(turned(n, count["ada"]), ps[0:9, 2 * (n % 2), 0:P], ACT.Identity).then_inc(evac_act, 1)
                        count["ada"] += 1
                        return
                    scale = SCALE if T_MK <= t < T_MK + 2 else 1.0
                    two = ps[:, 2 * (n % 2):2 * (n % 2) + 2, 0:TH]
                    if t < N_FM:
                        A(sT[:, t, :], two[:, 1, TH - NB:TH], ACT.Identity, scale=scale)
                        A(pT[:, t, :].rearrange("p (a n) -> p a n", a=2), two, ACT.Identity, scale=scale).then_inc(evac_act, 1)
                    else:
                        if TOKEN_ITEMS.index(n) >= 2:
                            act.wait_ge(tokens_done, TOKEN_ITEMS.index(n) - 1)
                        A(sq[:, n % 2, :].rearrange("p (a n) -> p a n", a=2), two, ACT.Identity).then_inc(evac_act, 1)
                    if t == 3:
                        act.wait_ge(evac_act, n + 1)
                        act.wait_ge(memset_done, 2)
                        for hh in range(NH):
                            rows = hr[hh // G]
                            last = A(qs[rows, :, hh], sT[rows, hh % G, :], ACT.Identity)
                        last.then_inc(qs_ready, 1)
                elif ev[0] == "tokens":
                    n = ev[1]
                    t = PART1[n][1]
                    act.wait_ge(tokens_done, TOKEN_ITEMS.index(n) + 1)
                    c = {T_VS: 7, T_VW: 8, T_MV: 4, T_MV + 1: 5}[t]
                    A(sn[0:NB, c * P:(c + 1) * P], ps[0:NB, 2 * (n % 2) + 1, 0:P], ACT.Identity)
                    one = ps[:, 2 * (n % 2), :]
                    if t < T_MV:
                        A(vn[:, :, (t - T_VS) * P:(t - T_VS + 1) * P], one.rearrange("p (i n) -> p i n", i=ST),
                          ACT.Identity).then_inc(tokens_evac, 1)
                    else:
                        if t == T_MV:
                            act.wait_ge(memset_done, 2)
                        v = one.rearrange("p (i a d) -> p i a d", i=ST, a=2)
                        A(vm[:, :, 2 * (t - T_MV):2 * (t - T_MV) + 2, 0:HD], v, ACT.Identity).then_inc(tokens_evac, 1)
                elif ev[0] == "slc":
                    _, b, s = ev
                    count["slc"] += 1
                    act.wait_ge(slc_scored, count["slc"])
                    if b and s == 0:
                        act.wait_ge(sst_moved, 32 * b)
                    for j in range(2):
                        at = (2 * s + j) * 512
                        last = A(sst[0:NH, at:at + 512], ps[0:NH, 6 + j, :], ACT.Identity)
                    last.then_inc(slc_evac, 1)
                elif ev[0] == "blocks":
                    act.wait_ge(blocks_done, ev[1] + 1)
                    A(kct[:, 0:NCB], ps[:, 4, 0:NCB], ACT.Identity, bias=par_("bk"))
                    A(vc[0:NCB, ev[1], :], ps[0:NCB, 5, 0:P], ACT.Identity).then_inc(blocks_evac, 1)
                elif ev[0] == "cmp":
                    b = ev[1]
                    act.wait_ge(cmp_scored, b + 1)
                    A(sst[0:NH, 2048:2048 + NCB], ps[0:NH, 4, 0:NCB], ACT.Identity).then_inc(cmp_evac, 1)
                    act.wait_ge(cmp_evac, b + 1)
                    act.wait_ge(slc_evac, 2 * b + 2)
                    act.dma_start(sall[8 * b:8 * b + 8, 0:2048], sst[0:NH, 0:2048]).then_inc(sst_moved, 16)
                    act.dma_start(scm[8 * b:8 * b + 8, 0:NCB], sst[0:NH, 2048:2048 + NCB]).then_inc(sst_moved, 16)

                elif ev == ("soft", "slc_exp"):
                    act.wait_ge(sx_in, 3)
                    A(sall[:, :], sall[:, :], ACT.Exp, bias=ssx[:, 7:8], scale=SCALE, accum_out=ssx[:, 8:9]).then_inc(sx_out, 1)

            for ev in EVENTS_A:
                step(ev)

            act.wait_ge(kn_T, 1)
            act.wait_ge(sst_moved, 32 * NB)
            act.wait_ge(pooled_ready, NB + 1)
            for t in range(2):
                last = A(kN[:, t, :, :], ps[:, 4 + t, :].rearrange("p (i n) -> p i n", i=ST), ACT.Identity)
            last.then_inc(kn_evac, 1)
            act.wait_ge(sn_T, 1)
            A(sn[0:NB, 0:512], ps[0:NB, 0, :], ACT.Identity)
            last = A(sn[0:NB, 6 * P:7 * P], ps[0:NB, 1, 0:P], ACT.Identity)
            last.then_inc(sn_evac, 1)
            act.wait_ge(g_T, 1)
            A(gN[:, :, :], ps[:, 3, :].rearrange("p (i n) -> p i n", i=ST)[:, :, 64:88], ACT.Exp, scale=-1.0).then_inc(g_exp, 1)
            act.wait_ge(blocks_done, NB + 1)
            for g in range(2):
                A(kct[hr[g], 64 + g * NCP:64 + (g + 1) * NCP], ps[hr[g], 6, 0:NCP], ACT.Identity, bias=par_("bk", lo=hr[g].start, hi=hr[g].stop))
            A(vcp[0:NCP, :], ps[0:NCP, 6, P:2 * P], ACT.Identity).then_inc(blocks_evac, 1)
            act.wait_ge(az_ready, 1)
            link(A(lfo[0:4, :], lfo[0:4, :], ACT.Exp, scale=-1.0))
            A(lfo[0:4, :], lfo[0:4, :], ACT.Ln, bias=1.0).then_inc(ln_ready, 1)

            def window_row(b):
                act.wait_ge(wsc_done, b + 1)
                if b >= 4:
                    act.wait_ge(w_moved[b % 4], 16)
                at = (b % 4) * S
                A(sst[0:NH, at:at + S], ps[0:NH, 2, :], ACT.Identity).then_inc(wsc_evac, 1)
                act.wait_ge(wsc_evac, b + 1)
                act.dma_start(swin[8 * b:8 * b + 8, 0:S], sst[0:NH, at:at + S]).then_inc(w_moved[b % 4], 16)

            for b in range(WINDOWS_FIRST):
                window_row(b)
            act.wait_ge(r_T, 1)
            r4 = ps[:, 5, 0:ST * 36].rearrange("p (i n) -> p i n", i=ST)
            A(rT[:, :, :], r4, ACT.Identity)
            A(enm[:, :, :], r4[:, :, 32:36], ACT.Exp, scale=-1.0).then_inc(rt_evac, 1)
            act.wait_ge(rt_evac, 1)
            for q in range(16):
                hh, j = q // 4, q % 4
                if q:
                    act.wait_ge(dmask_done, q + 1)
                for head in ([0] if q == 0 else [hh + 1] if j == 2 and hh < 3 else []):
                    act.wait_ge(bc_done, head + 1)
                    A(mrow[:, head % 2, :], ps[:, 7, :], ACT.Identity).then_inc(bc_evac, 1)
                if q == 0:
                    act.wait_ge(dmask_done, 1)
                last = A(dt_[:, q % 2, 0:P], dt_[:, q % 2, 0:P], ACT.Exp, bias=rT[:, j, hh:hh + 1])
                if j < 3:
                    last = A(dt_[:, q % 2, P:S - j * P], mrow[:, hh % 2, (j + 1) * P:S], ACT.Exp, bias=rT[:, j, hh:hh + 1])
                last.then_inc(dt_done, 1)
                if WINDOWS_FIRST + q < NB:
                    window_row(WINDOWS_FIRST + q)
                if q == 11:
                    act.wait_ge(sgate_moved, 16 * NB)
                    A(sg[:, 0:3], sg[:, 0:3], ACT.Exp, scale=-1.0).then_inc(sg_exp, 1)
                    act.wait_ge(sx_in, 1)
                    A(scm[:, 0:NCB], scm[:, 0:NCB], ACT.Exp, bias=ssx[:, 1:2], scale=SCALE, accum_out=ssx[:, 2:3]).then_inc(sx_out, 1)
                if q == 13:
                    act.wait_ge(sx_in, 2)
                    A(swin[0:64, 0:T], swin[0:64, 0:T], ACT.Exp, bias=ssx[:, 4:5], scale=SCALE, accum_out=ssx[:, 5:6]).then_inc(sx_out, 1)
                if q == 14:
                    act.wait_ge(saz_ready, 1)
                    link(A(mv[:, 4:5], mv[:, 4:5], ACT.Exp, scale=-1.0))
                    A(mv[:, 4:5], mv[:, 4:5], ACT.Ln, bias=1.0).then_inc(sln_ready, 1)
            act.wait_ge(sexp_in, 1)
            A(mv[:, 8:11], mv[:, 8:11], ACT.Exp).then_inc(sexp_ready, 1)
            act.wait_ge(w_done, 16)
            act.wait_ge(num_done, 3)
            for g in range(N_A + RAW, N_A + RAW + EXTRA):
                load_weights(g)
            A(emos[:, :, :], sT[:, T_MO:T_MO + 2, :], ACT.Exp, scale=-1.0)
            A(dt_[:, :, :], pT[:, T_MO:T_MO + 2, 0:S], ACT.Exp, scale=-1.0).then_inc(emo_ready, 1)
            act.wait_ge(pcx_ready, 1)
            A(pc[:, :, 0:NCP], pc[:, :, 0:NCP], ACT.Exp, scale=SCALE).then_inc(pcx_exp, 1)
            for ev in EVENTS_B:
                step(ev)
            hi(N_IN)
            hi(N_IN + 1)
            NU = len(UNITS)
            for u in range(NU + 1):
                if u < NU:
                    hh, i = UNITS[u]
                    act.wait_ge(mx_ready, u + 1)
                    if u >= 2:
                        act.wait_ge(t_done, u - 1)
                    for r in range(2):
                        last = A(pr[:, u % 2, r, 0:(i + 1) * P], ps[:, 2 * (u % 2) + r, 0:(i + 1) * P], ACT.Exp,
                                 bias=nmx[:, u % 2, r:r + 1], scale=SCALE, accum_out=sm[:, u % 2, r:r + 1])
                    last.then_inc(p_exp, 1)
                if u >= 1:
                    v = u - 1
                    n = (UNITS[v][1] + 1) * P
                    act.wait_ge(t_done, v + 1)
                    if v >= 2:
                        act.wait_ge(pv_done, v - 1)
                    A(prT[:, v % 2, 0, 0:n], ps[:, 4, 0:n], ACT.Identity).then_inc(pt_act, 1)
            N2 = len(PART1)
            for k in range(KD):
                if k == 0:
                    act.wait_ge(mix_ready, 1)
                A(hR[:, 0, k, :], mix[:, k, :], ACT.Identity).then_inc(h_hi, 1)
            nhi = N_IN + 2
            for m, (kind, t, _) in enumerate(PART2):
                n = N2 + m
                while SPLIT[nhi - 1] < (CHUNK0[n + 1] - 1) // KD:
                    hi(nhi)
                    nhi += 1
                if kind == "out" or kind == "up":
                    item_ready(act, n)
                while nhi < len(SPLIT) and SPLIT[nhi - 2] < CHUNK0[n + 1] // KD:
                    hi(nhi)
                    nhi += 1
                if kind == "out":
                    act.wait_ge(x_ready, t + 1)
                    squares(1, t)
                    if t == KD - 1:
                        act.wait_ge(var_ready, 2)
                        A(rstd[:, :], rstd[:, :], ACT.Sqrt).then_inc(root_ready, 1)
                        normed(1, 24)
                        act.wait_ge(late_done, 1)
                        A(sall[0:9, 0:D].rearrange("p (a n) -> p a n", a=2), ps[0:9, 6:8, :], ACT.Identity).then_inc(late_evac, 1)
                elif kind == "up":
                    j, b = t % FC, t // FC
                    v = 2 * j + b
                    if v >= 2:
                        act.wait_ge(y_used, v - 1)
                    if v == 0:
                        act.wait_ge(zero_done, 1)
                    link(A(zb[:, b, 2:T + 2].rearrange("p (a n) -> p a n", a=2), ps[:, 2 * (n % 2):2 * (n % 2) + 2, 0:TH],
                           ACT.Identity))
                    A(yab[:, b, :], zb[:, b, 2:T + 2], ACT.Identity, bias=par_("conv_b", t, t + 1),
                      scale=par_("conv_w", 3 * t + 2, 3 * t + 3)).then_inc(y_ready, 1)
                    if b == 0:
                        act.wait_ge(silu_in, j + 1)
                        if j:
                            act.wait_ge(f_ready, j)
                        A(sil[:, :], yab[:, 0, :], ACT.Silu).then_inc(silu_out, 1)
                    else:
                        act.wait_ge(f_ready, j + 1)
                        if j == FH:
                            act.wait_ge(evac_dve, PART2_AT["down0", KD - 1] + 1)
                        A(fR[:, 0, j % FH, :], yab[:, 1, :], ACT.Identity).then_inc(f_hi, 1)
                elif kind == "down1":
                    act.wait_ge(x_ready, KD + t + 1)
                    squares(2, t)
            act.wait_ge(var_ready, 3)
            A(rstd[:, :], rstd[:, :], ACT.Sqrt).then_inc(root_ready, 1)

        @block.vector
        def _(dve):
            V = nc.vector
            chain = [0]

            def link(ins):
                chain[0] += 1
                ins.then_inc(dve_step, 1)
                dve.wait_ge(dve_step, chain[0])

            def root(n):
                if n == 0:
                    dve.wait_ge(sq_used, KD)
                else:
                    dve.wait_ge(total_done, n)
                V.tensor_scalar(rstd[:, :].rearrange("p (a n) -> p a n", a=2), ps[:, 4:6, 0:TH], EPS, None, ALU.add).then_inc(var_ready, 1)
                dve.wait_ge(root_ready, n + 1)
                link(V.reciprocal(rstd[:, :], rstd[:, :]))

            def add_squares(n, k):
                dve.wait_ge(sq_ready, n * KD + k + 1)
                V.tensor_tensor(rstd[:, :], rstd[:, :], sq[:, k % 2, :], ALU.add).then_inc(sum_ready, 1)
                dve.wait_ge(sum_ready, (n - 1) * (KD - 1) + k)

            def normed(n, gain, scale, shift):
                link(V.scalar_tensor_tensor(ab[:, :, :], mod[:, scale:scale + KD, :], 1.0,
                                            par_(gain).unsqueeze(2).broadcast_to([P, KD, 9]), ALU.add, ALU.mult))
                link(V.tensor_tensor(sc2[:, :, 0:NB], x[:, :, S:T], rstd[:, S:T].unsqueeze(1).broadcast_to([P, KD, NB]), ALU.mult))
                link(V.tensor_tensor(sc2[:, :, 0:NB], sc2[:, :, 0:NB], ab[:, :, 1:9], ALU.mult))
                V.tensor_tensor(sc2[:, :, 0:NB], sc2[:, :, 0:NB], mod[:, shift:shift + KD, 1:9], ALU.add).then_inc(h_sample, 1)
                for k in range(KD + 1):
                    if k < KD:
                        V.scalar_tensor_tensor(sq[:, k % 2, 0:S], x[:, k, 0:S], ab[:, k, 0:1], rstd[:, 0:S], ALU.mult, ALU.mult)\
                            .then_inc(xn_ready, 1)
                    if k == 0:
                        dve.wait_ge(hs_hi, n + 1)
                        link(V.tensor_tensor(hR[:, 1, :, S:T], sc2[:, :, 0:NB], hR[:, 0, :, S:T].bitcast(F32), ALU.subtract))
                    else:
                        dve.wait_ge(h_hi, n * 2 * KD + k)
                        V.scalar_tensor_tensor(hR[:, 1, k - 1, 0:S], sq[:, (k - 1) % 2, 0:S], mod[:, shift + k - 1, 0:1],
                                               hR[:, 0, k - 1, 0:S].bitcast(F32), ALU.add, ALU.subtract)\
                            .then_inc(h_lo, 1)
                        dve.wait_ge(h_lo, n * 2 * KD + k)

            def half_sums(h):
                b, s = h // 2, h % 2
                dve.wait_ge(cache_landed[s], 16 * HALF * (b + 1))
                for w, dst in enumerate((poolA, poolB)):
                    ww = par_("wpos", 16 * w, 16 * w + 16).unsqueeze(1).unsqueeze(1).broadcast_to([P, HALF, 8, 16])
                    link(V.tensor_tensor(tmp.rearrange("p (a n j) -> p a n j", a=HALF, j=16),
                                         pages[:, s, :, 0:P].rearrange("p a (n j) -> p a n j", j=16), ww, ALU.mult))
                    link(V.tensor_reduce(dst[:, 0, 64 * s:64 * s + 64], tmp.rearrange("p (n j) -> p n j", j=16), AX, ALU.add))
                    dve.wait_ge(vmul_ready, 2 * h + w + 1)
                    V.tensor_reduce(dst[:, 1, 64 * s:64 * s + 64], tmpv.rearrange("p (n j) -> p n j", j=16), AX, ALU.add)\
                        .then_inc(vmul_used, 1)
                dve.wait_ge(vmul_used, 2 * h + 2)
                dve.sem_inc(comp_done, 1)

            def prompt_sums():
                for kv, src in enumerate((pT[:, T_KC, 0:S], pT[:, T_VC, 0:S])):
                    for half, dst in enumerate((poolA, poolB)):
                        w = par_("wpos", 32 * kv + 16 * half, 32 * kv + 16 * half + 16).unsqueeze(1).broadcast_to([P, S // 16, 16])
                        o = tmp[:, 0:S].rearrange("p (n j) -> p n j", j=16)
                        link(V.tensor_tensor(o, src.rearrange("p (n j) -> p n j", j=16), w, ALU.mult))
                        link(V.tensor_reduce(dst[:, kv, 0:S // 16], o, AX, ALU.add))

            dve.wait_ge(silu_exp, 1)
            link(V.tensor_scalar(sc2[:, :, :], sc2[:, :, :], 1.0, None, ALU.add))
            link(V.reciprocal(sc2[:, :, :], sc2[:, :, :]))
            V.tensor_tensor(sc[:, :, :], sc2[:, :, :], par_("c").rearrange("p (k n) -> p k n", k=KD), ALU.mult).then_inc(silu_ready, 1)
            root(0)
            half_sums(0)
            dve.wait_ge(turn_evac, 16)
            dve.wait_ge(x_landed, 16 * KD)
            normed(0, "g1", 8, 0)

            for b in range(NB):
                for h in range(2 * b + (b == 0), 2 * b + 2):
                    half_sums(h)
                if b:
                    dve.wait_ge(blocks_done, b)
                V.tensor_tensor(pooled[:, :, 0:NCB], poolA[:, :, 0:NCB], poolB[:, :, 1:NCB + 1], ALU.add).then_inc(pooled_ready, 1)
                dve.wait_ge(pooled_ready, b + 1)

            dve.wait_ge(evac_act, N_A)
            prompt_sums()
            dve.wait_ge(blocks_done, NB)
            dve.wait_ge(cmp_evac, NB)
            link(V.memset(kct[:, 64:64 + 2 * NCP], 0.0))
            V.tensor_tensor(pooled[:, :, 0:NCP], poolA[:, :, 0:NCP], poolB[:, :, 1:NCP + 1], ALU.add).then_inc(pooled_ready, 1)

            dve.wait_ge(pooled_ready, NB + 1)
            dve.wait_ge(tokens_evac, len(TOKEN_ITEMS))
            link(V.memset(r36[0:36, :], 0.0))
            link(V.memset(zro[0:4, :], 0.0))
            link(V.tensor_scalar(r36[0:4, :], pT[0:4, T_G, 0:S], par_("gate_b", hi=4), None, ALU.add))
            link(V.tensor_scalar(bro[0:4, :], pT[32:36, T_G, 0:S], par_("gate_b", lo=32, hi=36), None, ALU.add))
            V.scalar_tensor_tensor(lfo[0:4, :], bro[0:4, :], -1.0, bro[0:4, :], ALU.mult, ALU.max).then_inc(az_ready, 1)
            dve.wait_ge(ln_ready, 1)
            link(V.scalar_tensor_tensor(lfo[0:4, :], bro[0:4, :], 0.0, lfo[0:4, :], ALU.min, ALU.subtract))
            link(V.tensor_tensor_scan(bro[0:4, :], lfo[0:4, :], zro[0:4, :], 0.0, ALU.add, ALU.add))
            link(V.tensor_tensor(r36[0:4, :], r36[0:4, :], bro[0:4, :], ALU.subtract))
            link(V.tensor_tensor_scan(mro[0:4, :], r36[0:4, :], zro[0:4, :], 0.0, ALU.max, ALU.max))
            link(V.tensor_tensor(r36[32:36, :], bro[0:4, :], mro[0:4, :], ALU.add))
            link(V.tensor_copy(mout[0:4, 0:1], r36[32:36, S - 1:S]))
            V.tensor_scalar(mro[0:4, :], mro[0:4, :], -1.0, None, ALU.mult).then_inc(rows_ready, 1)

            dve.wait_ge(rt_evac, 1)
            dve.wait_ge(kn_evac, 1)
            def masked_row(q):
                hh, j = q // 4, q % 4
                dve.wait_ge(bc_evac, hh + 1)
                V.tensor_tensor(dt_[:, q % 2, 0:P], mrow[:, hh % 2, j * P:(j + 1) * P], con_("ct"), ALU.add)\
                    .then_inc(dmask_done, 1)

            def head_result(hh):
                dve.wait_ge(num_done, hh + 1)
                num = ps[:, 6, 0:4 * 65].rearrange("p (i n) -> p i n", i=ST)
                link(V.tensor_copy(d4[:, 0:4], num[:, :, HD]))
                link(V.scalar_tensor_tensor(d4[:, 4:8], d4[:, 0:4], -1.0, d4[:, 0:4], ALU.mult, ALU.max))
                link(V.tensor_tensor(d4[:, 4:8], d4[:, 4:8], enm[:, :, hh], ALU.max))
                link(V.reciprocal(d4[:, 4:8], d4[:, 4:8]))
                V.tensor_tensor(hN[:, :, hh * HD:(hh + 1) * HD], num[:, :, 0:HD], d4[:, 4:8].unsqueeze(2).broadcast_to([P, ST, HD]),
                                ALU.mult).then_inc(num_evac, 1)
                dve.wait_ge(num_evac, hh + 1)

            def samples_cmp_max():
                link(V.tensor_reduce(ssx[:, 0:1], scm[:, 0:NCB], AX, ALU.max))
                V.tensor_scalar(ssx[:, 1:2], ssx[:, 0:1], -SCALE, None, ALU.mult).then_inc(sx_in, 1)

            def samples_cmp_weights():
                dve.wait_ge(sg_exp, 1)
                link(V.tensor_scalar(sg[:, 0:3], sg[:, 0:3], 1.0, None, ALU.add))
                link(V.reciprocal(sg[:, 0:3], sg[:, 0:3]))
                dve.wait_ge(sx_out, 1)
                link(V.reciprocal(ssx[:, 9:10], ssx[:, 2:3]))
                V.tensor_scalar(scm[:, 0:NCB], scm[:, 0:NCB], ssx[:, 9:10], None, ALU.mult).then_inc(imp_in, 1)
                windows_moved(dve)
                link(V.memset(swin[0:64, 0:1], NEG))
                link(V.tensor_reduce(ssx[:, 3:4], swin[0:64, 0:T], AX, ALU.max))
                V.tensor_scalar(ssx[:, 4:5], ssx[:, 3:4], -SCALE, None, ALU.mult).then_inc(sx_in, 1)

            dve.wait_ge(snew_done, 1)
            dve.wait_ge(sst_moved, 32 * NB)
            link(V.tensor_tensor(sall[:, NPG * P:NPG * P + NB], ps[0:64, 6, 384:384 + NB], con_("newm", rows=64), ALU.add))
            link(V.tensor_tensor(swin[0:64, S:T], ps[0:64, 6, 384 + NB:384 + 2 * NB], con_("newm", rows=64), ALU.add))

            q_, k_, v_ = smr[:, 0:64], smr[:, 64:128], smr[:, 128:144]

            def samples_gates():
                dve.wait_ge(rows_moved, 16 * 48)
                dve.wait_ge(rec_landed, 32)
                link(V.tensor_tensor(mv[:, 0:1], smr[:, 144:145], par_("igb"), ALU.add))
                link(V.tensor_tensor(mv[:, 1:2], smr[:, 145:146], par_("fgb"), ALU.add))
                V.scalar_tensor_tensor(mv[:, 4:5], mv[:, 1:2], -1.0, mv[:, 1:2], ALU.mult, ALU.max).then_inc(saz_ready, 1)

            def samples_decay():
                dve.wait_ge(sln_ready, 1)
                link(V.scalar_tensor_tensor(mv[:, 1:2], mv[:, 1:2], 0.0, mv[:, 4:5], ALU.min, ALU.subtract))
                link(V.tensor_tensor(mv[:, 2:3], mv[:, 1:2], par_("mm"), ALU.add))
                link(V.tensor_tensor(mv[:, 3:4], mv[:, 2:3], mv[:, 0:1], ALU.max))
                V.tensor_tensor(mv[:, 8:9], mv[:, 0:1], mv[:, 3:4], ALU.subtract)
                V.tensor_tensor(mv[:, 9:10], mv[:, 2:3], mv[:, 3:4], ALU.subtract)
                V.tensor_scalar(mv[:, 10:11], mv[:, 3:4], -1.0, None, ALU.mult).then_inc(sexp_in, 1)

            masked_row(0)
            for q in range(17):
                if q < 16:
                    hh, j = q // 4, q % 4
                    if q < 15:
                        masked_row(q + 1)
                    dve.wait_ge(dt_done, q + 1)
                    dve.wait_ge(mscore_done, q + 1)
                    if hh >= 2 and j == 0:
                        dve.wait_ge(num_done, hh - 1)
                    n = S - j * P
                    V.tensor_tensor(wj[hh % 2][:, OFF[j]:OFF[j] + n], ps[:, 4 + q % 2, 0:n], dt_[:, q % 2, 0:n], ALU.mult)
                    V.tensor_scalar(wk[hh % 2][:, j, :], kN[:, hh // 2, j, (hh % 2) * HD:(hh % 2 + 1) * HD],
                                    dt_[:, q % 2, n - 1:n], None, ALU.mult).then_inc(w_done, 1)
                    dve.wait_ge(w_done, q + 1)
                if q >= 8 and q % 4 == 0:
                    head_result(q // 4 - 2)
                if q == 9:
                    samples_cmp_max()
                if q == 12:
                    samples_cmp_weights()
                if q == 13:
                    samples_gates()
                if q == 15:
                    samples_decay()
            dve.wait_ge(g_exp, 1)
            link(V.tensor_scalar(gN[:, :, :], gN[:, :, :], 1.0, None, ALU.add))
            link(V.reciprocal(gN[:, :, :], gN[:, :, :]))

            dve.wait_ge(csc_done, 1)
            dve.wait_ge(dt_done, 16)
            madd = con_("cadd").rearrange("p (i n) -> p i n", i=ST).unsqueeze(1).broadcast_to([P, 2, ST, NCP])
            for g in range(2):
                for half in range(2):
                    s4 = ps[:, half, 0:16 * NCP].rearrange("p (a i m) -> p a i m", a=2, i=ST)[:, :, :, g * NCP:(g + 1) * NCP]
                    u = 16 * g + 8 * half
                    p4 = pc[:, u:u + 8, :].rearrange("p (a i) n -> p a i n", a=2)
                    last = V.tensor_tensor(p4, s4, madd, ALU.add)
            link(last)
            link(V.tensor_reduce(mx[:, 0, :], pc[:, :, 0:NCP], AX, ALU.max))
            V.tensor_tensor(pc[:, :, 0:NCP], pc[:, :, 0:NCP], mx[:, 0, :].unsqueeze(2).broadcast_to([P, 32, NCP]), ALU.subtract)\
                .then_inc(pcx_ready, 1)
            dve.wait_ge(pcx_ready, 1)
            head_result(3)
            V.tensor_copy(cout[0:HD, :, :], ps[0:HD, 3, 0:260].rearrange("p (h n) -> p h n", h=4)).then_inc(cout_ready, 1)
            dve.wait_ge(emo_ready, 1)
            link(V.tensor_scalar(dt_[:, :, :], dt_[:, :, :], 1.0, None, ALU.add))
            link(V.reciprocal(dt_[:, :, :], dt_[:, :, :]))
            dve.wait_ge(hT_done, 1)
            windows_moved(dve)
            V.tensor_tensor(mix[:, 4:6, 0:S], ps[:, 4:6, :], dt_[:, :, :], ALU.mult).then_inc(mmix_ready, 1)

            link(V.memset(simp[0:64, :], 0.0))
            dve.wait_ge(imp_done, 1)
            link(V.tensor_copy(simp[0:64, 1:1 + NCB], ps[0:64, 7, 0:NCB]))
            link(V.tensor_reduce(sel[:, 0, 0:NSB], simp[0:64, 0:132].rearrange("p (n r) -> p n r", r=4), AX, ALU.add))
            link(V.tensor_tensor(sel[:, 0, 0:NSB], sel[:, 0, 0:NSB], simp[0:64, 4:133:4], ALU.add))
            link(V.memset(sel[:, 0, 0:1], 1e6))
            link(V.memset(sel[:, 0, NSB - 2:NSB], 1e6))
            s_i = sel[:, 0, 0:NSB].unsqueeze(1).broadcast_to([64, NSB, NSB])
            s_j = sel[:, 0, 0:NSB].unsqueeze(2).broadcast_to([64, NSB, NSB])
            rk = rank[0:64, :].rearrange("p (j i) -> p j i", j=NSB)
            te = tie[0:64, :].rearrange("p (j i) -> p j i", j=NSB - 1)
            link(V.tensor_tensor(rk, s_i, s_j, ALU.is_gt))
            link(V.tensor_tensor(te, s_i[:, 1:, 0:NSB - 1], s_j[:, 1:, 0:NSB - 1], ALU.is_equal))
            dve.wait_ge(ltri_landed, 16)
            link(V.tensor_tensor(tie[0:64, :], tie[0:64, :], ltri[0:64, :], ALU.mult))
            link(V.tensor_tensor(rk[:, 1:, 0:NSB - 1], rk[:, 1:, 0:NSB - 1], te, ALU.add))
            link(V.tensor_reduce(sel[:, 1, 0:NSB], rk, AX, ALU.add))
            link(V.tensor_scalar(sel[:, 2, 0:NSB], sel[:, 1, 0:NSB], float(NSEL) - 0.5, NEG, ALU.is_gt, ALU.mult))
            s3 = sall[:, 0:NPG * P].rearrange("p (n k) -> p n k", k=64)
            link(V.tensor_tensor(s3, s3, sel[:, 2, 0:32].unsqueeze(2).broadcast_to([64, 32, 64]), ALU.add))
            link(V.tensor_reduce(ssx[:, 6:7], sall[:, :], AX, ALU.max))
            V.tensor_scalar(ssx[:, 7:8], ssx[:, 6:7], -SCALE, None, ALU.mult).then_inc(sx_in, 1)
            link(V.tensor_scalar(scm[:, 0:NCB], scm[:, 0:NCB], sg[:, 0:1], None, ALU.mult))
            dve.wait_ge(pcx_exp, 1)
            for half in range(2):
                p4 = pc[:, 16 * half:16 * half + 16, :].rearrange("p (a i) n -> p a i n", a=4)[:, :, :, 0:NCP]
                mmul = con_("cmul").rearrange("p (i n) -> p i n", i=ST).unsqueeze(1).broadcast_to([P, 4, ST, NCP])
                link(V.tensor_tensor(p4, p4, mmul, ALU.mult))
            link(V.tensor_reduce(mx[:, 1, :], pc[:, :, 0:NCP], AX, ALU.add))
            link(V.tensor_scalar(mx[:, 1, :], mx[:, 1, :], float(np.finfo(np.float32).tiny), None, ALU.max))
            link(V.reciprocal(mx[:, 2, :], mx[:, 1, :]))
            g0 = gN[:, :, 0:22:3].rearrange("p i h -> p h i")
            link(V.tensor_tensor(mx[:, 3, :].rearrange("p (h i) -> p h i", h=NH), mx[:, 2, :].rearrange("p (h i) -> p h i", h=NH),
                                 g0, ALU.mult))
            V.tensor_tensor(pc[:, :, 0:NCP], pc[:, :, 0:NCP], mx[:, 3, :].unsqueeze(2).broadcast_to([P, 32, NCP]), ALU.mult)\
                .then_inc(pc_ready, 1)

            c_de = cst[:, :].rearrange("p (d e) -> p d e", e=16)
            t_ed = ctmp[:, :].rearrange("p (e d) -> p e d", d=64)
            t_de = ctmp[:, :].rearrange("p (d e) -> p d e", e=16)
            link(V.tensor_tensor(t_ed, c_de.rearrange("p d e -> p e d"), q_.unsqueeze(1).broadcast_to([P, 16, 64]), ALU.mult))
            link(V.tensor_reduce(qc[:, :], t_ed, AX, ALU.add))
            link(V.tensor_tensor(ctmp[:, 0:64], q_, k_, ALU.mult))
            link(V.tensor_reduce(mv[:, 11:12], ctmp[:, 0:64], AX, ALU.add))
            link(V.tensor_tensor(ctmp[:, 0:64], q_, par_("mn"), ALU.mult))
            link(V.tensor_reduce(mv[:, 12:13], ctmp[:, 0:64], AX, ALU.add))
            dve.wait_ge(sx_out, 3)
            for r, (n, buf) in enumerate(((8, sall[:, :]), (5, swin[0:64, 0:T]))):
                link(V.reciprocal(ssx[:, 10 + r:11 + r], ssx[:, n:n + 1]))
                link(V.tensor_tensor(ssx[:, 12 + r:13 + r], ssx[:, 10 + r:11 + r], sg[:, 1 + r:2 + r], ALU.mult))
                last = V.tensor_scalar(buf, buf, ssx[:, 12 + r:13 + r], None, ALU.mult)
            last.then_inc(sp_ready, 1)
            dve.wait_ge(spT_done, 1)
            V.tensor_copy(ptS[:, 0:NPG, :].rearrange("p (a c) r -> p a (c r)", a=2), ps[:, 4:6, :])
            V.tensor_copy(ptS[:, NPG:NPG + ST, :].rearrange("p c r -> p (c r)"), ps[:, 6, 0:256])
            V.tensor_copy(ptS[0:NCB, 20, :], ps[0:NCB, 7, 0:64])
            V.tensor_copy(ptS[0:NB, 21, :], ps[0:NB, 7, 64:128])
            V.tensor_copy(ptS[0:NB, 22, :], ps[0:NB, 7, 128:192]).then_inc(spT_evac, 1)

            dve.wait_ge(sexp_ready, 1)
            link(V.tensor_tensor(mv[:, 11:12], mv[:, 11:12], mv[:, 8:9], ALU.mult))
            link(V.scalar_tensor_tensor(mv[:, 13:14], mv[:, 12:13], mv[:, 9:10], mv[:, 11:12], ALU.mult, ALU.add))
            link(V.scalar_tensor_tensor(mv[:, 14:15], mv[:, 13:14], -1.0, mv[:, 13:14], ALU.mult, ALU.max))
            link(V.tensor_tensor(mv[:, 14:15], mv[:, 14:15], mv[:, 10:11], ALU.max))
            link(V.reciprocal(mv[:, 14:15], mv[:, 14:15]))
            link(V.tensor_scalar(qc[:, :], qc[:, :], mv[:, 9:10], None, ALU.mult))
            link(V.scalar_tensor_tensor(shh[:, :], v_, mv[:, 11:12], qc[:, :], ALU.mult, ALU.add))
            link(V.tensor_scalar(shh[:, :], shh[:, :], mv[:, 14:15], None, ALU.mult))
            link(V.tensor_copy(t_de, k_.unsqueeze(2).broadcast_to([P, 64, 16])))
            link(V.scalar_tensor_tensor(t_de, t_de, mv[:, 8:9], v_.unsqueeze(1).broadcast_to([P, 64, 16]), ALU.mult, ALU.mult))
            link(V.scalar_tensor_tensor(cst[:, :], cst[:, :], mv[:, 9:10], ctmp[:, :], ALU.mult, ALU.add))
            link(V.tensor_scalar(smr[:, 146:210], k_, mv[:, 8:9], None, ALU.mult))
            V.scalar_tensor_tensor(smr[:, 146:210], par_("mn"), mv[:, 9:10], smr[:, 146:210], ALU.mult, ALU.add)\
                .then_inc(srec_ready, 1)
            dve.wait_ge(srec_ready, 1)

            dve.wait_ge(pool_mm, 1)
            for t in range(2):
                V.tensor_scalar(mix[:, 6 + t, 0:S], ps[:, 4 + t, :], par_("pool_s", t, t + 1), None, ALU.mult)
                last = V.tensor_scalar(mix[:, 6 + t, S:T], ps[:, 6, t * NB:(t + 1) * NB], par_("pool_s", t, t + 1), None, ALU.mult)
            last.then_inc(side_mix, 1)

            NU = len(UNITS)
            for u in range(NU + 2):
                if u < NU:
                    hh, i = UNITS[u]
                    a = u % 2
                    two = ps[:, 2 * a:2 * a + 2, :]
                    dve.wait_ge(qk_done, u + 1)
                    d = two[:, :, i * P:(i + 1) * P]
                    link(V.tensor_tensor(d, d, con_("cq").unsqueeze(1).broadcast_to([P, 2, P]), ALU.add))
                    link(V.tensor_reduce(nmx[:, a, :], two[:, :, 0:(i + 1) * P], AX, ALU.max))
                    V.tensor_scalar(nmx[:, a, :], nmx[:, a, :], -SCALE, None, ALU.mult).then_inc(mx_ready, 1)
                if 1 <= u <= NU:
                    v = u - 1
                    n = (UNITS[v][1] + 1) * P
                    dve.wait_ge(t_done, v + 1)
                    if v >= 2:
                        dve.wait_ge(pv_done, v - 1)
                    V.tensor_copy(prT[:, v % 2, 1, 0:n], ps[:, 5, 0:n])
                    V.tensor_copy(pcT[0:NCP, v % 2, :], ps[0:NCP, 6, 0:P]).then_inc(pt_dve, 1)
                    dve.wait_ge(pt_dve, v + 1)
                if u < NU:
                    dve.wait_ge(p_exp, u + 1)
                    link(V.reciprocal(fac[:, a, :], sm[:, a, :]))
                    link(V.tensor_tensor(fac[:, a, :], fac[:, a, :], gN[:, i, 3 * hh + 1:3 * hh + 3], ALU.mult))
                    for r in range(2):
                        last = V.tensor_scalar(pr[:, a, r, 0:(i + 1) * P], pr[:, a, r, 0:(i + 1) * P], fac[:, a, r:r + 1], None,
                                               ALU.mult)
                    last.then_inc(p_ready, 1)
                if u >= 2:
                    hh, i = UNITS[u - 2]
                    rows = hr[hh // G]
                    dve.wait_ge(pv_done, u - 1)
                    if i == SAMPLE_AT:
                        b = (u - 2) // ST
                        dve.wait_ge(spv_done, b + 1)
                        V.tensor_copy(so8[0:NH, b * P:(b + 1) * P], ps[0:NH, 7, P:2 * P])
                    V.tensor_copy(mix[rows, hh % G, i * P:(i + 1) * P], ps[rows, 7, 0:P]).then_inc(o_evac, 1)

            link(V.tensor_scalar(emos[:, :, :], emos[:, :, :], 1.0, None, ALU.add))
            link(V.reciprocal(emos[:, :, :], emos[:, :, :]))
            dve.wait_ge(shT_done, 1)
            V.tensor_tensor(mix[:, 4:6, S:T], ps[:, 7, 0:2 * NB].rearrange("p (t b) -> p t b", t=2), emos[:, :, :], ALU.mult)
            dve.wait_ge(soT_done, 1)
            for hh in range(NH):
                rows = hr[hh // G]
                last = V.tensor_copy(mix[rows, hh % G, S:T], ps[rows, 6, 0:64].rearrange("p (b r) -> p b r", b=NB)[:, :, hh])
            last.then_inc(mix_ready, 1)

            for k in range(KD):
                dve.wait_ge(h_hi, KD + k + 1)
                V.tensor_tensor(hR[:, 1, k, :], mix[:, k, :], hR[:, 0, k, :].bitcast(F32), ALU.subtract).then_inc(h_lo, 1)

            def residual(m, gate, done):
                kind, t, _ = PART2[m]
                n = len(PART1) + m
                a = 2 * (n % 2)
                item_ready(dve, n)
                gp = mod[:, gate + t, 0:1]
                link(V.tensor_tensor(t8[:, :], ps[:, a + 1, TH - NB:TH], mod[:, gate + t, 1:9], ALU.mult))
                V.scalar_tensor_tensor(x[:, t, 0:TH], ps[:, a, 0:TH], gp, x[:, t, 0:TH], ALU.mult, ALU.add)
                V.scalar_tensor_tensor(x[:, t, TH:S], ps[:, a + 1, 0:TH - NB], gp, x[:, t, TH:S], ALU.mult, ALU.add)\
                    .then_inc(evac_dve, 1)
                last = V.tensor_tensor(x[:, t, S:T], x[:, t, S:T], t8[:, :], ALU.add)
                if done:
                    last.then_inc(x_ready, 1)
                    dve.wait_ge(x_ready, done)
                else:
                    link(last)

            for m, (kind, t, _) in enumerate(PART2):
                if kind == "out":
                    residual(m, 16, t + 1)
                    if t >= 2:
                        add_squares(1, t - 1)
                    if t == KD - 1:
                        add_squares(1, KD - 1)
                        root(1)
                        normed(1, "g2", 32, 24)
                        V.memset(zb[:, :, 0:2], 0.0).then_inc(zero_done, 1)
                        dve.wait_ge(ffst_landed, 16)
                        dve.wait_ge(early_out, 16 * 5)
                        dve.wait_ge(state_out, 16 * 8)
                        link(V.tensor_copy(ffo_s[:, :, 0, :], ffst_t[:, :, 1, :]))
                elif kind == "up":
                    j, b = t % FC, t // FC
                    v = 2 * j + b
                    w = [par_("conv_w", 3 * t + c, 3 * t + c + 1) for c in range(3)]
                    y, z = yab[:, b, :], zb[:, b, :]
                    dve.wait_ge(y_ready, v + 1)
                    nc.vector.tensor_copy(ffo_p[:, t, :], z[:, S:S + 2]).then_inc(evac_dve, 1)
                    V.tensor_copy(ffo_s[:, t, 1, :], z[:, S + 2:T + 2])
                    link(V.scalar_tensor_tensor(y[:, S:T], ffst_t[:, t, 1, :], w[1], y[:, S:T], ALU.mult, ALU.add))
                    link(V.scalar_tensor_tensor(y[:, S:T], ffst_t[:, t, 0, :], w[0], y[:, S:T], ALU.mult, ALU.add))
                    link(V.scalar_tensor_tensor(y[:, 0:S], z[:, 1:S + 1], w[1], y[:, 0:S], ALU.mult, ALU.add))
                    last = V.scalar_tensor_tensor(y[:, 0:S], z[:, 0:S], w[0], y[:, 0:S], ALU.mult, ALU.add)
                    if b == 0:
                        last.then_inc(silu_in, 1)
                        dve.wait_ge(silu_out, j + 1)
                        dve.sem_inc(y_used, 1)
                    else:
                        link(last)
                        V.tensor_tensor(y, sil[:, :], y, ALU.mult).then_inc(f_ready, 1)
                        dve.wait_ge(f_hi, j + 1)
                        V.tensor_tensor(fR[:, 1, j % FH, :], y, fR[:, 0, j % FH, :].bitcast(F32), ALU.subtract).then_inc(f_lo, 1)
                        dve.wait_ge(f_lo, j + 1)
                        dve.sem_inc(y_used, 1)
                else:
                    if m == PART2_AT["down0", 0]:
                        dve.wait_ge(late_turned, 1)
                        link(V.tensor_tensor(mod[:, 40:48, :], ps[:, 6, 0:72].rearrange("p (t c) -> p t c", c=9),
                                             par_("ada_b", 40, 48).unsqueeze(2).broadcast_to([P, KD, 9]), ALU.add))
                    residual(m, 40, KD + t + 1 if kind == "down1" else 0)
                    if kind == "down1" and t >= 2:
                        add_squares(2, t - 1)
            add_squares(2, KD - 1)
            root(2)
            for k in range(KD):
                V.scalar_tensor_tensor(x[:, k, :], x[:, k, :], par_("gf", k, k + 1), rstd[:, :], ALU.mult, ALU.mult)\
                    .then_inc(out_ready, 1)


def _constants():
    c = np.zeros((P, NCON), np.float32)

    def put(name, a, rows=P):
        at, n = CON[name]
        c[:rows, at:at + n] = a.reshape(rows, n)

    put("ident", np.eye(P))
    put("ones", np.ones((P, P)))
    put("mean", np.full((P, P), 1.0 / D))
    i = np.arange(P)
    put("cq", np.where(i[None, :] <= i[:, None], 0.0, NEG))
    put("ct", np.where(i[None, :] >= i[:, None], 0.0, NEG))
    pos = (np.arange(ST)[None, :] * P + i[:, None])[:, :, None]
    seen = 16 * np.arange(NCP)[None, None, :] + 31 <= pos
    put("cadd", np.where(seen, 0.0, NEG))
    put("cmul", np.where(seen, 1.0, 0.0))
    win = np.array([[2, 8], [4, 16]], np.float32)[(i >= HD).astype(int)]
    put("rw", 1.0 / win)
    put("rcnt", 1.0 / np.minimum(win[:, :, None], np.arange(1, 17)[None, None, :]))
    r = np.arange(64)
    put("grp", (r[:, None] // 4 == r[None, :] // 4) * 1.0, 64)
    put("newm", np.where(r[:, None] // 8 == np.arange(NB)[None, :], 0.0, NEG), 64)
    return c


def _chunks(w):
    return w.reshape(-1, P, w.shape[1]).transpose(1, 0, 2)


def _stream(w):
    ada, w_in, w_out, up, down = (np.asarray(w[n])[0] for n in ("ada_w", "w_in", "w_out", "ffn_w_up", "ffn_w_down"))
    q, kv, ng, mq, mk, mv_, mif, mo, pu = np.split(w_in, np.cumsum([512, 768, 24, 256, 256, 256, 8, 256]), axis=1)
    q = q.reshape(D, 2, G, HD).transpose(0, 2, 1, 3).reshape(D, 512)
    gates = np.zeros((D, P), np.float32)
    gates[:, 0:4], gates[:, 32:36], gates[:, 64:88] = mif[:, :4], mif[:, 4:], ng
    kc, vc, ks, vs, kw, vw = np.split(kv, 6, axis=1)
    cols = np.concatenate([q, kc, vc, ks, kw, mk, mq, mo, pu, gates, vs, vw, mv_], axis=1)
    rows = np.concatenate([w_out[:512].reshape(2, G, HD, D).transpose(1, 0, 2, 3).reshape(512, D), w_out[512:]])
    src = {"ada": _chunks(ada), "in": _chunks(cols), "out": _chunks(rows), "up": _chunks(up), "down": _chunks(down)}
    src["down0"], src["down1"] = src["down"][:, :FH], src["down"][:, FH:]
    stream = np.concatenate([src[kind][:, :, t * P:(t + 1) * P] for kind, t, _ in ITEMS], axis=1)
    return stream.reshape(P, NSLOT, KD * P).transpose(1, 0, 2)


def _params(w):
    p = np.zeros((P, NPAR), np.float32)

    def put(name, a, rows=slice(0, P)):
        at, n = PAR[name]
        p[rows, at:at + n] = np.asarray(a).reshape(-1, n)

    col = lambda a: np.asarray(a).reshape(-1, P).T
    put("g1", col(w["norm1_g"][0]))
    put("g2", col(w["norm2_g"][0]))
    put("gf", col(w["final_g"]))
    put("ada_b", col(w["ada_b"][0]))
    put("conv_w", np.asarray(w["ffn_conv_w"])[0].reshape(3, 2 * FC, P).transpose(2, 1, 0))
    put("conv_b", col(w["ffn_conv_b"][0]))
    put("pool_s", col(w["pool_scale"][0]))
    wpos = np.asarray(w["nsa_cmp_pos"])[0].transpose(2, 0, 1)
    put("wpos", np.concatenate([wpos, wpos]))
    b = np.asarray(w["nsa_cmp_b"])[0]
    put("bk", np.concatenate([b[0], b[0]]))
    put("bv", np.concatenate([b[1], b[1]]), slice(0, 1))
    gb = np.asarray(w["mlstm_gate_b"])[0]
    put("gate_b", gb[:4], slice(0, 4))
    put("gate_b", gb[4:], slice(32, 36))
    put("igb", np.tile(np.repeat(gb[:4], NB), 4))
    put("fgb", np.tile(np.repeat(gb[4:], NB), 4))
    c = np.concatenate([np.asarray(w["c_prompt"]), np.asarray(w["c_sample"])])
    put("c", c.reshape(9, KD, P).transpose(2, 1, 0))
    cw = np.zeros((P, 2, P), np.float32)
    pw = np.zeros((P, 2, P), np.float32)
    for t in range(2):
        for g in range(2):
            r = slice(g * HD, (g + 1) * HD)
            cw[r, t, r] = np.asarray(w["nsa_cmp_w"])[0, t]
            pw[r, t, r] = np.asarray(w["pool_w"])[0, 2 * t + g]
    put("cw", cw)
    put("pw", pw)
    put("mn", np.tile(np.asarray(w["state_mlstm_n"])[0].transpose(1, 0, 2).reshape(32, HD), (4, 1)))
    put("mm", np.tile(np.asarray(w["state_mlstm_m"])[0].T.reshape(32, 1), (4, 1)))
    return p


def kernel(**w):
    import concourse.bacc as bacc
    from concourse.bass_utils import run_bass_kernel_spmd

    f = {n: np.asarray(a) for n, a in w.items()}
    tokens = np.concatenate([f["x_prompt"][0], f["x_sample"][:, 0]])
    ck = f["cache_k"][0].reshape(NPHYS, PAGE, 2, P)
    cv = f["cache_v"][0].reshape(NPHYS, PAGE, 2, P)
    fm = lambda a: a.transpose(0, 2, 1)
    ins = {
        "xT": tokens.T.reshape(KD, P, T).transpose(1, 0, 2),
        "weights": _stream(w),
        "params": _params(w),
        "constants": _constants(),
        "hot": np.repeat(np.eye(4, dtype=np.float32), P, axis=1),
        "ltri": np.tile(np.tril(np.ones((NSB - 1, NSB - 1), np.float32)).reshape(1, -1), (64, 1)),
        "page_table": f["page_table"].reshape(1, NB * NPG),
        "cache_keys": np.concatenate([fm(ck[:, :, 0]), fm(ck[:, :, 1]), fm(cv[:, :, 0])], axis=2),
        "cache_values": cv[:, :, 1],
        "win_keys": f["cache_win_k"][0].reshape(NB, S, P).transpose(2, 0, 1),
        "win_values": f["cache_win_v"][0].reshape(NB, ST, P, P).transpose(2, 0, 1, 3),
        "mlstm_C": f["state_mlstm_C"][0].reshape(NB, 4, HD, 4, 16).transpose(3, 1, 0, 2, 4).reshape(P, HD * 16),
        "mlstm_m": f["state_mlstm_m"][0],
        "pool_state": f["state_pool"][0].reshape(NB, 15, 2, P).transpose(3, 2, 0, 1),
        "ffn_state": f["state_ffn_conv"][0].reshape(NB, 2, 2 * FC, P).transpose(3, 2, 1, 0),
    }
    outs = {
        "y": (P, KD, T), "kv_fm": (P, 4, S), "v_tm": (P, ST, 2 * P), "sample_proj": (P, N_FM, NB), "sample_v": (NB, 2 * P),
        "wk": (P, NB, S - 1), "wv": (P, NB, ST, P), "C": (HD, 4, HD + 1), "m": (4, 1), "pool": (P, 2, 15),
        "sC": (P, HD * 16), "sn": (32, HD), "sm": (32, 1), "spool": (P, 2, NB, 15), "ffp": (P, 2 * FC, 2),
        "ffs": (P, 2 * FC, 2, NB),
    }
    nc = bacc.Bacc("TRN2", target_bir_lowering=False, num_devices=1)
    arrays = {n: np.ascontiguousarray(a) for n, a in ins.items()}
    args = [nc.dram_tensor(n, a.shape, I32 if n == "page_table" else F32, kind="ExternalInput").ap() for n, a in arrays.items()]
    args += [nc.dram_tensor("out_" + n, s, F32, kind="ExternalOutput").ap() for n, s in outs.items()]
    trunk_kernel(nc, *args)
    res = run_bass_kernel_spmd(nc, [arrays], core_ids=[0]).results[0]
    o = {n: res["out_" + n] for n in outs}

    y = o["y"].transpose(2, 1, 0).reshape(T, D)
    heads = lambda a: a.reshape(a.shape[:-1] + (2, HD))
    kc, vc, ks, kw = (heads(o["kv_fm"][:, i].T) for i in range(4))
    vt = o["v_tm"].transpose(1, 0, 2).reshape(S, 2 * P)
    vs, vw = heads(vt[:, :P]), heads(vt[:, P:])
    s = lambda t: o["sample_proj"][:, t].T
    svs, svw = o["sample_v"][:, :P], o["sample_v"][:, P:]
    new = lambda a, b: np.stack([a, b], axis=1)
    swk = np.concatenate([o["wk"].transpose(1, 2, 0), s(T_KW)[:, None]], axis=1)
    wv = o["wv"].transpose(1, 2, 0, 3).reshape(NB, S, P)
    swv = np.concatenate([wv[:, 1:], svw[:, None]], axis=1)
    C = o["C"].transpose(1, 0, 2)
    sC = o["sC"].reshape(4, 4, NB, HD, 16).transpose(2, 1, 3, 0, 4).reshape(NB, 4, HD, HD)
    return (
        y[:S][None], y[S:][:, None],
        new(kc, ks)[None, None], new(vc, vs)[None, None], kw[None, None], vw[None, None],
        np.ascontiguousarray(C[:, :, :HD])[None, None], np.ascontiguousarray(C[:, :, HD])[None, None], o["m"].reshape(1, 1, 4),
        o["pool"].transpose(2, 1, 0).reshape(1, 1, 15, 2 * P), o["ffp"].transpose(2, 1, 0).reshape(1, 1, 2, 2 * FF),
        new(heads(s(T_KC)), heads(s(T_KS)))[None, :, None], new(heads(s(T_VC)), heads(svs))[None, :, None],
        heads(swk)[None], heads(swv)[None],
        sC[None], o["sn"].reshape(4, NB, HD).transpose(1, 0, 2)[None], o["sm"].reshape(4, NB).T[None],
        o["spool"].transpose(2, 3, 1, 0).reshape(1, NB, 15, 2 * P),
        o["ffs"].transpose(3, 2, 1, 0).reshape(1, NB, 2, 2 * FF),
    )
```
